# Optimizing a Trainium2 kernel written in Bass

```python
import jax, jax.numpy as jnp
from jax import lax
import numpy as np

D_MODEL = 1024
BATCH = 1
SEQ = 2048
DEPTH = 1
DEC_BATCH = 1
DEC_SEQ = 32
PAST_LEN = 2048

CHUNK = 64
CONV_DIM = D_MODEL // 2
CONV_W = 3
N_HEADS = 8
HEAD_DIM = 64
ATT_DIM = N_HEADS * HEAD_DIM
QBLOCK = 128
FORGET_BIAS = 2.0
LN_EPS = 1e-5
ALPHA = (2.0 * DEPTH) ** 0.25
BETA = (8.0 * DEPTH) ** -0.25
IN_COLS = 4 * CONV_DIM + 3 * ATT_DIM + N_HEADS + ATT_DIM + 2 * D_MODEL

kernel_name = "hybrid_shortconv_fox_stream_step"

def _split_points():
    sizes = [CONV_DIM] * 4 + [ATT_DIM] * 3 + [N_HEADS, ATT_DIM]
    pts, acc = [], 0
    for s in sizes:
        acc += s
        pts.append(acc)
    return pts

def _layer_norm(x, g, b):
    xf = x.astype(jnp.float32)
    mu = jnp.mean(xf, axis=-1, keepdims=True)
    var = jnp.mean(jnp.square(xf - mu), axis=-1, keepdims=True)
    y = (xf - mu) * lax.rsqrt(var + LN_EPS) * g.astype(jnp.float32) + b.astype(jnp.float32)
    return y.astype(x.dtype)

def _fox_attention(q, k, v, cq, ck, q_offset):
    b, tq, h, dh = q.shape
    tk = k.shape[1]
    qb = min(QBLOCK, tq)
    nb = tq // qb
    scale = dh ** -0.5
    q_blocks = q.reshape(b, nb, qb, h, dh).swapaxes(0, 1)
    cq_blocks = cq.reshape(b, nb, qb, h).swapaxes(0, 1)
    q_pos = (q_offset + jnp.arange(tq, dtype=jnp.int32)).reshape(nb, qb)
    k_pos = jnp.arange(tk, dtype=jnp.int32)
    ck_t = ck.swapaxes(1, 2)

    def one_block(args):
        qblk, cblk, pblk = args
        logits = jnp.einsum('bqhd,bkhd->bhqk', qblk, k, preferred_element_type=jnp.float32) * scale
        logits = logits + cblk.swapaxes(1, 2)[..., None] - ck_t[:, :, None, :]
        mask = k_pos[None, :] <= pblk[:, None]
        logits = jnp.where(mask, logits, -jnp.inf)
        probs = jax.nn.softmax(logits, axis=-1)
        return jnp.einsum('bhqk,bkhd->bqhd', probs.astype(v.dtype), v)

    out = lax.map(one_block, (q_blocks, cq_blocks, q_pos))
    return out.swapaxes(0, 1).reshape(b, tq, h, dh)

def _trunk_layer(x, w_in, b_f, conv_w, w_proj_a, w_proj_b, w_out, ln_g, ln_b,
                 conv_prev, past_k, past_v, past_logf):
    bsz, t, _ = x.shape
    proj = x @ w_in
    x_a, gate_b, gate_c, z_a, q, k, v, f_logit, z_b, merge = jnp.split(proj, _split_points(), axis=-1)

    u = gate_c * x_a
    if conv_prev is None:
        conv_prev = jnp.zeros((bsz, CONV_W - 1, CONV_DIM), u.dtype)
    full = jnp.concatenate([conv_prev.astype(u.dtype), u], axis=1)
    conv = sum(full[:, i:i + t] * conv_w[i] for i in range(CONV_W))
    y_a = gate_b * conv * jax.nn.silu(z_a)
    new_conv = full[:, -(CONV_W - 1):]

    q = q.reshape(bsz, t, N_HEADS, HEAD_DIM)
    k = k.reshape(bsz, t, N_HEADS, HEAD_DIM)
    v = v.reshape(bsz, t, N_HEADS, HEAD_DIM)
    logf = jax.nn.log_sigmoid(f_logit.astype(jnp.float32) + b_f.astype(jnp.float32))
    if past_k is None:
        c_new = jnp.cumsum(logf, axis=1)
        keys, vals, ck, offset = k, v, c_new, 0
    else:
        c_past = jnp.cumsum(past_logf.astype(jnp.float32), axis=1)
        c_new = c_past[:, -1:] + jnp.cumsum(logf, axis=1)
        keys = jnp.concatenate([past_k.astype(k.dtype), k], axis=1)
        vals = jnp.concatenate([past_v.astype(v.dtype), v], axis=1)
        ck = jnp.concatenate([c_past, c_new], axis=1)
        offset = past_k.shape[1]
    att = _fox_attention(q, keys, vals, c_new, ck, offset).reshape(bsz, t, ATT_DIM)
    y_b = att * jax.nn.silu(z_b)

    g = jax.nn.sigmoid(merge)
    g_a, g_b = g[..., :D_MODEL], g[..., D_MODEL:]
    mixed = g_a * (y_a @ w_proj_a) + g_b * (y_b @ w_proj_b)
    sub = mixed @ w_out
    y = _layer_norm(ALPHA * x + sub, ln_g, ln_b)
    return y, k, v, logf.astype(x.dtype), new_conv

def _run_trunk(x, ln_in_g, ln_in_b, w_in, b_f, conv_w, w_proj_a, w_proj_b, w_out, ln_g, ln_b,
               cache_k=None, cache_v=None, cache_logf=None, state_conv=None):
    h = _layer_norm(x, ln_in_g, ln_in_b)
    ks, vs, lfs, cs = [], [], [], []
    for l in range(DEPTH):
        has_past = cache_k is not None
        h, k, v, lf, cv = _trunk_layer(
            h, w_in[l], b_f[l], conv_w[l], w_proj_a[l], w_proj_b[l], w_out[l], ln_g[l], ln_b[l],
            state_conv[l] if has_past else None,
            cache_k[l] if has_past else None,
            cache_v[l] if has_past else None,
            cache_logf[l] if has_past else None)
        ks.append(k); vs.append(v); lfs.append(lf); cs.append(cv)
    return h, jnp.stack(ks), jnp.stack(vs), jnp.stack(lfs), jnp.stack(cs)

def setup_inputs(seed: int = 0) -> dict:
    key = jax.random.key(seed)
    ks = jax.random.split(key, 18)
    n = jax.random.normal
    f32 = jnp.float32
    return {
        "x_prompt": n(ks[0], (BATCH, SEQ, D_MODEL), f32),
        "x_sample": n(ks[1], (DEC_BATCH, DEC_SEQ, D_MODEL), f32),
        "cache_k": n(ks[2], (DEPTH, DEC_BATCH, PAST_LEN, N_HEADS, HEAD_DIM), f32),
        "cache_v": n(ks[3], (DEPTH, DEC_BATCH, PAST_LEN, N_HEADS, HEAD_DIM), f32),
        "cache_logf": jax.nn.log_sigmoid(FORGET_BIAS + n(ks[4], (DEPTH, DEC_BATCH, PAST_LEN, N_HEADS), f32)),
        "state_conv": n(ks[5], (DEPTH, DEC_BATCH, CONV_W - 1, CONV_DIM), f32),
        "ln_in_g": 1.0 + 0.02 * n(ks[6], (D_MODEL,), f32),
        "ln_in_b": 0.02 * n(ks[7], (D_MODEL,), f32),
        "w_in": n(ks[8], (DEPTH, D_MODEL, IN_COLS), f32) * D_MODEL ** -0.5,
        "b_f": FORGET_BIAS + 0.1 * n(ks[9], (DEPTH, N_HEADS), f32),
        "conv_w": n(ks[10], (DEPTH, CONV_W, CONV_DIM), f32) * CONV_W ** -0.5,
        "w_proj_a": n(ks[11], (DEPTH, CONV_DIM, D_MODEL), f32) * (CONV_DIM ** -0.5 * BETA),
        "w_proj_b": n(ks[12], (DEPTH, ATT_DIM, D_MODEL), f32) * (ATT_DIM ** -0.5 * BETA),
        "w_out": n(ks[13], (DEPTH, D_MODEL, D_MODEL), f32) * (D_MODEL ** -0.5 * BETA),
        "ln_g": 1.0 + 0.02 * n(ks[14], (DEPTH, D_MODEL), f32),
        "ln_b": 0.02 * n(ks[15], (DEPTH, D_MODEL), f32),
    }

def reference(x_prompt, x_sample, cache_k, cache_v, cache_logf, state_conv,
              ln_in_g, ln_in_b, w_in, b_f, conv_w, w_proj_a, w_proj_b, w_out, ln_g, ln_b):
    y_prompt, k_prompt, v_prompt, logf_prompt, conv_prompt = _run_trunk(
        x_prompt, ln_in_g, ln_in_b, w_in, b_f, conv_w, w_proj_a, w_proj_b, w_out, ln_g, ln_b)
    y_sample, k_sample, v_sample, logf_sample, conv_sample = _run_trunk(
        x_sample, ln_in_g, ln_in_b, w_in, b_f, conv_w, w_proj_a, w_proj_b, w_out, ln_g, ln_b,
        cache_k, cache_v, cache_logf, state_conv)
    return (y_prompt, y_sample, k_prompt, v_prompt, logf_prompt, conv_prompt,
            k_sample, v_sample, logf_sample, conv_sample)


_drawn_inputs = setup_inputs


def setup_inputs(seed=0):
    import zlib

    import numpy as np

    out = dict(_drawn_inputs(seed))
    spreads = {}
    factors = {'cache_k': 6.839,
     'cache_v': 5.028,
     'cache_logf': 8.0,
     'state_conv': 4.178,
     'ln_g': 2.875,
     'ln_b': 2.865}
    for name, (base, spread) in spreads.items():
        noise = np.random.default_rng([zlib.crc32(name.encode()), seed]).standard_normal(out[name].shape)
        drawn = base * np.exp(spread * noise) if base else spread * noise
        out[name] = __import__('jax').numpy.asarray(drawn.astype(out[name].dtype))
    for name, factor in factors.items():
        out[name] = (out[name] * factor).astype(out[name].dtype)
    return out
```

```python
from contextlib import ExitStack

import concourse.bass as bass
from concourse import mybir

F32 = mybir.dt.float32
F32R = mybir.dt.float32r
BF16 = mybir.dt.bfloat16
ALU = mybir.AluOpType
ACT = mybir.ActivationFunctionType
AX_X = mybir.AxisListType.X

P = 128
D = 1024
KT = D // P
SEQ = 2048
DEC = 32
PAST = 2048
T = SEQ + DEC
CH = 416
NCH = T // CH
SUB = CH // 4
TAIL = SEQ - (NCH - 1) * CH
H = 8
HD = 64
ATT = H * HD
CONV = 512
CW = 3
NB = SEQ // P
QW = 512
NQ = SEQ // QW
EPS = 1e-5
ALPHA = 2.0 ** 0.25
SCALE = HD ** -0.5
MASKED = -1e30
CKW = SEQ + PAST + DEC

N_TILES = 48


def build(nc, x_prompt, x_sample, cache_k, cache_v, cache_logf, state_conv, ln_in, w_tiles, w_f, b_f,
          conv_w, wpa_tiles, wpb_tiles, w_out, ln_out, ident, causal, blocks,
          y_prompt, y_sample, k_prompt, v_prompt, logf_prompt, conv_prompt,
          k_sample, v_sample, logf_sample, conv_sample):
    with ExitStack() as root:
        def dram(name, shape):
            return nc.dram_tensor(name, shape, F32, kind="Internal").ap()

        s = dict(
            h=dram("h_rows", (T, D)), qh=dram("q_hi", (ATT, T)), ql=dram("q_lo", (ATT, T)),
            kh=dram("k_hi", (ATT, T)), kl=dram("k_lo", (ATT, T)),
            vh=dram("v_hi", (T, ATT)), vl=dram("v_lo", (T, ATT)),
            zb=dram("silu_zb", (ATT, T)), g=dram("merge_gates", (2 * D, T)),
            yah=dram("ya_hi", (CONV, T)), yal=dram("ya_lo", (CONV, T)),
            ybh=dram("yb_hi", (ATT, T)), ybl=dram("yb_lo", (ATT, T)),
            ck=dram("forget_rows", (2, H, CKW)), sums=dram("sums", (H, SEQ)), rcps=dram("rcps", (H, SEQ)), mixed=dram("mixed", (D, T)),
        )
        with ExitStack() as ctx:
            hT_hi = ctx.enter_context(nc.sbuf_tensor("hT_hi", [P, KT, T], F32R))
            hT_lo = ctx.enter_context(nc.sbuf_tensor("hT_lo", [P, KT, T], F32R))
            input_norm(nc, root, s, hT_hi, hT_lo, x_prompt, x_sample, ln_in, ident)
            forget_gates(nc, root, s, hT_hi, hT_lo, w_f, b_f, cache_logf, ident, logf_prompt, logf_sample)
            projections(nc, root, s, hT_hi, hT_lo, w_tiles, conv_w, state_conv, ident,
                        k_prompt, v_prompt, k_sample, v_sample, conv_prompt, conv_sample)
        prompt_attention(nc, root, s, ident, causal)
        sample_attention(nc, root, s, cache_k, cache_v, ident, causal, blocks)
        merge(nc, root, s, wpa_tiles, wpb_tiles)
        output_norm(nc, root, s, w_out, ln_out, y_prompt, y_sample)


def tools(nc, ctx, root, tag):
    def sb(name, shape, dt=F32):
        return ctx.enter_context(nc.sbuf_tensor(f"{tag}_{name}", shape, dt))

    def pb(name, shape=(P, 512), dt=F32):
        return ctx.enter_context(nc.psum_tensor(f"{tag}_{name}", list(shape), dt))

    def sem(name):
        held.append(nc.alloc_semaphore(name=f"{tag}_{name}"))
        return held[-1]

    def clear():
        nc.clear_and_free_semaphores(held)
        nc.all_engine_barrier()

    held = []
    ctx.callback(clear)
    return sb, pb, sem


def settled(sp, passed):
    def wait(q, n):
        sp.wait_ge(q, n)
        if not isinstance(n, int):
            sp.sem_inc(passed, 1)
    return wait


def input_norm(nc, root, s, hT_hi, hT_lo, x_prompt, x_sample, ln_in, ident):
    with ExitStack() as ctx:
        sb, pb, sem = tools(nc, ctx, root, "ln0")
        x = sb("x", [P, 4, D])
        xn = sb("xn", [P, 2, D])
        h = sb("h", [P, 2, D])
        gain = sb("gain", [P, D])
        shift = sb("shift", [P, D])
        eye = sb("eye", [P, P])
        stats = sb("stats", [P, 2, 12])
        mv = sb("mv", [P, 2, 2])
        rstd = sb("rstd", [P, 2])
        nmr = sb("nmr", [P, 2])
        var = sb("var", [P, 2])
        power = sb("power", [P, 1])
        tp = [pb(f"tp{i}", (P, KT, P)) for i in range(4)]

        const_in = sem("const_in")
        x_in = [sem(f"x_in{i}") for i in range(4)]
        aux, aggr_done, passed, sp_passed = sem("aux"), sem("aggr"), sem("passed"), sem("sp_passed")
        stats_done, mv_done, rstd_done, coef_done = sem("stats"), sem("mv"), sem("rstd"), sem("coef")
        xn_done, gained, h_done, turned, hi_done, lo_done = (
            sem("xn"), sem("gained"), sem("h"), sem("turned"), sem("hi"), sem("lo"))
        h_out = [sem(f"h_out{i}") for i in range(2)]
        N = NB + 1

        block = ctx.enter_context(nc.Block())

        @block.sync
        def _(sp):
            wait = settled(sp, sp_passed)

            def load(t, rows=P, slot=None):
                src = x_sample if rows == DEC else x_prompt[bass.ds(t * P, P), :]
                sp.dma_start(x[0:rows, slot, :], src).then_inc(x_in[slot], 16)

            def store(t, b, rows=P):
                wait(h_done, t + 1)
                sp.dma_start(s["h"][bass.ds(t * P, rows), :], h[0:rows, b, :]).then_inc(h_out[b], 16)

            for t in range(4):
                load(t, P, t)
                if t == 0:
                    sp.dma_start(gain[:, :], ln_in[0:1, :].broadcast_to([P, D])).then_inc(const_in, 16)
                    sp.dma_start(shift[:, :], ln_in[1:2, :].broadcast_to([P, D])).then_inc(const_in, 16)
                    sp.dma_start(eye[:, :], ident).then_inc(const_in, 16)
            with sp.Fori(0, 3) as i:
                for c in range(4):
                    wait(xn_done, 4 * i + c + 1)
                    load(4 * i + c + 4, P, c)
                    store(4 * i + c, c % 2)
            sp.wait_ge(xn_done, 13)
            load(16, DEC, 0)
            for t in range(12, 16):
                store(t, t % 2)
            store(16, 0, DEC)
            sp.wait_ge(h_out[0], 16 * 9)
            sp.wait_ge(h_out[1], 16 * 8)

        @block.vector
        def _(dve):
            def stat(t, c, rows=P):
                r, b = slice(0, rows), c % 2
                dve.wait_ge(x_in[c], t * 4 + 16 - 4 * c)
                dve.bn_stats(stats[r, b, 0:6], x[r, c, 0:512])
                dve.bn_stats(stats[r, b, 6:12], x[r, c, 512:1024]).then_inc(stats_done, 1)
                dve.wait_ge(stats_done, t + 1)
                dve.sem_inc(passed, 1)
                dve.bn_aggr(mv[r, b, :], stats[r, b, :]).then_inc(aggr_done, 1)
                dve.wait_ge(aggr_done, t + 1)
                dve.tensor_scalar(var[r, b:b + 1], mv[r, b, 1:2], EPS, None, ALU.add).then_inc(mv_done, 1)

            def coef(t, c, rows=P):
                r, b = slice(0, rows), c % 2
                dve.wait_ge(rstd_done, t + 1)
                dve.tensor_scalar(nmr[r, b:b + 1], mv[r, b, 0:1], rstd[r, b:b + 1], -1.0, ALU.mult, ALU.mult)\
                   .then_inc(coef_done, 1)

            def times_gain(t, c, rows=P):
                r, b = slice(0, rows), c % 2
                dve.wait_ge(xn_done, t + 1)
                dve.tensor_tensor(xn[r, b, :], xn[r, b, :], gain[r, :], ALU.mult).then_inc(gained, 1)

            def low(t, c, rows=P):
                dve.wait_ge(hi_done, t + 1)
                tok = bass.ds(t * P, rows)
                dve.tensor_tensor(hT_lo[:, :, tok], tp[c][:, :, 0:rows], hT_hi[:, :, tok].bitcast(F32),
                                  ALU.subtract).then_inc(lo_done, 1)

            def step(t, c, next_rows=P):
                stat(t + 1, (c + 1) % 4, next_rows)
                times_gain(t, c)
                coef(t + 1, (c + 1) % 4, next_rows)
                if not isinstance(t, int) or t >= 2:
                    low(t - 2, (c + 2) % 4)

            stat(0, 0)
            coef(0, 0)
            dve.wait_ge(const_in, 48)
            step(0, 0)
            step(1, 1)
            with dve.Fori(0, 3) as i:
                for c in range(4):
                    step(4 * i + c + 2, (c + 2) % 4)
            step(14, 2)
            step(15, 3, DEC)
            times_gain(16, 0, DEC)
            low(14, 2)
            low(15, 3)
            low(16, 0, DEC)

        @block.scalar
        def _(act):
            def norm(t, c, rows=P):
                r, b = slice(0, rows), c % 2
                act.wait_ge(coef_done, t + 1)
                if not isinstance(t, int) or t >= 2:
                    act.wait_ge(h_done, t - 1)
                act.activation(xn[r, b, :], x[r, c, :], ACT.Identity, bias=nmr[r, b:b + 1],
                               scale=rstd[r, b:b + 1]).then_inc(xn_done, 1)

            def high(t, c, rows=P):
                act.wait_ge(turned, t + 1)
                act.activation(hT_hi[:, :, bass.ds(t * P, rows)], tp[c][:, :, 0:rows], ACT.Copy)\
                   .then_inc(hi_done, 1)

            norm(0, 0)
            norm(1, 1)
            with act.Fori(0, 3) as i:
                for c in range(4):
                    norm(4 * i + c + 2, (c + 2) % 4)
                    high(4 * i + c, c)
            norm(14, 2)
            high(12, 0)
            norm(15, 3)
            high(13, 1)
            norm(16, 0, DEC)
            for t in (14, 15):
                high(t, t % 4)
            high(16, 0, DEC)

        @block.gpsimd
        def _(pool):
            def add_shift(t, c, rows=P):
                r, b = slice(0, rows), c % 2
                pool.wait_ge(gained, t + 1)
                if not isinstance(t, int) or t >= 2:
                    pool.wait_ge(turned, t - 1)
                    pool.wait_ge(h_out[b], t * 8 - 8 * b)
                pool.tensor_tensor(h[r, b, :], xn[r, b, :], shift[r, :], ALU.add).then_inc(h_done, 1)

            def inverse_std(t, c, rows=P):
                r, b = slice(0, rows), c % 2
                pool.wait_ge(mv_done, t + 1)
                pool.tensor_tensor(rstd[r, b:b + 1], var[r, b:b + 1], power[r, :], ALU.pow).then_inc(rstd_done, 1)

            pool.memset(power[:, :], -0.5).then_inc(aux, 1)
            pool.wait_ge(aux, 1)
            inverse_std(0, 0)
            pool.wait_ge(const_in, 48)
            for t in range(2):
                inverse_std(t + 1, t + 1)
                add_shift(t, t)
            with pool.Fori(0, 3) as i:
                for c in range(4):
                    inverse_std(4 * i + c + 3, (c + 3) % 4)
                    add_shift(4 * i + c + 2, (c + 2) % 4)
            inverse_std(15, 3)
            add_shift(14, 2)
            inverse_std(16, 0, DEC)
            add_shift(15, 3)
            add_shift(16, 0, DEC)

        @block.tensor
        def _(pe):
            def turn(t, c, rows=P):
                pe.wait_ge(h_done, t + 1)
                if not isinstance(t, int) or t >= 4:
                    pe.wait_ge(lo_done, t - 3)
                for k in range(KT):
                    last = pe.transpose(tp[c][:, k, 0:rows], h[0:rows, c % 2, k * P:(k + 1) * P],
                                        eye[0:rows, 0:rows])
                last.then_inc(turned, 1)

            pe.wait_ge(const_in, 48)
            for t in range(4):
                turn(t, t)
            with pe.Fori(1, 4) as i:
                for c in range(4):
                    turn(4 * i + c, c)
            turn(16, 0, DEC)


def forget_gates(nc, root, s, hT_hi, hT_lo, w_f, b_f, cache_logf, ident, logf_prompt, logf_sample):
    with ExitStack() as ctx:
        sb, pb, sem = tools(nc, ctx, root, "fg")
        wf = sb("wf", [P, KT, H])
        wf_hi = sb("wf_hi", [P, KT, P], F32R)
        wf_lo = sb("wf_lo", [P, KT, P], F32R)
        bias = sb("bias", [H, 1])
        eye = sb("eye", [P, P])
        past_rows = sb("past_rows", [P, NB, H])
        z = sb("z", [H, T])
        cum = sb("cum", [H, T])
        logf = sb("logf", [H, T])
        past = sb("past", [H, PAST])
        ones = sb("ones", [H, PAST])
        cum_past = sb("cum_past", [H, PAST])
        hi = sb("hi", [H, T], F32R)
        lo = sb("lo", [H, T], F32R)
        logf_rows = sb("logf_rows", [SUB, T // SUB, H])
        proj = [pb(f"proj{i}") for i in range(NCH)]
        tp = pb("tp")
        tq = [pb(f"tq{i}") for i in range(2)]
        loaded, zeroed, w_hi, w_lo, proj_done = sem("loaded"), sem("zeroed"), sem("w_hi"), sem("w_lo"), sem("proj")
        z_done, soft, logf_done, summed = sem("z"), sem("soft"), sem("logf"), sem("summed")
        past_turned, past_copied, rows_turned, rows_copied = (
            sem("past_turned"), sem("past_copied"), sem("rows_turned"), sem("rows_copied"))
        hi_done, lo_done, out, out_ck = sem("hi"), sem("lo"), sem("out"), sem("out_ck")
        ck = s["ck"]
        parts = [(cum_past, PAST, [(0, PAST, SEQ)]), (cum, T, [(0, SEQ, 0), (SEQ, T, SEQ + PAST)])]
        full = SEQ // SUB
        rest = SEQ - full * SUB

        block = ctx.enter_context(nc.Block())

        @block.sync
        def _(sp):
            sp.dma_start(wf[:, :, :], w_f).then_inc(loaded, 16)
            sp.dma_start(bias[:, :], b_f).then_inc(loaded, 16)
            sp.dma_start(eye[:, :], ident).then_inc(loaded, 16)
            sp.dma_start(past_rows[:, :, :], cache_logf.rearrange("(b p) h -> p b h", p=P)).then_inc(loaded, 16)
            n = 0
            for i, (_, _, cols) in enumerate(parts):
                sp.wait_ge(lo_done, i + 1)
                for a, b, at in cols:
                    sp.dma_start(ck[0, :, at:at + b - a], hi[:, a:b].bitcast(F32)).then_inc(out_ck, 16)
                    sp.dma_start(ck[1, :, at:at + b - a], lo[:, a:b].bitcast(F32)).then_inc(out_ck, 16)
                    n += 32
                sp.wait_ge(out_ck, n)
            sp.wait_ge(rows_copied, 1)
            sp.dma_start(logf_prompt[0:full * SUB, :].rearrange("(a p) h -> p a h", p=SUB),
                         logf_rows[:, 0:full, :]).then_inc(out, 16)
            sp.dma_start(logf_prompt[full * SUB:SEQ, :], logf_rows[0:rest, full, :]).then_inc(out, 16)
            sp.dma_start(logf_sample, logf_rows[rest:SUB, full, :]).then_inc(out, 16)
            sp.wait_ge(out, 48)

        @block.gpsimd
        def _(pool):
            pool.memset(wf_hi[:, :, :].bitcast(F32), 0.0).then_inc(zeroed, 1)
            pool.memset(wf_lo[:, :, :].bitcast(F32), 0.0).then_inc(zeroed, 1)
            pool.memset(ones[:, :], 1.0).then_inc(zeroed, 1)

        @block.vector
        def _(dve):
            dve.wait_ge(loaded, 64)
            dve.wait_ge(zeroed, 3)
            dve.tensor_copy(wf_hi[:, :, 0:H], wf[:, :, :]).then_inc(w_hi, 1)
            dve.wait_ge(w_hi, 1)
            dve.tensor_tensor(wf_lo[:, :, 0:H], wf[:, :, :], wf_hi[:, :, 0:H].bitcast(F32), ALU.subtract)\
               .then_inc(w_lo, 1)
            for q in range(4):
                dve.wait_ge(past_turned, q + 1)
                dve.tensor_copy(past[:, q * 512:(q + 1) * 512], tq[q % 2][0:H, :]).then_inc(past_copied, 1)
            dve.wait_ge(past_copied, 4)
            dve.tensor_tensor_scan(cum_past[:, :], ones[:, :], past[:, :], 0.0, ALU.mult, ALU.add)\
               .then_inc(summed, 1)
            dve.wait_ge(hi_done, 1)
            dve.scalar_tensor_tensor(out=lo[:, 0:PAST], in0=cum_past[:, :], scalar=-8.0,
                                     in1=hi[:, 0:PAST].bitcast(F32), op0=ALU.mult, op1=ALU.subtract)\
               .then_inc(lo_done, 1)
            dve.wait_ge(soft, 3)
            dve.scalar_tensor_tensor(out=logf[:, :], in0=z[:, :], scalar=0.0, in1=cum[:, :],
                                     op0=ALU.min, op1=ALU.subtract).then_inc(logf_done, 1)
            dve.wait_ge(logf_done, 1)
            dve.tensor_tensor_scan(cum[:, 0:SEQ], ones[:, :], logf[:, 0:SEQ], 0.0, ALU.mult, ALU.add)\
               .then_inc(summed, 1)
            dve.tensor_tensor_scan(cum[:, SEQ:T], ones[:, 0:DEC], logf[:, SEQ:T], cum_past[:, PAST - 1:PAST],
                                   ALU.mult, ALU.add).then_inc(summed, 1)
            dve.wait_ge(hi_done, 2)
            dve.scalar_tensor_tensor(out=lo[:, :], in0=cum[:, :], scalar=-8.0, in1=hi[:, :].bitcast(F32),
                                     op0=ALU.mult, op1=ALU.subtract).then_inc(lo_done, 1)
            dve.wait_ge(rows_turned, 1)
            dve.tensor_copy(logf_rows[:, :, :], tp[0:SUB, 0:T // SUB * H].rearrange("p (a h) -> p a h", h=H))\
               .then_inc(rows_copied, 1)

        @block.scalar
        def _(act):
            act.wait_ge(summed, 1)
            act.activation(hi[:, 0:PAST], cum_past[:, :], ACT.Copy, scale=-8.0).then_inc(hi_done, 1)
            for n in range(NCH):
                act.wait_ge(proj_done, n + 1)
                act.activation(z[:, n * CH:(n + 1) * CH], proj[n][0:H, 0:CH], ACT.Identity,
                               bias=bias[:, :]).then_inc(z_done, 1)
            act.wait_ge(z_done, NCH)
            act.activation(cum[:, :], z[:, :], ACT.Abs).then_inc(soft, 1)
            act.wait_ge(soft, 1)
            act.activation(cum[:, :], cum[:, :], ACT.Exp, scale=-1.0).then_inc(soft, 1)
            act.wait_ge(soft, 2)
            act.activation(cum[:, :], cum[:, :], ACT.Ln, bias=1.0).then_inc(soft, 1)
            act.wait_ge(summed, 3)
            act.wait_ge(out_ck, 32)
            act.activation(hi[:, :], cum[:, :], ACT.Copy, scale=-8.0).then_inc(hi_done, 1)

        @block.tensor
        def _(pe):
            pe.wait_ge(loaded, 64)
            for q in range(4):
                if q >= 2:
                    pe.wait_ge(past_copied, q - 1)
                for b in range(4):
                    last = pe.transpose(tq[q % 2][0:H, b * P:(b + 1) * P], past_rows[:, 4 * q + b, :], eye[:, :])
                last.then_inc(past_turned, 1)
            pe.wait_ge(w_lo, 1)
            for n in range(NCH):
                tok = slice(n * CH, (n + 1) * CH)
                project(pe, proj[n][:, 0:CH], [(wf_hi[:, k, :], wf_lo[:, k, :], hT_hi[:, k, tok], hT_lo[:, k, tok])
                                               for k in range(KT)]).then_inc(proj_done, 1)
            pe.wait_ge(logf_done, 1)
            for a in range(T // SUB):
                last = pe.transpose(tp[0:SUB, a * H:(a + 1) * H], logf[:, a * SUB:(a + 1) * SUB], eye[0:H, 0:H])
            last.then_inc(rows_turned, 1)


def project(pe, out, parts):
    for i, (w_hi, w_lo, x_hi, x_lo) in enumerate(parts):
        pe.matmul(out, w_hi, x_hi, start=(i == 0), stop=False)
        pe.matmul(out, w_hi, x_lo, start=False, stop=False)
        last = pe.matmul(out, w_lo, x_hi, start=False, stop=(i == len(parts) - 1))
    return last


def projections(nc, root, s, hT_hi, hT_lo, w_tiles, conv_w, state_conv, ident,
                k_prompt, v_prompt, k_sample, v_sample, conv_prompt, conv_sample):
    with ExitStack() as ctx:
        sb, pb, sem = tools(nc, ctx, root, "pr")
        w = sb("w", [P, 2, KT, P])
        w_hi = sb("w_hi", [P, 2, KT, P], F32R)
        w_lo = sb("w_lo", [P, 2, KT, P], F32R)
        eye = sb("eye", [P, P])
        cw = sb("cw", [P, CONV // P, CW])
        GAP = SEQ + CW - 1
        U = sb("u", [P, T + 2 * (CW - 1)])
        xa = sb("xa", [P, T])
        conv = sb("conv", [P, T + CW - 1])
        full_t = sb("full_t", [P, 2, CH])
        out_a = sb("out_a", [P, 2, 512], F32R)
        out_b = sb("out_b", [P, 2, 512], F32R)
        out_c = sb("out_c", [SUB, 2, 4, P])
        bank = [pb(f"bank{i}") for i in range(NCH)]
        turn_bank = pb("turn")

        const_in = sem("const_in")
        w_in = [sem(f"w_in{i}") for i in range(2)]
        w_hi_done, w_lo_done, proj_done = sem("w_hi"), sem("w_lo"), sem("proj_done")
        bank_free = [sem(f"bank_free{i}") for i in range(NCH)]
        a_done, b_done, c_done = sem("a_done"), sem("b_done"), sem("c_done")
        a_out, b_out, c_out = ([sem(f"{x}_out{i}") for i in range(2)] for x in "abc")
        edges, state_in, conv_done, frames_out, tail_out = (
            sem("edges"), sem("state_in"), sem("conv"), sem("frames_out"), sem("tail_out"))
        full_done, gated, turned, sp_passed = sem("full"), sem("gated"), sem("turned"), sem("sp_passed")

        def toks(n):
            return slice(n * CH, (n + 1) * CH)

        def left(a, n):
            return 48 * a + 16 * (n // 2) + 16 if n % 2 == 0 else 32 * a + 16 * (n // 2) + 16

        def spans(n, shift):
            if n < NCH - 1:
                return [(slice(n * CH + shift, (n + 1) * CH + shift), slice(0, CH))]
            return [(slice(n * CH + shift, SEQ + shift), slice(0, TAIL)),
                    (slice(GAP + shift, GAP + DEC + shift), slice(TAIL, CH))]

        block = ctx.enter_context(nc.Block())

        @block.sync
        def _(sp):
            wait = settled(sp, sp_passed)
            sp.dma_start(w[:, 0], w_tiles[0]).then_inc(w_in[0], 16)
            sp.dma_start(w[:, 1], w_tiles[1]).then_inc(w_in[1], 16)
            sp.dma_start(eye[:, :], ident).then_inc(const_in, 16)
            sp.dma_start(cw[:, :, :], conv_w).then_inc(const_in, 16)
            for q in (*a_out, *b_out, *c_out, tail_out):
                sp.sem_inc(q, 16)
            sp.sem_inc(frames_out, 16)

            def next_w(t, b):
                wait(w_lo_done, t + 1)
                sp.dma_start(w[:, b], w_tiles[bass.ds(t + 2, 1)].rearrange("a p k n -> (a p) k n"))\
                  .then_inc(w_in[b], 16)

            def rows_out(dst, n, a=None, t=None):
                if a is None:
                    wait(bank_free[n], t + 2)
                else:
                    wait(a_done, 5 * a + n + 1)
                sp.dma_start(dst, out_a[:, n % 2, 0:CH].bitcast(F32)).then_inc(a_out[n % 2], 16)

            def lows_out(dst, t, n, done=None):
                if done is None:
                    wait(bank_free[n], t + 2)
                else:
                    wait(b_done, done)
                sp.dma_start(dst, out_b[:, n % 2, 0:CH].bitcast(F32)).then_inc(b_out[n % 2], 16)

            def tokens_out(dst, dst_sample, cols, c, n):
                wait(c_done, 5 * c + n + 1)
                src = out_c[:, n % 2]
                at = n * CH
                if n < NCH - 1:
                    sp.dma_start(dst[at:at + CH, cols].rearrange("(a p) c -> p a c", p=SUB), src)\
                      .then_inc(c_out[n % 2], 16)
                    return
                m = TAIL // SUB
                r = TAIL - m * SUB
                sp.dma_start(dst[at:at + m * SUB, cols].rearrange("(a p) c -> p a c", p=SUB), src[:, 0:m, :])\
                  .then_inc(tail_out, 16)
                sp.dma_start(dst[at + m * SUB:SEQ, cols], src[0:r, m, :]).then_inc(tail_out, 16)
                sp.dma_start(dst_sample[:, cols], src[r:SUB, m, :]).then_inc(c_out[n % 2], 16)

            with sp.Fori(0, 4) as j:
                ch = bass.ds(j * P, P)
                wait(conv_done, 3 * j + 1)
                sp.dma_start(U[:, GAP:GAP + CW - 1], state_conv[ch, :]).then_inc(state_in, 16)
                next_w(4 * j, 0)
                next_w(4 * j + 1, 1)
                wait(bank_free[NCH - 1], 4 * j + 3)
                sp.dma_start(conv_prompt[ch, :], U[:, SEQ:SEQ + CW - 1]).then_inc(frames_out, 16)
                sp.dma_start(conv_sample[ch, :], U[:, GAP + DEC:GAP + DEC + CW - 1]).then_inc(frames_out, 16)
                next_w(4 * j + 2, 0)
                next_w(4 * j + 3, 1)
                for n in range(NCH):
                    rows_out(s["yah"][ch, toks(n)], n, a=j)
                    lows_out(s["yal"][ch, toks(n)], 0, n, 5 * j + n + 1)
            with sp.Fori(0, 4) as j:
                ch = bass.ds(j * P, P)
                next_w(16 + 2 * j, 0)
                for n in range(NCH):
                    rows_out(s["kh"][ch, toks(n)], n, a=4 + 2 * j)
                    lows_out(s["kl"][ch, toks(n)], 16 + 2 * j, n)
                    if n:
                        tokens_out(k_prompt, k_sample, ch, 2 * j, n - 1)
                tokens_out(k_prompt, k_sample, ch, 2 * j, NCH - 1)
                next_w(17 + 2 * j, 1)
                for n in range(NCH):
                    tokens_out(v_prompt, v_sample, ch, 2 * j + 1, n)
                    for name, src, done, value, gone in (
                            ("vh", out_a, a_done, 5 * (5 + 2 * j) + n + 1, a_out[n % 2]),
                            ("vl", out_b, b_done, 5 * (4 + j) + n + 1, b_out[n % 2])):
                        wait(done, value)
                        sp.dma_start(s[name][n * CH:(n + 1) * CH, ch].rearrange("(a p) c -> p a c", p=SUB),
                                     src[0:SUB, n % 2, :].bitcast(F32).rearrange("p (a c) -> p a c", a=4))\
                          .then_inc(gone, 16)
            with sp.Fori(0, 4) as j:
                ch = bass.ds(j * P, P)
                next_w(24 + 2 * j, 0)
                for n in range(NCH):
                    rows_out(s["qh"][ch, toks(n)], n, a=12 + j)
                    lows_out(s["ql"][ch, toks(n)], 24 + 2 * j, n)
                next_w(25 + 2 * j, 1)
                for n in range(NCH):
                    rows_out(s["zb"][ch, toks(n)], n, t=25 + 2 * j)
            with sp.Fori(0, 7) as j:
                for b in range(2):
                    next_w(32 + 2 * j + b, b)
                    for n in range(NCH):
                        rows_out(s["g"][bass.ds((2 * j + b) * P, P), toks(n)], n, t=32 + 2 * j + b)
            for b in range(2):
                for n in range(NCH):
                    rows_out(s["g"][(14 + b) * P:(15 + b) * P, toks(n)], n, t=46 + b)
            for q, tiles in ((a_out, 36), (b_out, 16), (c_out, 8)):
                wait(q[0], left(tiles, 0))
                wait(q[1], left(tiles, 1))
            wait(frames_out, 16 + 32 * 4)
            wait(tail_out, 16 + 32 * 8)

        @block.tensor
        def _(pe):
            def chunk(t, b, n):
                if n == 0:
                    pe.wait_ge(w_lo_done, t + 1)
                pe.wait_ge(bank_free[n], t + 1)
                project(pe, bank[n][:, 0:CH], [(w_hi[:, b, k, :], w_lo[:, b, k, :], hT_hi[:, k, toks(n)],
                                                hT_lo[:, k, toks(n)]) for k in range(KT)]).then_inc(proj_done, 1)

            def turn(j, b, n):
                if b == 0:
                    pe.wait_ge(full_done, 5 * j + n + 1)
                else:
                    pe.wait_ge(bank_free[n], 17 + 2 * j + 2)
                if (b == 0) == (n > 0):
                    pe.wait_ge(c_done, 10 * j + n if b == 0 else 10 * j + 5)
                else:
                    pe.wait_ge(b_done, 20 + 5 * j + n)
                for a in range(4):
                    last = pe.transpose(turn_bank[0:SUB, a * P:(a + 1) * P], full_t[:, n % 2, a * SUB:(a + 1) * SUB],
                                        eye[:, :])
                last.then_inc(turned, 1)

            pe.wait_ge(const_in, 32)
            with pe.Fori(0, 8) as i:
                for b in range(2):
                    for n in range(NCH):
                        chunk(2 * i + b, b, n)
            with pe.Fori(0, 4) as j:
                for b in range(2):
                    for n in range(NCH):
                        chunk(16 + 2 * j + b, b, n)
                        if n:
                            turn(j, b, n - 1)
                    turn(j, b, NCH - 1)
            with pe.Fori(0, 12) as i:
                for b in range(2):
                    for n in range(NCH):
                        chunk(24 + 2 * i + b, b, n)

        @block.gpsimd
        def _(pool):
            def low_w(t, b):
                pool.wait_ge(w_hi_done, t + 1)
                pool.tensor_tensor(w_lo[:, b], w[:, b], w_hi[:, b].bitcast(F32), ALU.subtract).then_inc(w_lo_done, 1)

            with pool.Fori(0, N_TILES // 2) as i:
                low_w(2 * i, 0)
                low_w(2 * i + 1, 1)

        @block.scalar
        def _(act):
            def high_w(t, b):
                act.wait_ge(w_in[b], 8 * t + 16 - 8 * b)
                act.wait_ge(proj_done, 5 * t - 5)
                act.activation(w_hi[:, b], w[:, b], ACT.Copy).then_inc(w_hi_done, 1)

            def through(t, n, a, func):
                act.wait_ge(proj_done, 5 * t + n + 1)
                act.wait_ge(a_out[n % 2], left(a, n))
                to = out_a[:, n % 2, 0:CH]
                if func != ACT.Copy:
                    to = to.bitcast(F32)
                return act.activation(to, bank[n][:, 0:CH], func)

            def keep_full(t, c, n, done):
                act.wait_ge(proj_done, 5 * t + n + 1)
                act.wait_ge(turned, 5 * c + n + 1 if n == 0 else 5 * c + n)
                return act.activation(full_t[:, n % 2, :], bank[n][:, 0:CH], ACT.Copy).then_inc(done, 1)

            def rows_c(c, n):
                act.wait_ge(turned, 5 * c + n + 2)
                act.wait_ge(c_out[n % 2], left(c, n))
                if n == 0:
                    act.wait_ge(tail_out, 32 * c + 16)
                return act.activation(out_c[:, n % 2], turn_bank[0:SUB, :].rearrange("p (a c) -> p a c", a=4), ACT.Copy)

            for q in bank_free:
                act.sem_inc(q, 1)
            act.sem_inc(turned, 1)
            act.sem_inc(gated, 5)
            act.sem_inc(conv_done, 1)
            act.wait_ge(w_in[0], 16)
            act.activation(w_hi[:, 0], w[:, 0], ACT.Copy).then_inc(w_hi_done, 1)
            act.wait_ge(w_in[1], 16)
            act.activation(w_hi[:, 1], w[:, 1], ACT.Copy).then_inc(w_hi_done, 1)
            with act.Fori(0, 4) as j:
                for n in range(NCH):
                    act.wait_ge(proj_done, 20 * j + n + 1)
                    act.wait_ge(gated, 5 * j + n + 1)
                    act.activation(xa[:, toks(n)], bank[n][:, 0:CH], ACT.Copy).then_inc(bank_free[n], 1)
                high_w(4 * j + 2, 0)
                high_w(4 * j + 3, 1)
                for n in range(NCH):
                    act.wait_ge(proj_done, 20 * j + 10 + n + 1)
                    act.activation(xa[:, toks(n)], bank[n][:, 0:CH], ACT.Silu).then_inc(bank_free[n], 1)
                high_w(4 * j + 4, 0)
                for n in range(NCH):
                    if n < 2:
                        act.wait_ge(bank_free[0], 4 * j + 3)
                    else:
                        act.wait_ge(b_done, 5 * j + n - 1)
                    act.wait_ge(gated, 5 * j + n + 6)
                    act.wait_ge(a_out[n % 2], left(j, n))
                    act.activation(out_a[:, n % 2, 0:CH], full_t[:, n % 2, :], ACT.Copy).then_inc(a_done, 1)
                high_w(4 * j + 5, 1)
            act.wait_ge(b_done, 20)
            with act.Fori(0, 4) as j:
                for n in range(NCH):
                    keep_full(16 + 2 * j, 2 * j, n, full_done)
                    if n < 2:
                        act.wait_ge(b_done, 5 * (4 + j))
                    else:
                        act.wait_ge(bank_free[n - 2], 18 + 2 * j)
                    through(16 + 2 * j, n, 4 + 2 * j, ACT.Copy).then_inc(a_done, 1)
                    if n:
                        rows_c(2 * j, n - 1).then_inc(c_done, 1)
                rows_c(2 * j, NCH - 1).then_inc(c_done, 1)
                high_w(18 + 2 * j, 0)
                for n in range(NCH + 1):
                    if n < NCH:
                        keep_full(17 + 2 * j, 2 * j + 1, n, bank_free[n])
                    if n:
                        rows_c(2 * j + 1, n - 1).then_inc(c_done, 1)
                        act.wait_ge(a_out[(n - 1) % 2], left(5 + 2 * j, n - 1))
                        if n < 3:
                            act.wait_ge(bank_free[5 - n], 18 + 2 * j)
                        else:
                            act.wait_ge(b_done, 5 * (4 + j) + n - 2)
                        act.activation(out_a[0:SUB, (n - 1) % 2, :], turn_bank[0:SUB, :], ACT.Copy)\
                           .then_inc(a_done, 1)
                high_w(19 + 2 * j, 1)
            with act.Fori(0, 4) as j:
                for n in range(NCH):
                    if n >= 2:
                        act.wait_ge(bank_free[n - 2], 26 + 2 * j)
                    else:
                        act.wait_ge(b_done, 40)
                        act.wait_ge(bank_free[4 - n], 24 + 2 * j)
                    through(24 + 2 * j, n, 12 + 2 * j, ACT.Copy).then_inc(a_done, 1)
                high_w(26 + 2 * j, 0)
                for n in range(NCH):
                    if n < 2:
                        act.wait_ge(bank_free[4 - n], 26 + 2 * j)
                    through(25 + 2 * j, n, 13 + 2 * j, ACT.Silu).then_inc(bank_free[n], 1)
                high_w(27 + 2 * j, 1)
            with act.Fori(0, 7) as j:
                for b in range(2):
                    for n in range(NCH):
                        through(32 + 2 * j + b, n, 20 + 2 * j + b, ACT.Sigmoid).then_inc(bank_free[n], 1)
                    high_w(34 + 2 * j + b, b)
            for b in range(2):
                for n in range(NCH):
                    through(46 + b, n, 34 + b, ACT.Sigmoid).then_inc(bank_free[n], 1)

        @block.vector
        def _(dve):
            dve.memset(U[:, 0:CW - 1], 0.0).then_inc(edges, 1)
            dve.wait_ge(edges, 1)
            dve.wait_ge(const_in, 32)

            def low(n, a, b, src, rows, width):
                dve.wait_ge(a_done, 5 * a + n + 1)
                dve.wait_ge(b_out[n % 2], left(b, n))
                return dve.tensor_tensor(out_b[0:rows, n % 2, 0:width], src,
                                         out_a[0:rows, n % 2, 0:width].bitcast(F32), ALU.subtract)

            with dve.Fori(0, 4) as j:
                t = 4 * j + 1
                dve.wait_ge(frames_out, 32 * j + 16)
                dve.wait_ge(conv_done, 3 * j + 1)
                for n in range(NCH):
                    dve.wait_ge(proj_done, 5 * t + n + 1)
                    for to, col in spans(n, CW - 1):
                        last = dve.tensor_tensor(U[:, to], bank[n][:, col], xa[:, toks(n)][:, col], ALU.mult)
                    last.then_inc(bank_free[n], 1)
                for n in range(NCH):
                    dve.wait_ge(bank_free[n], t + 2)
                dve.wait_ge(state_in, 16 * j + 16)
                dve.wait_ge(gated, 5 * j + 5)
                L = T + CW - 1
                tap = cw[:, bass.ds(j, 1), :].rearrange("p j w -> p (j w)")
                dve.tensor_scalar(conv[:, :], U[:, 0:L], tap[:, 0:1], None, ALU.mult).then_inc(conv_done, 1)
                for x in range(1, CW):
                    dve.wait_ge(conv_done, 3 * j + x + 1)
                    dve.scalar_tensor_tensor(out=conv[:, :], in0=U[:, x:x + L], scalar=tap[:, x:x + 1],
                                             in1=conv[:, :], op0=ALU.mult, op1=ALU.add).then_inc(conv_done, 1)
                dve.wait_ge(conv_done, 3 * j + CW + 1)
                for n in range(NCH + 1):
                    if n < NCH:
                        dve.wait_ge(proj_done, 5 * (t + 2) + n + 1)
                        if n >= 2:
                            dve.wait_ge(b_done, 5 * j + n - 1)
                        for to, col in spans(n, 0):
                            last = dve.tensor_tensor(full_t[:, n % 2, col], bank[n][:, col], conv[:, to], ALU.mult)
                        last.then_inc(bank_free[n], 1)
                        dve.wait_ge(bank_free[n], t + 4)
                        dve.tensor_tensor(full_t[:, n % 2, :], full_t[:, n % 2, :], xa[:, toks(n)], ALU.mult)\
                           .then_inc(gated, 1)
                    if n:
                        low(n - 1, j, j, full_t[:, (n - 1) % 2, :], P, CH).then_inc(b_done, 1)
            with dve.Fori(0, 4) as j:
                for n in range(NCH):
                    low(n, 4 + 2 * j, 4 + 2 * j, bank[n][:, 0:CH], P, CH).then_inc(bank_free[n], 1)
                for n in range(NCH):
                    low(n, 5 + 2 * j, 5 + 2 * j, turn_bank[0:SUB, :], SUB, 4 * P).then_inc(b_done, 1)
            with dve.Fori(0, 4) as j:
                for n in range(NCH):
                    low(n, 12 + j, 12 + j, bank[n][:, 0:CH], P, CH).then_inc(bank_free[n], 1)


def prompt_attention(nc, root, s, ident, causal):
    with ExitStack() as ctx:
        sb, pb, sem = tools(nc, ctx, root, "at")
        HR = HD + 4
        ks = sb("ks", [P, 2, SEQ], F32R)
        qs = sb("qs", [P, 2, SEQ], F32R)
        k2 = sb("k2", [HR, 2, SEQ], F32R)
        q2 = sb("q2", [HR, 2, SEQ], F32R)
        km = sb("km", [HR, 2, SEQ], F32R)
        qm = sb("qm", [HR, 2, SEQ], F32R)
        v_hi = sb("v_hi", [P, 2, NB, P], F32R)
        v_lo = sb("v_lo", [P, 2, NB, P], F32R)
        zb = sb("zb", [HD, 2, SEQ])
        RING = 4
        p = sb("p", [P, RING, QW])
        p_hi = sb("p_hi", [P, RING, QW], F32R)
        p_lo = sb("p_lo", [P, RING, QW], F32R)
        eye = sb("eye", [P, P])
        mask = sb("mask", [P, P])
        eye_b = sb("eye_b", [P, P], BF16)
        mask_b = sb("mask_b", [P, P], BF16)
        piece_max = sb("piece_max", [P, NB, NQ])
        row_max = sb("row_max", [P, NB])
        neg_max = sb("neg_max", [P, 2 * NB], F32R)
        neg_rows = sb("neg_rows", [2 * NB, P])
        y = sb("y", [HD + 1, 2, SEQ])
        sums = sb("sums", [P, NB])
        rcp = sb("rcp", [P, NB])
        rcp_all = sb("rcp_all", [HD, SEQ])
        y_hi = sb("y_hi", [HD, 2, QW], F32R)
        y_lo = sb("y_lo", [HD, 2, QW], F32R)
        s_bank = [pb(f"s{i}") for i in range(RING)]
        o_bank = [pb(f"o{i}") for i in range(2)]
        m_bank = [pb(f"m{i}") for i in range(2)]

        const_in, ones_set, consts = sem("const_in"), sem("ones_set"), sem("consts")
        main_in = [sem(f"main_in{i}") for i in range(2)]
        max_in = [sem(f"max_in{i}") for i in range(2)]
        m_in = [sem(f"m_in{i}") for i in range(2)]
        s_done = sem("s_done")
        p_done = sem("p_done")
        lo_dve, lo_pool = sem("lo_dve"), sem("lo_pool")
        pv_done = sem("pv_done")
        unit_done = sem("unit_done")
        unit_read = sem("unit_read")
        maxed, split, turned, rows_done = sem("maxed"), sem("split"), sem("turned"), sem("rows_done")
        o_read = sem("o_read")
        sum_out, sums_in, rcp_done, rcp_out, rcp_in = (
            sem("sum_out"), sem("sums_in"), sem("rcp_done"), sem("rcp_out"), sem("rcp_in"))
        zb_in = [sem(f"zb_in{i}") for i in range(2)]
        y_scaled = sem("y_scaled")
        y_gated, yh_done, yl_done = sem("y_gated"), sem("yh_done"), sem("yl_done")
        y_out = [sem(f"y_out{i}") for i in range(2)]
        sp_passed = sem("sp_passed")

        steps = [(q, kb) for q in range(NQ) for kb in range(4 * q + 4)]
        NS = len(steps)
        ends = [steps.index((q, 4 * q + 3)) for q in range(NQ)]
        units = [(i, c) for i in range(NB) for c in range(i // 4 + 1)]
        NU = len(units)
        LEAD = 3
        POOLS = 4

        def step_units(st):
            return range(min(NU, st * 4 // 3), min(NU, (st + 1) * 4 // 3))

        INVERT = 13
        FINISH = {14 + 6 * q + 2 * x: (q, x) for x in range(3) for q in range(NQ)}
        FINISH_LOW = {st + 5: q for st, (q, x) in FINISH.items() if x == 0}
        TURN = 31

        def low_value(h, st):
            if st % POOLS == POOLS - 1:
                return lo_pool, NS // POOLS * h + st // POOLS + 1
            return lo_dve, (NS - NS // POOLS) * h + st - st // POOLS + 1

        def used(h, b, per):
            return per * (h // 2 + 1) if isinstance(h, int) else (h - b) * (per // 2) + per

        def finishing(eng):
            def scale(h, b, q):
                if q == 0:
                    eng.wait_ge(rcp_in, 16 * h + 16)
                    eng.wait_ge(zb_in[b], used(h, b, 16))
                at = y[0:HD, b, q * QW:(q + 1) * QW]
                eng.tensor_tensor(at, at, rcp_all[:, q * QW:(q + 1) * QW], ALU.mult).then_inc(y_scaled, 1)

            def gate(h, b, q):
                eng.wait_ge(y_scaled, NQ * h + q + 1)
                at = y[0:HD, b, q * QW:(q + 1) * QW]
                eng.tensor_tensor(at, at, zb[:, b, q * QW:(q + 1) * QW], ALU.mult).then_inc(y_gated, 1)

            def lower(h, b, q):
                eng.wait_ge(yh_done, NQ * h + q + 1)
                eng.tensor_tensor(y_lo[:, q % 2, :], y[0:HD, b, q * QW:(q + 1) * QW], y_hi[:, q % 2, :].bitcast(F32),
                                  ALU.subtract).then_inc(yl_done, 1)
            return scale, gate, lower

        block = ctx.enter_context(nc.Block())

        @block.sync
        def _(sp):
            wait = settled(sp, sp_passed)
            sp.dma_start(eye[:, :], ident).then_inc(const_in, 16)
            sp.dma_start(mask[:, :], causal).then_inc(const_in, 16)
            for q in y_out:
                sp.sem_inc(q, 16)
            sp.wait_ge(ones_set, 6)

            def load_max(h, b):
                rows = bass.ds(h * HD, HD)
                for to, of in ((km[0:HD, b], s["kh"][rows, 0:SEQ]), (qm[0:HD, b], s["qh"][rows, 0:SEQ]),
                               (km[HD:HD + 2, b], s["ck"][:, bass.ds(h, 1), 0:SEQ].rearrange("a h t -> a (h t)"))):
                    sp.dma_start(to.bitcast(F32), of).then_inc(max_in[b], 16)

            def load_main(h, b):
                rows = bass.ds(h * HD, HD)
                ck = s["ck"][:, bass.ds(h, 1), 0:SEQ].rearrange("a h t -> a (h t)")
                for to, of in ((ks[0:HD, b], s["kh"][rows, 0:SEQ]), (ks[HD:P, b], s["kl"][rows, 0:SEQ]),
                               (qs[0:HD, b], s["qh"][rows, 0:SEQ]), (qs[HD:P, b], s["qh"][rows, 0:SEQ]),
                               (k2[0:HD, b], s["kh"][rows, 0:SEQ]), (k2[HD:HD + 2, b], ck),
                               (q2[0:HD, b], s["ql"][rows, 0:SEQ])):
                    sp.dma_start(to.bitcast(F32), of).then_inc(main_in[b], 16)
                for to, of in ((v_hi, s["vh"]), (v_lo, s["vl"])):
                    sp.dma_start(to[:, b, :, 0:HD].bitcast(F32), of[0:SEQ, rows].rearrange("(b p) c -> p b c", p=P))\
                      .then_inc(main_in[b], 16)

            def max_rows(h, b):
                wait(rows_done, h + 1)
                for i in range(2):
                    sp.dma_start(q2[HD + 2 + i:HD + 3 + i, b, :].bitcast(F32).rearrange("a (t q) -> a t q", q=P),
                                 neg_rows[i * NB:(i + 1) * NB, :]).then_inc(m_in[b], 16)

            def y_store(h, b, q):
                wait(yl_done, NQ * h + q + 1)
                for to, of in ((s["ybh"], y_hi), (s["ybl"], y_lo)):
                    sp.dma_start(to[bass.ds(h * HD, HD), q * QW:(q + 1) * QW], of[:, q % 2, :].bitcast(F32))\
                      .then_inc(y_out[q % 2], 16)

            def sum_store(h, b, q):
                wait(o_read, NQ * h + q + 3)
                sp.dma_start(s["sums"][bass.ds(h, 1), q * QW:(q + 1) * QW], y[HD:HD + 1, b, q * QW:(q + 1) * QW])\
                  .then_inc(sum_out, 16)

            def rcp_rows(h):
                row = s["sums"][bass.ds(h, 1), :]
                wait(sum_out, 64 * h + 64)
                sp.dma_start(sums[:, :], row.rearrange("a (p b) -> (a p) b", p=P)).then_inc(sums_in, 16)
                wait(rcp_done, h + 1)
                row = s["rcps"][bass.ds(h, 1), :]
                sp.dma_start(row.rearrange("a (p b) -> (a p) b", p=P), rcp[:, :]).then_inc(rcp_out, 16)
                wait(rcp_out, 16 * h + 16)
                sp.dma_start(rcp_all[:, :], row.broadcast_to([HD, SEQ])).then_inc(rcp_in, 16)

            def head(h, b, more=True, most=True):
                before = not isinstance(h, int) or h > 0
                if more:
                    wait(pv_done, NS * h + RING)
                    load_main(h + 1, 1 - b)
                if most:
                    load_max(h + 2, b)
                sp.dma_start(zb[:, b], s["zb"][bass.ds(h * HD, HD), 0:SEQ]).then_inc(zb_in[b], 16)
                if before:
                    rcp_rows(h - 1)
                for q in range(2):
                    sum_store(h, b, q)
                if before:
                    y_store(h - 1, 1 - b, 0)
                sum_store(h, b, 2)
                if before:
                    y_store(h - 1, 1 - b, 1)
                if more:
                    max_rows(h + 1, 1 - b)
                if before:
                    y_store(h - 1, 1 - b, 2)
                    y_store(h - 1, 1 - b, 3)
                sum_store(h, b, 3)

            load_max(0, 0)
            load_main(0, 0)
            load_max(1, 1)
            max_rows(0, 0)
            head(0, 0)
            head(1, 1)
            with sp.Fori(1, H // 2 - 1) as i:
                head(2 * i, 0)
                head(2 * i + 1, 1)
            head(H - 2, 0, True, False)
            head(H - 1, 1, False, False)
            rcp_rows(H - 1)
            for q in range(NQ):
                y_store(H - 1, 1, q)
            sp.wait_ge(y_out[0], 16 + 32 * NQ // 2 * H)
            sp.wait_ge(y_out[1], 16 + 32 * NQ // 2 * H)

        @block.tensor
        def _(pe):
            def scores(h, b, st):
                q, kb = steps[st]
                d = max(0, kb - 4 * q)
                keys, cols = slice(kb * P, (kb + 1) * P), slice(d * P, QW)
                asked = slice(q * QW + d * P, (q + 1) * QW)
                if st == 0:
                    pe.wait_ge(main_in[b], used(h, b, 144))
                    pe.wait_ge(m_in[b], used(h, b, 32))
                pe.wait_ge(p_done, NS * h + st + 1)
                bank = s_bank[st % RING]
                diagonal = kb >= 4 * q
                pe.matmul(bank[:, cols], ks[:, b, keys], qs[:, b, asked], start=True, stop=False)
                last = pe.matmul(bank[:, cols], k2[:, b, keys], q2[:, b, asked], start=False, stop=not diagonal)
                if diagonal:
                    last = pe.matmul(bank[:, d * P:(d + 1) * P], eye_b[:, :], mask_b[:, :], start=False, stop=True)
                last.then_inc(s_done, 1)

            def values(h, b, st):
                q, kb = steps[st]
                d = max(0, kb - 4 * q)
                cols = slice(d * P, QW)
                if kb == 0:
                    pe.wait_ge(o_read, NQ * h + q + 1)
                pe.wait_ge(*low_value(h, st))
                r = st % RING
                o = o_bank[q % 2][:, cols]
                pe.matmul(o, v_hi[:, b, kb, :], p_hi[:, r, cols], start=(kb == 0), stop=False)
                pe.matmul(o, v_hi[:, b, kb, :], p_lo[:, r, cols], start=False, stop=False)
                pe.matmul(o, v_lo[:, b, kb, :], p_hi[:, r, cols], start=False, stop=(kb == 4 * q + 3))\
                  .then_inc(pv_done, 1)

            def unit(h, b, u):
                i, c = units[u]
                end = min((c + 1) * QW, (i + 1) * P)
                width = end - c * QW
                if u == 0:
                    pe.wait_ge(max_in[b], used(h, b, 48))
                    if not isinstance(h, int) or h:
                        pe.wait_ge(rows_done, h)
                pe.wait_ge(unit_read, NU * h + u + 1)
                bank = m_bank[u % 2]
                last = pe.matmul(bank[:, 0:width], qm[0:HD + 2, b, i * P:(i + 1) * P], km[0:HD + 2, b, c * QW:end],
                                 start=True, stop=(c < i // 4))
                if c == i // 4:
                    last = pe.matmul(bank[:, width - P:width], mask_b[:, :], eye_b[:, :], start=False, stop=True)
                last.then_inc(unit_done, 1)

            def turn(h):
                pe.wait_ge(split, h + 1)
                pe.transpose(m_bank[0][0:2 * NB, 0:P], neg_max[:, :].bitcast(F32), eye[:, :]).then_inc(turned, 1)

            def head(h, b, more=True, ahead=True):
                for st in range(NS):
                    if st + LEAD < NS:
                        scores(h, b, st + LEAD)
                    elif ahead:
                        scores(h + 1, 1 - b, st + LEAD - NS)
                    if more:
                        for u in step_units(st):
                            unit(h + 1, 1 - b, u)
                        if st == TURN:
                            turn(h + 1)
                    values(h, b, st)

            pe.wait_ge(consts, 2)
            for u in range(NU):
                unit(0, 0, u)
            turn(0)
            for st in range(LEAD):
                scores(0, 0, st)
            with pe.Fori(0, H // 2 - 1) as i:
                head(2 * i, 0)
                head(2 * i + 1, 1)
            head(H - 2, 0)
            head(H - 1, 1, False, False)

        @block.scalar
        def _(act):
            act.sem_inc(p_done, RING)
            act.sem_inc(pv_done, RING)
            act.sem_inc(unit_read, 2)
            act.sem_inc(o_read, 2)

            def probs(h, st):
                q, kb = steps[st]
                cols = slice(max(0, kb - 4 * q) * P, QW)
                r = st % RING
                act.wait_ge(s_done, NS * h + st + 1)
                act.wait_ge(pv_done, NS * h + st + 1)
                act.activation(p[:, r, cols], s_bank[r][:, cols], ACT.Exp, scale=SCALE)
                act.activation(p_hi[:, r, cols], s_bank[r][:, cols], ACT.Exp, scale=SCALE).then_inc(p_done, 1)

            def copy_rows(h, b):
                act.wait_ge(turned, h + 1)
                if not isinstance(h, int) or h:
                    act.wait_ge(m_in[1 - b], used(h - 1, 1 - b, 32))
                act.activation(neg_rows[:, :], m_bank[0][0:2 * NB, 0:P], ACT.Copy).then_inc(rows_done, 1)

            def head(h, b, more=True):
                for st in range(NS):
                    probs(h, st)
                    if more and st == TURN + 1:
                        copy_rows(h + 1, 1 - b)
                    if st in FINISH and FINISH[st][1] == 2 and (not isinstance(h, int) or h):
                        upper(h - 1, 1 - b, FINISH[st][0])

            def upper(h, b, q):
                act.wait_ge(y_gated, NQ * h + q + 1)
                act.wait_ge(y_out[q % 2], 64 * h + 32 * (q // 2) + 16)
                act.activation(y_hi[:, q % 2, :], y[0:HD, b, q * QW:(q + 1) * QW], ACT.Copy).then_inc(yh_done, 1)

            copy_rows(0, 0)
            head(0, 0)
            head(1, 1)
            with act.Fori(1, H // 2 - 1) as i:
                head(2 * i, 0)
                head(2 * i + 1, 1)
            head(H - 2, 0)
            head(H - 1, 1, False)
            for q in range(NQ):
                upper(H - 1, 1, q)

        @block.vector
        def _(dve):
            dve.wait_ge(const_in, 32)
            dve.tensor_copy(eye_b[:, :], eye[:, :]).then_inc(consts, 1)
            dve.tensor_copy(mask_b[:, :], mask[:, :]).then_inc(consts, 1)

            scale, gate, lower = finishing(dve)

            def low(h, st):
                if st % POOLS == POOLS - 1:
                    return
                q, kb = steps[st]
                cols = slice(max(0, kb - 4 * q) * P, QW)
                r = st % RING
                dve.wait_ge(p_done, NS * h + st + 1 + RING)
                dve.tensor_tensor(p_lo[:, r, cols], p[:, r, cols], p_hi[:, r, cols].bitcast(F32), ALU.subtract)\
                   .then_inc(lo_dve, 1)

            def unit(h, u):
                i, c = units[u]
                width = min((c + 1) * QW, (i + 1) * P) - c * QW
                dve.wait_ge(unit_done, NU * h + u + 1)
                dve.tensor_reduce(piece_max[:, i, c:c + 1], m_bank[u % 2][:, 0:width], AX_X, ALU.max)\
                   .then_inc(unit_read, 1)

            def whole_max(h):
                dve.wait_ge(unit_read, NU * h + NU + 2)
                if not isinstance(h, int) or h:
                    dve.wait_ge(turned, h)
                dve.tensor_reduce(row_max[:, :], piece_max[:, :, :], AX_X, ALU.max).then_inc(maxed, 1)
                dve.wait_ge(maxed, 2 * h + 1)
                dve.tensor_scalar(neg_max[:, 0:NB], row_max[:, :], -1.0, None, ALU.mult).then_inc(maxed, 1)
                dve.wait_ge(maxed, 2 * h + 2)
                dve.scalar_tensor_tensor(out=neg_max[:, NB:2 * NB], in0=row_max[:, :], scalar=-1.0,
                                         in1=neg_max[:, 0:NB].bitcast(F32), op0=ALU.mult, op1=ALU.subtract)\
                   .then_inc(split, 1)

            def take(h, b, q):
                dve.wait_ge(pv_done, NS * h + ends[q] + 1 + RING)
                if not isinstance(h, int) or h > 1:
                    dve.wait_ge(yl_done, NQ * (h - 1))
                dve.tensor_copy(y[:, b, q * QW:(q + 1) * QW], o_bank[q % 2][0:HD + 1, :]).then_inc(o_read, 1)

            def invert(h):
                dve.wait_ge(sums_in, 16 * h + 16)
                if not isinstance(h, int) or h:
                    dve.wait_ge(rcp_out, 16 * h)
                dve.reciprocal(rcp[:, :], sums[:, :]).then_inc(rcp_done, 1)

            def head(h, b, more=True):
                for st in range(NS):
                    if st + 1 < NS:
                        low(h, st + 1)
                    elif more or not b:
                        low(h + 1, 0)
                    if more:
                        for u in step_units(st):
                            unit(h + 1, u)
                            if u == NU - 1:
                                whole_max(h + 1)
                    if st - 2 in ends[:-1]:
                        take(h, b, ends.index(st - 2))
                    if b and st == 1:
                        take(h - 1, 1 - b, NQ - 1)
                    if st == INVERT and (not isinstance(h, int) or h):
                        invert(h - 1)
                if b:
                    take(h, b, NQ - 1)

            for t in (k2, q2, qm):
                dve.memset(t[HD:HR, :, :].bitcast(F32), 1.0).then_inc(ones_set, 1)
            dve.wait_ge(ones_set, 6)
            for u in range(NU):
                unit(0, u)
            whole_max(0)
            low(0, 0)
            head(0, 0)
            head(1, 1)
            with dve.Fori(1, H // 2 - 1) as i:
                head(2 * i, 0)
                head(2 * i + 1, 1)
            head(H - 2, 0)
            head(H - 1, 1, False)
            invert(H - 1)
            for q in range(NQ):
                scale(H - 1, 1, q)
                gate(H - 1, 1, q)
            for q in range(NQ):
                lower(H - 1, 1, q)

        @block.gpsimd
        def _(pool):
            pool.memset(v_hi[:, :, :, HD:P].bitcast(F32), 1.0).then_inc(ones_set, 1)
            pool.memset(v_lo[:, :, :, HD:P].bitcast(F32), 0.0).then_inc(ones_set, 1)
            pool.memset(piece_max[:, :, :], -3e38).then_inc(ones_set, 1)

            def low(h, st):
                q, kb = steps[st]
                cols = slice(max(0, kb - 4 * q) * P, QW)
                r = st % RING
                pool.wait_ge(p_done, NS * h + st + 1 + RING)
                pool.tensor_tensor(p_lo[:, r, cols], p[:, r, cols], p_hi[:, r, cols].bitcast(F32), ALU.subtract)\
                    .then_inc(lo_pool, 1)

            scale, gate, lower = finishing(pool)

            def head(h, b):
                before = not isinstance(h, int) or h > 0
                for st in range(NS):
                    if st % POOLS == POOLS - 1:
                        low(h, st)
                    if before and st in FINISH_LOW:
                        lower(h - 1, 1 - b, FINISH_LOW[st])
                    if before and st in FINISH and FINISH[st][1] < 2:
                        (scale, gate)[FINISH[st][1]](h - 1, 1 - b, FINISH[st][0])

            head(0, 0)
            head(1, 1)
            with pool.Fori(1, H // 2) as i:
                head(2 * i, 0)
                head(2 * i + 1, 1)


def sample_attention(nc, root, s, cache_k, cache_v, ident, causal, blocks):
    with ExitStack() as ctx:
        sb, pb, sem = tools(nc, ctx, root, "sa")
        NK = NB + 1
        KEYS = NK * P
        PAIRS = H // 2
        HQ = H * DEC
        kT_hi = sb("kT_hi", [P, PAIRS, KEYS], F32R)
        kT_lo = sb("kT_lo", [P, PAIRS, KEYS], F32R)
        v_hi = sb("v_hi", [P, NK, ATT], F32R)
        v_lo = sb("v_lo", [P, NK, ATT], F32R)
        k_rows = sb("k_rows", [P, 2, ATT])
        v_rows = sb("v_rows", [P, 2, ATT])
        ck = sb("ck", [2 * H + 2, KEYS], F32R)
        pick32 = sb("pick32", [2 * H, HQ])
        pick = sb("pick", [2 * H + 2, HQ], F32R)
        q_hi = sb("q_hi", [P, PAIRS, HQ], F32R)
        q_lo = sb("q_lo", [P, PAIRS, HQ], F32R)
        zb = sb("zb", [P, PAIRS, DEC])
        ones = sb("ones", [P, P], F32R)
        p = sb("p", [P, 2, HQ])
        p_hi = sb("p_hi", [P, 2, HQ], F32R)
        p_lo = sb("p_lo", [P, 2, HQ], F32R)
        eye = sb("eye", [P, P])
        mask = sb("mask", [P, P])
        eye_b = sb("eye_b", [P, P], BF16)
        mask_b = sb("mask_b", [P, H, DEC], BF16)
        piece_max = sb("piece_max", [P, 2, 5])
        row_max = sb("row_max", [P, 2])
        neg_max = sb("neg_max", [P, 4], F32R)
        neg_rows = sb("neg_rows", [4, P])
        rcp = sb("rcp", [P, HQ])
        y = sb("y", [P, PAIRS, DEC])
        y_hi = sb("y_hi", [P, PAIRS, DEC], F32R)
        y_lo = sb("y_lo", [P, PAIRS, DEC], F32R)
        t_bank = [pb(f"t{i}") for i in range(2)]
        s_bank = [pb(f"s{i}") for i in range(2)]
        o_bank, sum_bank = pb("o"), pb("sum")

        const_in, zeroed, ck_set, consts = sem("const_in"), sem("zeroed"), sem("ck_set"), sem("consts")
        k_in = [sem(f"k_in{i}") for i in range(2)]
        v_in = [sem(f"v_in{i}") for i in range(2)]
        new_in, ck_in, m_in, out = sem("new_in"), sem("ck_in"), sem("m_in"), sem("out")
        turned, k_hi_done, k_lo_done, v_hi_done, v_lo_done = (
            sem("turned"), sem("k_hi"), sem("k_lo"), sem("v_hi"), sem("v_lo"))
        unit_done, unit_read, maxed, split, m_turned, rows_done = (
            sem("unit"), sem("unit_read"), sem("maxed"), sem("split"), sem("m_turned"), sem("rows"))
        s_done, p_done, lo_done, pv_done = sem("s"), sem("p"), sem("lo"), sem("pv")
        rcp_done, y_done, yh_done, yl_done, sp_passed = (
            sem("rcp"), sem("y"), sem("yh"), sem("yl"), sem("sp_passed"))
        pieces = [(c * 512, 512) for c in range(4)] + [(PAST, DEC)]
        NEW = slice(PAST, PAST + DEC)

        block = ctx.enter_context(nc.Block())

        @block.sync
        def _(sp):
            wait = settled(sp, sp_passed)

            def load(t, b):
                rows = slice(t * P, (t + 1) * P) if isinstance(t, int) else bass.ds(t * P, P)
                sp.dma_start(k_rows[:, b], cache_k[rows, :]).then_inc(k_in[b], 16)
                sp.dma_start(v_rows[:, b], cache_v[rows, :]).then_inc(v_in[b], 16)

            sp.dma_start(eye[:, :], ident).then_inc(const_in, 16)
            load(0, 0)
            load(1, 1)
            sp.dma_start(mask[:, :], causal).then_inc(const_in, 16)
            sp.dma_start(pick32[:, :], blocks).then_inc(const_in, 16)
            sp.dma_start(zb[:, :, :], s["zb"][:, SEQ:T].rearrange("(a p) q -> p a q", p=P)).then_inc(const_in, 16)
            sp.wait_ge(zeroed, 7)
            sp.wait_ge(ck_set, 1)
            for i in range(2):
                sp.dma_start(ck[i * H:(i + 1) * H, 0:PAST + DEC].bitcast(F32), s["ck"][i, :, SEQ:CKW]).then_inc(ck_in, 16)
            for to, of in ((q_hi, s["qh"]), (q_lo, s["ql"])):
                for h in range(H):
                    a, at = h // 2, HD * (h % 2)
                    sp.dma_start(to[at:at + HD, a, h * DEC:(h + 1) * DEC].bitcast(F32),
                                 of[h * HD:(h + 1) * HD, SEQ:T]).then_inc(new_in, 16)
            for to, of in ((kT_hi, s["kh"]), (kT_lo, s["kl"])):
                sp.dma_start(to[:, :, NEW].bitcast(F32), of[:, SEQ:T].rearrange("(a p) q -> p a q", p=P)).then_inc(new_in, 16)
            for to, of in ((v_hi, s["vh"]), (v_lo, s["vl"])):
                sp.dma_start(to[0:DEC, NB, :].bitcast(F32), of[SEQ:T, :]).then_inc(new_in, 16)
            with sp.Fori(0, NB // 2 - 1) as i:
                for b in range(2):
                    wait(turned, 2 * i + b + 1)
                    wait(v_lo_done, 2 * i + b + 1)
                    load(2 * i + b + 2, b)
            sp.wait_ge(rows_done, 1)
            for i in range(4):
                sp.dma_start(pick[2 * H + i // 2:2 * H + i // 2 + 1, (i % 2) * P:(i % 2 + 1) * P].bitcast(F32),
                             neg_rows[i:i + 1, :]).then_inc(m_in, 16)
            sp.wait_ge(yl_done, 1)
            for to, of in ((s["ybh"], y_hi), (s["ybl"], y_lo)):
                sp.dma_start(to[:, SEQ:T].rearrange("(a p) q -> p a q", p=P), of[:, :, :].bitcast(F32)).then_inc(out, 16)
            sp.wait_ge(out, 32)

        @block.gpsimd
        def _(pool):
            for n, (t, x) in enumerate(((q_hi[:, :, :], 0.0), (q_lo[:, :, :], 0.0), (kT_hi[:, :, PAST:KEYS], 0.0),
                                        (kT_lo[:, :, PAST:KEYS], 0.0), (v_hi[:, NB, :], 0.0), (v_lo[:, NB, :], 0.0),
                                        (ones[:, :], 1.0))):
                pool.memset(t.bitcast(F32), x).then_inc(zeroed, 1)

        @block.scalar
        def _(act):
            act.sem_inc(k_lo_done, 2)
            with act.Fori(0, NB // 2) as i:
                for b in range(2):
                    t = 2 * i + b
                    act.wait_ge(turned, t + 1)
                    act.activation(kT_hi[:, :, bass.ds(t * P, P)], t_bank[b][:, :].rearrange("p (a c) -> p a c", a=PAIRS),
                                   ACT.Copy).then_inc(k_hi_done, 1)
                    act.wait_ge(v_in[b], 16 * i + 16)
                    act.activation(v_hi[:, bass.ds(t, 1), :].rearrange("p a c -> p (a c)"), v_rows[:, b], ACT.Copy)\
                       .then_inc(v_hi_done, 1)
            act.wait_ge(m_turned, 1)
            act.activation(neg_rows[:, :], t_bank[0][0:4, 0:P], ACT.Copy).then_inc(rows_done, 1)
            for kb in range(NK):
                r = kb % 2
                act.wait_ge(s_done, kb + 1)
                if kb >= 2:
                    act.wait_ge(pv_done, kb - 1)
                act.activation(p[:, r, :], s_bank[r][:, 0:HQ], ACT.Exp, scale=SCALE)
                act.activation(p_hi[:, r, :], s_bank[r][:, 0:HQ], ACT.Exp, scale=SCALE).then_inc(p_done, 1)
            act.wait_ge(y_done, 3)
            act.activation(y_hi[:, :, :], y[:, :, :], ACT.Copy).then_inc(yh_done, 1)

        @block.vector
        def _(dve):
            dve.memset(ck[:, :].bitcast(F32), 1.0).then_inc(ck_set, 1)
            dve.memset(pick[:, :].bitcast(F32), 0.0).then_inc(consts, 1)
            dve.wait_ge(const_in, 64)
            dve.wait_ge(consts, 1)
            dve.tensor_copy(pick[0:2 * H, :], pick32[:, :]).then_inc(consts, 1)
            dve.tensor_copy(eye_b[:, :], eye[:, :]).then_inc(consts, 1)
            for h in range(H):
                dve.tensor_copy(mask_b[:, h, :], mask[:, 0:DEC]).then_inc(consts, 1)
            with dve.Fori(0, NB // 2) as i:
                for b in range(2):
                    t = 2 * i + b
                    dve.wait_ge(k_hi_done, t + 1)
                    at = bass.ds(t * P, P)
                    dve.tensor_tensor(kT_lo[:, :, at], t_bank[b][:, :].rearrange("p (a c) -> p a c", a=PAIRS),
                                      kT_hi[:, :, at].bitcast(F32), ALU.subtract).then_inc(k_lo_done, 1)
                    dve.wait_ge(v_hi_done, t + 1)
                    one = bass.ds(t, 1)
                    dve.tensor_tensor(v_lo[:, one, :].rearrange("p a c -> p (a c)"), v_rows[:, b],
                                      v_hi[:, one, :].rearrange("p a c -> p (a c)").bitcast(F32), ALU.subtract)\
                       .then_inc(v_lo_done, 1)
            for g in range(2):
                for c, (_, width) in enumerate(pieces):
                    dve.wait_ge(unit_done, 5 * g + c + 1)
                    dve.tensor_reduce(piece_max[:, g, c:c + 1], t_bank[(5 * g + c) % 2][:, 0:width], AX_X, ALU.max)\
                       .then_inc(unit_read, 1)
            dve.wait_ge(unit_read, 10)
            dve.tensor_reduce(row_max[:, :], piece_max[:, :, :], AX_X, ALU.max).then_inc(maxed, 1)
            dve.wait_ge(maxed, 1)
            dve.tensor_scalar(neg_max[:, 0:2], row_max[:, :], -1.0, None, ALU.mult).then_inc(maxed, 1)
            dve.wait_ge(maxed, 2)
            dve.scalar_tensor_tensor(out=neg_max[:, 2:4], in0=row_max[:, :], scalar=-1.0,
                                     in1=neg_max[:, 0:2].bitcast(F32), op0=ALU.mult, op1=ALU.subtract)\
               .then_inc(split, 1)
            for kb in range(NK):
                r = kb % 2
                dve.wait_ge(p_done, kb + 1)
                dve.tensor_tensor(p_lo[:, r, :], p[:, r, :], p_hi[:, r, :].bitcast(F32), ALU.subtract).then_inc(lo_done, 1)
            dve.wait_ge(pv_done, NK)
            dve.reciprocal(rcp[:, :], sum_bank[:, 0:HQ]).then_inc(rcp_done, 1)
            dve.wait_ge(rcp_done, 1)
            for i in range(2):
                rows = slice(i * HD, (i + 1) * HD)
                o = o_bank[rows, 0:HQ].rearrange("p (a c) -> p a c", a=PAIRS)[:, :, i * DEC:(i + 1) * DEC]
                w = rcp[rows, :].rearrange("p (a c) -> p a c", a=PAIRS)[:, :, i * DEC:(i + 1) * DEC]
                dve.tensor_tensor(y[rows, :, :], o, w, ALU.mult).then_inc(y_done, 1)
            dve.wait_ge(y_done, 2)
            dve.tensor_tensor(y[:, :, :], y[:, :, :], zb[:, :, :], ALU.mult).then_inc(y_done, 1)
            dve.wait_ge(yh_done, 1)
            dve.tensor_tensor(y_lo[:, :, :], y[:, :, :], y_hi[:, :, :].bitcast(F32), ALU.subtract).then_inc(yl_done, 1)

        @block.tensor
        def _(pe):
            pe.wait_ge(const_in, 64)
            with pe.Fori(0, NB // 2) as i:
                for b in range(2):
                    t = 2 * i + b
                    pe.wait_ge(k_in[b], 16 * i + 16)
                    pe.wait_ge(k_lo_done, t + 1)
                    for a in range(PAIRS):
                        last = pe.transpose(t_bank[b][:, a * P:(a + 1) * P], k_rows[:, b, a * P:(a + 1) * P], eye[:, :])
                    last.then_inc(turned, 1)
            pe.wait_ge(k_lo_done, NB + 2)
            pe.wait_ge(consts, 3 + H)
            pe.wait_ge(zeroed, 7)
            pe.wait_ge(ck_in, 32)
            pe.wait_ge(new_in, 16 * (2 * H + 4))
            for g in range(2):
                rows = slice(g * P, (g + 1) * P)
                for c, (at, width) in enumerate(pieces):
                    u = 5 * g + c
                    if u >= 2:
                        pe.wait_ge(unit_read, u - 1)
                    to = t_bank[u % 2][:, 0:width]
                    keys = slice(at, at + width)
                    pe.matmul(to, pick[0:2 * H, rows], ck[0:2 * H, keys], start=True, stop=False)
                    for a in (2 * g, 2 * g + 1):
                        last = pe.matmul(to, q_hi[:, a, rows], kT_hi[:, a, keys], start=False,
                                         stop=(a == 2 * g + 1 and c < 4))
                    if c == 4:
                        last = pe.matmul(to, mask_b[:, 4 * g:4 * g + 4, :].rearrange("p h q -> p (h q)"),
                                         eye_b[:, 0:DEC], start=False, stop=True)
                    last.then_inc(unit_done, 1)
            pe.wait_ge(split, 1)
            pe.transpose(t_bank[0][0:4, 0:P], neg_max[:, :].bitcast(F32), eye[:, :]).then_inc(m_turned, 1)
            pe.wait_ge(m_in, 64)
            pe.wait_ge(v_lo_done, NB)

            def scores(kb):
                if kb >= 2:
                    pe.wait_ge(p_done, kb - 1)
                keys = slice(kb * P, (kb + 1) * P)
                bank = s_bank[kb % 2]
                pe.matmul(bank[:, 0:HQ], ck[:, keys], pick[:, :], start=True, stop=False, skip_group_check=True)
                for a in range(PAIRS):
                    own = slice(a * 2 * DEC, (a + 1) * 2 * DEC)
                    for w, x in ((kT_hi, q_hi), (kT_hi, q_lo), (kT_lo, q_hi)):
                        last = pe.matmul(bank[:, own], w[:, a, keys], x[:, a, own], start=False,
                                         stop=(kb < NB and a == PAIRS - 1 and w is kT_lo), skip_group_check=True)
                if kb == NB:
                    last = pe.matmul(bank[:, 0:HQ], eye_b[:, :], mask_b[:, :, :].rearrange("p h q -> p (h q)"),
                                     start=False, stop=True, skip_group_check=True)
                last.then_inc(s_done, 1)

            def values(kb):
                pe.wait_ge(lo_done, kb + 1)
                r = kb % 2
                first, final = kb == 0, kb == NK - 1
                for a in range(PAIRS):
                    own = slice(a * 2 * DEC, (a + 1) * 2 * DEC)
                    feat = slice(a * P, (a + 1) * P)
                    for n, (w, x) in enumerate(((v_hi, p_hi), (v_hi, p_lo), (v_lo, p_hi))):
                        pe.matmul(o_bank[:, own], w[:, kb, feat], x[:, r, own], start=(first and a == 0 and n == 0),
                                  stop=(final and a == PAIRS - 1 and n == 2), skip_group_check=True)
                pe.matmul(sum_bank[:, 0:HQ], ones[:, :], p_hi[:, r, :], start=first, stop=False)
                pe.matmul(sum_bank[:, 0:HQ], ones[:, :], p_lo[:, r, :], start=False, stop=final).then_inc(pv_done, 1)

            scores(0)
            for kb in range(NK):
                if kb + 1 < NK:
                    scores(kb + 1)
                values(kb)


def merge(nc, root, s, wpa_tiles, wpb_tiles):
    with ExitStack() as ctx:
        sb, pb, sem = tools(nc, ctx, root, "mg")
        YT = CONV // P
        names = ("yah", "yal", "ybh", "ybl")
        ys = {n: sb(n, [P, YT, T], F32R) for n in names}
        w = sb("w", [P, 2, 2 * YT, P])
        w_hi = sb("w_hi", [P, 2, 2 * YT, P], F32R)
        w_lo = sb("w_lo", [P, 2, 2 * YT, P], F32R)
        gates = sb("gates", [P, 2, 2, CH])
        part = sb("part", [P, 2, 2, CH])
        mixed = sb("mixed", [P, 2, CH])
        banks = [[pb(f"b{i}{x}") for x in "ab"] for i in range(2)]
        y_in = [sem(f"y_in{n}") for n in range(NCH)]
        w_in = [sem(f"w_in{i}") for i in range(2)]
        g_in = [sem(f"g_in{i}") for i in range(2)]
        m_out = [sem(f"m_out{i}") for i in range(2)]
        w_hi_done, w_lo_done, proj_done, gated, added, sp_passed = (
            sem("w_hi"), sem("w_lo"), sem("proj"), sem("gated"), sem("added"), sem("sp_passed"))
        NI = D // P

        block = ctx.enter_context(nc.Block())

        @block.sync
        def _(sp):
            wait = settled(sp, sp_passed)

            def load_w(i, b):
                for x, tiles in enumerate((wpa_tiles, wpb_tiles)):
                    sp.dma_start(w[:, b, x * YT:(x + 1) * YT], tiles[bass.ds(i, 1)].rearrange("a p k n -> (a p) k n"))\
                      .then_inc(w_in[b], 16)

            def load_gates(i, n, r):
                for x in range(2):
                    sp.dma_start(gates[:, r, x], s["g"][bass.ds(i * P + x * D, P), n * CH:(n + 1) * CH])\
                      .then_inc(g_in[r], 16)

            def store(i, n, r):
                c = 5 * i + n
                wait(added, c + 1)
                sp.dma_start(s["mixed"][bass.ds(i * P, P), n * CH:(n + 1) * CH], mixed[:, r]).then_inc(m_out[r], 16)

            load_w(0, 0)
            for n in range(NCH):
                tok = slice(n * CH, (n + 1) * CH)
                for name in names:
                    sp.dma_start(ys[name][:, :, tok].bitcast(F32), s[name][:, tok].rearrange("(k p) t -> p k t", p=P))\
                      .then_inc(y_in[n], 16)
                if n == 0:
                    load_w(1, 1)
                    load_gates(0, 0, 0)
                    load_gates(0, 1, 1)

            def tile(i, b, more=True, most=True):
                for n in range(NCH):
                    r = (b * NCH + n) % 2
                    wait(gated, 5 * i + n + 1)
                    if n < NCH - 2:
                        load_gates(i, n + 2, r)
                    elif more:
                        load_gates(i + 1, n + 2 - NCH, r)
                    if n == NCH - 1 and most:
                        wait(w_lo_done, i + 1)
                        load_w(i + 2, b)
                    store(i, n, r)

            with sp.Fori(0, NI // 2 - 1) as j:
                tile(2 * j, 0)
                tile(2 * j + 1, 1)
            tile(NI - 2, 0, True, False)
            tile(NI - 1, 1, False, False)
            sp.wait_ge(m_out[0], 16 * NI * NCH // 2)
            sp.wait_ge(m_out[1], 16 * NI * NCH // 2)

        @block.scalar
        def _(act):
            for i in range(2):
                act.wait_ge(w_in[i], 32)
                act.activation(w_hi[:, i], w[:, i], ACT.Copy).then_inc(w_hi_done, 1)
            with act.Fori(0, NI // 2 - 1) as j:
                for b in range(2):
                    i = 2 * j + b
                    act.wait_ge(w_in[b], 32 * j + 64)
                    act.wait_ge(proj_done, 5 * i + 5)
                    act.activation(w_hi[:, b], w[:, b], ACT.Copy).then_inc(w_hi_done, 1)

        @block.gpsimd
        def _(pool):
            def low_w(i, b):
                pool.wait_ge(w_hi_done, i + 1)
                pool.tensor_tensor(w_lo[:, b], w[:, b], w_hi[:, b].bitcast(F32), ALU.subtract).then_inc(w_lo_done, 1)

            def tile(i, b, most=True):
                for n in range(NCH):
                    r = (b * NCH + n) % 2
                    c = 5 * i + n
                    pool.wait_ge(gated, c + 1)
                    before = (b * NCH + n) // 2
                    if not isinstance(i, int) or i or n >= 2:
                        pool.wait_ge(m_out[r], 40 * (i - b) + 16 * before)
                    pool.tensor_tensor(mixed[:, r], part[:, r, 0], part[:, r, 1], ALU.add).then_inc(added, 1)
                if most:
                    low_w(i + 2, b)

            low_w(0, 0)
            low_w(1, 1)
            tile(0, 0)
            tile(1, 1)
            with pool.Fori(1, NI // 2 - 1) as j:
                tile(2 * j, 0)
                tile(2 * j + 1, 1)
            tile(NI - 2, 0, False)
            tile(NI - 1, 1, False)

        @block.vector
        def _(dve):
            def tile(i, b):
                for n in range(NCH):
                    r = (b * NCH + n) % 2
                    c = 5 * i + n
                    dve.wait_ge(proj_done, c + 1)
                    dve.wait_ge(g_in[r], 80 * (i - b) + 32 * ((b * NCH + n) // 2) + 32)
                    if not isinstance(i, int) or i or n >= 2:
                        dve.wait_ge(added, c - 1)
                    for x in range(2):
                        last = dve.tensor_tensor(part[:, r, x], banks[r][x][:, 0:CH], gates[:, r, x], ALU.mult)
                    last.then_inc(gated, 1)

            tile(0, 0)
            tile(1, 1)
            with dve.Fori(1, NI // 2) as j:
                tile(2 * j, 0)
                tile(2 * j + 1, 1)

        @block.tensor
        def _(pe):
            def tile(i, b):
                for n in range(NCH):
                    r = (b * NCH + n) % 2
                    c = 5 * i + n
                    tok = slice(n * CH, (n + 1) * CH)
                    if n == 0:
                        pe.wait_ge(w_lo_done, i + 1)
                    if isinstance(i, int) and i == 0:
                        pe.wait_ge(y_in[n], 64)
                    if not isinstance(i, int) or i or n >= 2:
                        pe.wait_ge(gated, c - 1)
                    for x, (hi, lo) in enumerate((("yah", "yal"), ("ybh", "ybl"))):
                        last = project(pe, banks[r][x][:, 0:CH],
                                       [(w_hi[:, b, x * YT + k, :], w_lo[:, b, x * YT + k, :], ys[hi][:, k, tok],
                                         ys[lo][:, k, tok]) for k in range(YT)])
                    last.then_inc(proj_done, 1)

            tile(0, 0)
            tile(1, 1)
            with pe.Fori(1, NI // 2) as j:
                tile(2 * j, 0)
                tile(2 * j + 1, 1)


def output_norm(nc, root, s, w_out, ln_out, y_prompt, y_sample):
    with ExitStack() as ctx:
        sb, pb, sem = tools(nc, ctx, root, "ln1")
        w = sb("w", [P, KT, D])
        w_hi = sb("w_hi", [P, KT, D], F32R)
        w_lo = sb("w_lo", [P, KT, D], F32R)
        m = [sb(f"m{i}", [P, KT, P]) for i in range(2)]
        m_hi = [sb(f"m_hi{i}", [P, KT, P], F32R) for i in range(2)]
        m_lo = [sb(f"m_lo{i}", [P, KT, P], F32R) for i in range(2)]
        h = sb("h", [P, 2, D])
        y = sb("y", [P, 2, D])
        gain = sb("gain", [P, D])
        shift = sb("shift", [P, D])
        stats = sb("stats", [P, 2, 12])
        mv = sb("mv", [P, 2, 2])
        var = sb("var", [P, 2])
        rstd = sb("rstd", [P, 2])
        nmr = sb("nmr", [P, 2])
        power = sb("power", [P, 1])
        banks = [pb(f"b{i}", (P, D)) for i in range(2)]
        const_in, w_in, aux = sem("const_in"), [sem(f"w_in{k}") for k in range(KT)], sem("aux")
        m_in = [sem(f"m_in{i}") for i in range(2)]
        h_in = [sem(f"h_in{i}") for i in range(2)]
        y_out = [sem(f"y_out{i}") for i in range(2)]
        w_hi_done, w_lo_done, m_hi_done, m_lo_done, proj_done = (
            sem("w_hi"), sem("w_lo"), sem("m_hi"), sem("m_lo"), sem("proj"))
        summed, stats_done, aggr_done, mv_done, rstd_done, coef_done, yn_done, gained, y_done, passed, sp_passed = (
            sem(x) for x in ("summed", "stats", "aggr", "mv", "rstd", "coef", "yn", "gained", "y", "passed",
                             "sp_passed"))
        N = NB + 1

        block = ctx.enter_context(nc.Block())

        @block.sync
        def _(sp):
            wait = settled(sp, sp_passed)

            def load(t, b, rows):
                sp.dma_start(m[b][:, :, 0:rows], s["mixed"][:, bass.ds(t * P, rows)].rearrange("(k p) t -> p k t", p=P))\
                  .then_inc(m_in[b], 16)

            def load_h(t, b, rows):
                sp.dma_start(h[0:rows, b], s["h"][bass.ds(t * P, rows), :]).then_inc(h_in[b], 16)

            def store(t, b, rows):
                wait(y_done, t + 1)
                to = y_sample if rows == DEC else y_prompt[bass.ds(t * P, P), :]
                sp.dma_start(to, y[0:rows, b]).then_inc(y_out[b], 16)

            for k in range(KT):
                sp.dma_start(w[:, k], w_out[k * P:(k + 1) * P, :]).then_inc(w_in[k], 16)
                if k == 0:
                    load(0, 0, P)
                    load(1, 1, P)
            load_h(0, 0, P)
            load_h(1, 1, P)
            sp.dma_start(gain[:, :], ln_out[0:1, :].broadcast_to([P, D])).then_inc(const_in, 16)
            sp.dma_start(shift[:, :], ln_out[1:2, :].broadcast_to([P, D])).then_inc(const_in, 16)

            def turn(t, b, rows, next_rows):
                if next_rows:
                    wait(m_lo_done, t + 1)
                    load(t + 2, b, next_rows)
                    wait(summed, t + 1)
                    load_h(t + 2, b, next_rows)
                store(t, b, rows)

            with sp.Fori(0, 7) as i:
                turn(2 * i, 0, P, P)
                turn(2 * i + 1, 1, P, P)
            turn(14, 0, P, DEC)
            turn(15, 1, P, 0)
            turn(16, 0, DEC, 0)
            sp.wait_ge(y_out[0], 16 * 9)
            sp.wait_ge(y_out[1], 16 * 8)

        @block.tensor
        def _(pe):
            def tile(t, b, first=False):
                pe.wait_ge(m_lo_done, t + 1)
                if not first:
                    pe.wait_ge(summed, t - 1)
                for half in range(2):
                    cols = slice(half * 512, (half + 1) * 512)
                    for k in range(KT):
                        if first and b == 0 and half == 0:
                            pe.wait_ge(w_lo_done, k + 1)
                        to = banks[b][:, cols]
                        pe.matmul(to, m_hi[b][:, k, :], w_hi[:, k, cols], start=(k == 0), stop=False)
                        pe.matmul(to, m_hi[b][:, k, :], w_lo[:, k, cols], start=False, stop=False)
                        last = pe.matmul(to, m_lo[b][:, k, :], w_hi[:, k, cols], start=False, stop=(k == KT - 1))
                last.then_inc(proj_done, 1)

            tile(0, 0, True)
            tile(1, 1, True)
            with pe.Fori(1, 8) as i:
                tile(2 * i, 0)
                tile(2 * i + 1, 1)
            tile(16, 0)

        @block.scalar
        def _(act):
            def high(t, b, rows, first=False):
                act.wait_ge(m_in[b], 8 * t + 16 - 8 * b)
                if not first:
                    act.wait_ge(proj_done, t - 1)
                act.activation(m_hi[b][:, :, 0:rows], m[b][:, :, 0:rows], ACT.Copy).then_inc(m_hi_done, 1)

            def norm(t, b, rows):
                act.wait_ge(coef_done, t + 1)
                act.activation(y[0:rows, b], y[0:rows, b], ACT.Identity, bias=nmr[0:rows, b:b + 1],
                               scale=rstd[0:rows, b:b + 1]).then_inc(yn_done, 1)

            high(0, 0, P, True)
            for k in range(KT):
                act.wait_ge(w_in[k], 16)
                act.activation(w_hi[:, k], w[:, k], ACT.Copy).then_inc(w_hi_done, 1)
            high(1, 1, P, True)
            with act.Fori(0, 7) as i:
                high(2 * i + 2, 0, P)
                norm(2 * i, 0, P)
                high(2 * i + 3, 1, P)
                norm(2 * i + 1, 1, P)
            high(16, 0, DEC)
            norm(14, 0, P)
            norm(15, 1, P)
            norm(16, 0, DEC)

        @block.vector
        def _(dve):
            def low(t, b, rows):
                dve.wait_ge(m_hi_done, t + 1)
                dve.tensor_tensor(m_lo[b][:, :, 0:rows], m[b][:, :, 0:rows], m_hi[b][:, :, 0:rows].bitcast(F32),
                                  ALU.subtract).then_inc(m_lo_done, 1)

            def stat(t, b, rows, first=False):
                r = slice(0, rows)
                dve.wait_ge(proj_done, t + 1)
                dve.wait_ge(h_in[b], 8 * t + 16 - 8 * b)
                if not first:
                    dve.wait_ge(y_out[b], 8 * t - 8 * b)
                dve.scalar_tensor_tensor(out=y[r, b], in0=h[r, b], scalar=ALPHA, in1=banks[b][r, :],
                                         op0=ALU.mult, op1=ALU.add).then_inc(summed, 1)
                dve.wait_ge(summed, t + 1)
                dve.bn_stats(stats[r, b, 0:6], y[r, b, 0:512])
                dve.bn_stats(stats[r, b, 6:12], y[r, b, 512:1024]).then_inc(stats_done, 1)
                dve.wait_ge(stats_done, t + 1)
                dve.sem_inc(passed, 1)
                dve.bn_aggr(mv[r, b, :], stats[r, b, :]).then_inc(aggr_done, 1)
                dve.wait_ge(aggr_done, t + 1)
                dve.tensor_scalar(var[r, b:b + 1], mv[r, b, 1:2], EPS, None, ALU.add).then_inc(mv_done, 1)
                dve.wait_ge(rstd_done, t + 1)
                dve.tensor_scalar(nmr[r, b:b + 1], mv[r, b, 0:1], rstd[r, b:b + 1], -1.0, ALU.mult, ALU.mult)\
                   .then_inc(coef_done, 1)

            def gained_(t, b, rows):
                r = slice(0, rows)
                dve.wait_ge(yn_done, t + 1)
                dve.tensor_tensor(y[r, b], y[r, b], gain[r, :], ALU.mult).then_inc(gained, 1)

            low(0, 0, P)
            for k in range(KT):
                dve.wait_ge(w_hi_done, k + 1)
                dve.tensor_tensor(w_lo[:, k], w[:, k], w_hi[:, k].bitcast(F32), ALU.subtract).then_inc(w_lo_done, 1)
            low(1, 1, P)
            dve.wait_ge(const_in, 32)
            stat(0, 0, P, True)
            low(2, 0, P)
            gained_(0, 0, P)
            stat(1, 1, P, True)
            low(3, 1, P)
            gained_(1, 1, P)
            with dve.Fori(1, 7) as i:
                for b in range(2):
                    stat(2 * i + b, b, P)
                    low(2 * i + b + 2, b, P)
                    gained_(2 * i + b, b, P)
            stat(14, 0, P)
            low(16, 0, DEC)
            gained_(14, 0, P)
            stat(15, 1, P)
            gained_(15, 1, P)
            stat(16, 0, DEC)
            gained_(16, 0, DEC)

        @block.gpsimd
        def _(pool):
            def tile(t, b, rows):
                r = slice(0, rows)
                pool.wait_ge(mv_done, t + 1)
                pool.tensor_tensor(rstd[r, b:b + 1], var[r, b:b + 1], power[r, :], ALU.pow).then_inc(rstd_done, 1)
                pool.wait_ge(gained, t + 1)
                pool.tensor_tensor(y[r, b], y[r, b], shift[r, :], ALU.add).then_inc(y_done, 1)

            pool.memset(power[:, :], -0.5).then_inc(aux, 1)
            pool.wait_ge(aux, 1)
            pool.wait_ge(const_in, 32)
            with pool.Fori(0, 8) as i:
                tile(2 * i, 0, P)
                tile(2 * i + 1, 1, P)
            tile(16, 0, DEC)


def kernel(**inputs):
    import numpy as np
    import concourse.bacc as bacc
    from concourse.bass_utils import run_bass_kernel_spmd

    a = {k: np.asarray(v) for k, v in inputs.items()}
    w = a["w_in"][0]
    xa, b, c, za, q, k, v, f, zb, g = (0, 512, 1024, 1536, 2048, 2560, 3072, 3584, 3592, 4104)
    at = [x + P * j for j in range(4) for x in (xa, c, za, b)]
    at += [x + P * j for j in range(4) for x in (k, v)] + [x + P * j for j in range(4) for x in (q, zb)]
    at += [g + P * i for i in range(2 * D // P)]

    def tiles(m, starts):
        return np.ascontiguousarray(np.stack([m[:, x:x + P].reshape(-1, P, P).transpose(1, 0, 2) for x in starts]))

    every = range(0, D, P)
    feed = dict(
        x_prompt=a["x_prompt"][0], x_sample=a["x_sample"][0],
        cache_k=a["cache_k"][0, 0].reshape(PAST, ATT), cache_v=a["cache_v"][0, 0].reshape(PAST, ATT),
        cache_logf=a["cache_logf"][0, 0], state_conv=a["state_conv"][0, 0].T,
        ln_in=np.stack([a["ln_in_g"], a["ln_in_b"]]), w_tiles=tiles(w, at),
        w_f=w[:, f:f + H].reshape(KT, P, H).transpose(1, 0, 2), b_f=a["b_f"][0].reshape(H, 1),
        conv_w=a["conv_w"][0].reshape(CW, CONV // P, P).transpose(2, 1, 0), wpa_tiles=tiles(a["w_proj_a"][0], every), wpb_tiles=tiles(a["w_proj_b"][0], every),
        w_out=a["w_out"][0], ln_out=np.stack([a["ln_g"][0], a["ln_b"][0]]),
        ident=np.eye(P, dtype=np.float32), causal=np.tril(np.full((P, P), MASKED, np.float32), -1),
        blocks=np.tile(np.repeat(np.eye(H, dtype=np.float32), DEC, axis=1), (2, 1)),
    )
    feed = {n: np.ascontiguousarray(x) for n, x in feed.items()}
    shapes = dict(
        y_prompt=(SEQ, D), y_sample=(DEC, D), k_prompt=(SEQ, ATT), v_prompt=(SEQ, ATT), logf_prompt=(SEQ, H),
        conv_prompt=(CONV, CW - 1), k_sample=(DEC, ATT), v_sample=(DEC, ATT), logf_sample=(DEC, H),
        conv_sample=(CONV, CW - 1))
    nc = bacc.Bacc("TRN2", target_bir_lowering=False, num_devices=1)
    args = {n: nc.dram_tensor(n, x.shape, mybir.dt.from_np(x.dtype), kind="ExternalInput").ap()
            for n, x in feed.items()}
    args |= {n: nc.dram_tensor(n, x, F32, kind="ExternalOutput").ap() for n, x in shapes.items()}
    build(nc, **args)
    r = run_bass_kernel_spmd(nc, [feed], core_ids=[0]).results[0]
    y = {n: np.asarray(r[n]) for n in shapes}
    return (y["y_prompt"].reshape(1, SEQ, D), y["y_sample"].reshape(1, DEC, D),
            y["k_prompt"].reshape(1, 1, SEQ, H, HD), y["v_prompt"].reshape(1, 1, SEQ, H, HD),
            y["logf_prompt"].reshape(1, 1, SEQ, H), y["conv_prompt"].T.reshape(1, 1, CW - 1, CONV),
            y["k_sample"].reshape(1, 1, DEC, H, HD), y["v_sample"].reshape(1, 1, DEC, H, HD),
            y["logf_sample"].reshape(1, 1, DEC, H), y["conv_sample"].T.reshape(1, 1, CW - 1, CONV))
```

```python
from contextlib import ExitStack

import concourse.bass as bass
from concourse import mybir

F32 = mybir.dt.float32
F32R = mybir.dt.float32r
BF16 = mybir.dt.bfloat16
ALU = mybir.AluOpType
ACT = mybir.ActivationFunctionType
AX_X = mybir.AxisListType.X

P = 128
D = 1024
KT = D // P
SEQ = 2048
DEC = 32
PAST = 2048
T = SEQ + DEC
CH = 416
NCH = T // CH
SUB = CH // 4
TAIL = SEQ - (NCH - 1) * CH
H = 8
HD = 64
ATT = H * HD
CONV = 512
CW = 3
NB = SEQ // P
QW = 512
NQ = SEQ // QW
EPS = 1e-5
ALPHA = 2.0 ** 0.25
SCALE = HD ** -0.5
MASKED = -1e30
CKW = SEQ + PAST + DEC

N_TILES = 48


def build(nc, x_prompt, x_sample, cache_k, cache_v, cache_logf, state_conv, ln_in, w_tiles, w_f, b_f,
          conv_w, wpa_tiles, wpb_tiles, w_out, ln_out, ident, causal, blocks,
          y_prompt, y_sample, k_prompt, v_prompt, logf_prompt, conv_prompt,
          k_sample, v_sample, logf_sample, conv_sample):
    with ExitStack() as root:
        def dram(name, shape):
            return nc.dram_tensor(name, shape, F32, kind="Internal").ap()

        s = dict(
            h=dram("h_rows", (T, D)), qh=dram("q_hi", (ATT, T)), ql=dram("q_lo", (ATT, T)),
            kh=dram("k_hi", (ATT, T)), kl=dram("k_lo", (ATT, T)),
            vh=dram("v_hi", (T, ATT)), vl=dram("v_lo", (T, ATT)),
            zb=dram("silu_zb", (ATT, T)), g=dram("merge_gates", (2 * D, T)),
            yah=dram("ya_hi", (CONV, T)), yal=dram("ya_lo", (CONV, T)),
            ybh=dram("yb_hi", (ATT, T)), ybl=dram("yb_lo", (ATT, T)),
            ck=dram("forget_rows", (2, H, CKW)), sums=dram("sums", (H, SEQ)), rcps=dram("rcps", (H, SEQ)), mixed=dram("mixed", (D, T)),
        )
        with ExitStack() as ctx:
            hT_hi = ctx.enter_context(nc.sbuf_tensor("hT_hi", [P, KT, T], F32R))
            hT_lo = ctx.enter_context(nc.sbuf_tensor("hT_lo", [P, KT, T], F32R))
            input_norm(nc, root, s, hT_hi, hT_lo, x_prompt, x_sample, ln_in, ident)
            forget_gates(nc, root, s, hT_hi, hT_lo, w_f, b_f, cache_logf, ident, logf_prompt, logf_sample)
            projections(nc, root, s, hT_hi, hT_lo, w_tiles, conv_w, state_conv, ident,
                        k_prompt, v_prompt, k_sample, v_sample, conv_prompt, conv_sample)
        prompt_attention(nc, root, s, ident, causal)
        sample_attention(nc, root, s, cache_k, cache_v, ident, causal, blocks)
        merge(nc, root, s, wpa_tiles, wpb_tiles)
        output_norm(nc, root, s, w_out, ln_out, y_prompt, y_sample)


def tools(nc, ctx, root, tag):
    def sb(name, shape, dt=F32):
        return ctx.enter_context(nc.sbuf_tensor(f"{tag}_{name}", shape, dt))

    def pb(name, shape=(P, 512), dt=F32):
        return ctx.enter_context(nc.psum_tensor(f"{tag}_{name}", list(shape), dt))

    def sem(name):
        held.append(nc.alloc_semaphore(name=f"{tag}_{name}"))
        return held[-1]

    def clear():
        nc.clear_and_free_semaphores(held)
        nc.all_engine_barrier()

    held = []
    ctx.callback(clear)
    return sb, pb, sem


def settled(sp, passed):
    def wait(q, n):
        sp.wait_ge(q, n)
        if not isinstance(n, int):
            sp.sem_inc(passed, 1)
    return wait


def input_norm(nc, root, s, hT_hi, hT_lo, x_prompt, x_sample, ln_in, ident):
    with ExitStack() as ctx:
        sb, pb, sem = tools(nc, ctx, root, "ln0")
        x = sb("x", [P, 4, D])
        xn = sb("xn", [P, 2, D])
        h = sb("h", [P, 2, D])
        gain = sb("gain", [P, D])
        shift = sb("shift", [P, D])
        eye = sb("eye", [P, P])
        stats = sb("stats", [P, 2, 12])
        mv = sb("mv", [P, 2, 2])
        rstd = sb("rstd", [P, 2])
        nmr = sb("nmr", [P, 2])
        var = sb("var", [P, 2])
        power = sb("power", [P, 1])
        tp = [pb(f"tp{i}", (P, KT, P)) for i in range(4)]

        const_in = sem("const_in")
        x_in = [sem(f"x_in{i}") for i in range(4)]
        aux, aggr_done, passed, sp_passed = sem("aux"), sem("aggr"), sem("passed"), sem("sp_passed")
        stats_done, mv_done, rstd_done, coef_done = sem("stats"), sem("mv"), sem("rstd"), sem("coef")
        xn_done, gained, h_done, turned, hi_done, lo_done = (
            sem("xn"), sem("gained"), sem("h"), sem("turned"), sem("hi"), sem("lo"))
        h_out = [sem(f"h_out{i}") for i in range(2)]
        N = NB + 1

        block = ctx.enter_context(nc.Block())

        @block.sync
        def _(sp):
            wait = settled(sp, sp_passed)

            def load(t, rows=P, slot=None):
                src = x_sample if rows == DEC else x_prompt[bass.ds(t * P, P), :]
                sp.dma_start(x[0:rows, slot, :], src).then_inc(x_in[slot], 16)

            def store(t, b, rows=P):
                wait(h_done, t + 1)
                sp.dma_start(s["h"][bass.ds(t * P, rows), :], h[0:rows, b, :]).then_inc(h_out[b], 16)

            for t in range(4):
                load(t, P, t)
                if t == 0:
                    sp.dma_start(gain[:, :], ln_in[0:1, :].broadcast_to([P, D])).then_inc(const_in, 16)
                    sp.dma_start(shift[:, :], ln_in[1:2, :].broadcast_to([P, D])).then_inc(const_in, 16)
                    sp.dma_start(eye[:, :], ident).then_inc(const_in, 16)
            with sp.Fori(0, 3) as i:
                for c in range(4):
                    wait(xn_done, 4 * i + c + 1)
                    load(4 * i + c + 4, P, c)
                    store(4 * i + c, c % 2)
            sp.wait_ge(xn_done, 13)
            load(16, DEC, 0)
            for t in range(12, 16):
                store(t, t % 2)
            store(16, 0, DEC)
            sp.wait_ge(h_out[0], 16 * 9)
            sp.wait_ge(h_out[1], 16 * 8)

        @block.vector
        def _(dve):
            def stat(t, c, rows=P):
                r, b = slice(0, rows), c % 2
                dve.wait_ge(x_in[c], t * 4 + 16 - 4 * c)
                dve.bn_stats(stats[r, b, 0:6], x[r, c, 0:512])
                dve.bn_stats(stats[r, b, 6:12], x[r, c, 512:1024]).then_inc(stats_done, 1)
                dve.wait_ge(stats_done, t + 1)
                dve.sem_inc(passed, 1)
                dve.bn_aggr(mv[r, b, :], stats[r, b, :]).then_inc(aggr_done, 1)
                dve.wait_ge(aggr_done, t + 1)
                dve.tensor_scalar(var[r, b:b + 1], mv[r, b, 1:2], EPS, None, ALU.add).then_inc(mv_done, 1)

            def coef(t, c, rows=P):
                r, b = slice(0, rows), c % 2
                dve.wait_ge(rstd_done, t + 1)
                dve.tensor_scalar(nmr[r, b:b + 1], mv[r, b, 0:1], rstd[r, b:b + 1], -1.0, ALU.mult, ALU.mult)\
                   .then_inc(coef_done, 1)

            def times_gain(t, c, rows=P):
                r, b = slice(0, rows), c % 2
                dve.wait_ge(xn_done, t + 1)
                dve.tensor_tensor(xn[r, b, :], xn[r, b, :], gain[r, :], ALU.mult).then_inc(gained, 1)

            def low(t, c, rows=P):
                dve.wait_ge(hi_done, t + 1)
                tok = bass.ds(t * P, rows)
                dve.tensor_tensor(hT_lo[:, :, tok], tp[c][:, :, 0:rows], hT_hi[:, :, tok].bitcast(F32),
                                  ALU.subtract).then_inc(lo_done, 1)

            def step(t, c, next_rows=P):
                stat(t + 1, (c + 1) % 4, next_rows)
                times_gain(t, c)
                coef(t + 1, (c + 1) % 4, next_rows)
                if not isinstance(t, int) or t >= 2:
                    low(t - 2, (c + 2) % 4)

            stat(0, 0)
            coef(0, 0)
            dve.wait_ge(const_in, 48)
            step(0, 0)
            step(1, 1)
            with dve.Fori(0, 3) as i:
                for c in range(4):
                    step(4 * i + c + 2, (c + 2) % 4)
            step(14, 2)
            step(15, 3, DEC)
            times_gain(16, 0, DEC)
            low(14, 2)
            low(15, 3)
            low(16, 0, DEC)

        @block.scalar
        def _(act):
            def norm(t, c, rows=P):
                r, b = slice(0, rows), c % 2
                act.wait_ge(coef_done, t + 1)
                if not isinstance(t, int) or t >= 2:
                    act.wait_ge(h_done, t - 1)
                act.activation(xn[r, b, :], x[r, c, :], ACT.Identity, bias=nmr[r, b:b + 1],
                               scale=rstd[r, b:b + 1]).then_inc(xn_done, 1)

            def high(t, c, rows=P):
                act.wait_ge(turned, t + 1)
                act.activation(hT_hi[:, :, bass.ds(t * P, rows)], tp[c][:, :, 0:rows], ACT.Copy)\
                   .then_inc(hi_done, 1)

            norm(0, 0)
            norm(1, 1)
            with act.Fori(0, 3) as i:
                for c in range(4):
                    norm(4 * i + c + 2, (c + 2) % 4)
                    high(4 * i + c, c)
            norm(14, 2)
            high(12, 0)
            norm(15, 3)
            high(13, 1)
            norm(16, 0, DEC)
            for t in (14, 15):
                high(t, t % 4)
            high(16, 0, DEC)

        @block.gpsimd
        def _(pool):
            def add_shift(t, c, rows=P):
                r, b = slice(0, rows), c % 2
                pool.wait_ge(gained, t + 1)
                if not isinstance(t, int) or t >= 2:
                    pool.wait_ge(turned, t - 1)
                    pool.wait_ge(h_out[b], t * 8 - 8 * b)
                pool.tensor_tensor(h[r, b, :], xn[r, b, :], shift[r, :], ALU.add).then_inc(h_done, 1)

            def inverse_std(t, c, rows=P):
                r, b = slice(0, rows), c % 2
                pool.wait_ge(mv_done, t + 1)
                pool.tensor_tensor(rstd[r, b:b + 1], var[r, b:b + 1], power[r, :], ALU.pow).then_inc(rstd_done, 1)

            pool.memset(power[:, :], -0.5).then_inc(aux, 1)
            pool.wait_ge(aux, 1)
            inverse_std(0, 0)
            pool.wait_ge(const_in, 48)
            for t in range(2):
                inverse_std(t + 1, t + 1)
                add_shift(t, t)
            with pool.Fori(0, 3) as i:
                for c in range(4):
                    inverse_std(4 * i + c + 3, (c + 3) % 4)
                    add_shift(4 * i + c + 2, (c + 2) % 4)
            inverse_std(15, 3)
            add_shift(14, 2)
            inverse_std(16, 0, DEC)
            add_shift(15, 3)
            add_shift(16, 0, DEC)

        @block.tensor
        def _(pe):
            def turn(t, c, rows=P):
                pe.wait_ge(h_done, t + 1)
                if not isinstance(t, int) or t >= 4:
                    pe.wait_ge(lo_done, t - 3)
                for k in range(KT):
                    last = pe.transpose(tp[c][:, k, 0:rows], h[0:rows, c % 2, k * P:(k + 1) * P],
                                        eye[0:rows, 0:rows])
                last.then_inc(turned, 1)

            pe.wait_ge(const_in, 48)
            for t in range(4):
                turn(t, t)
            with pe.Fori(1, 4) as i:
                for c in range(4):
                    turn(4 * i + c, c)
            turn(16, 0, DEC)


def forget_gates(nc, root, s, hT_hi, hT_lo, w_f, b_f, cache_logf, ident, logf_prompt, logf_sample):
    with ExitStack() as ctx:
        sb, pb, sem = tools(nc, ctx, root, "fg")
        wf = sb("wf", [P, KT, H])
        wf_hi = sb("wf_hi", [P, KT, P], F32R)
        wf_lo = sb("wf_lo", [P, KT, P], F32R)
        bias = sb("bias", [H, 1])
        eye = sb("eye", [P, P])
        past_rows = sb("past_rows", [P, NB, H])
        z = sb("z", [H, T])
        cum = sb("cum", [H, T])
        logf = sb("logf", [H, T])
        past = sb("past", [H, PAST])
        ones = sb("ones", [H, PAST])
        cum_past = sb("cum_past", [H, PAST])
        hi = sb("hi", [H, T], F32R)
        lo = sb("lo", [H, T], F32R)
        logf_rows = sb("logf_rows", [SUB, T // SUB, H])
        proj = [pb(f"proj{i}") for i in range(NCH)]
        tp = pb("tp")
        tq = [pb(f"tq{i}") for i in range(2)]
        loaded, zeroed, w_hi, w_lo, proj_done = sem("loaded"), sem("zeroed"), sem("w_hi"), sem("w_lo"), sem("proj")
        z_done, soft, logf_done, summed = sem("z"), sem("soft"), sem("logf"), sem("summed")
        past_turned, past_copied, rows_turned, rows_copied = (
            sem("past_turned"), sem("past_copied"), sem("rows_turned"), sem("rows_copied"))
        hi_done, lo_done, out, out_ck = sem("hi"), sem("lo"), sem("out"), sem("out_ck")
        ck = s["ck"]
        parts = [(cum_past, PAST, [(0, PAST, SEQ)]), (cum, T, [(0, SEQ, 0), (SEQ, T, SEQ + PAST)])]
        full = SEQ // SUB
        rest = SEQ - full * SUB

        block = ctx.enter_context(nc.Block())

        @block.sync
        def _(sp):
            sp.dma_start(wf[:, :, :], w_f).then_inc(loaded, 16)
            sp.dma_start(bias[:, :], b_f).then_inc(loaded, 16)
            sp.dma_start(eye[:, :], ident).then_inc(loaded, 16)
            sp.dma_start(past_rows[:, :, :], cache_logf.rearrange("(b p) h -> p b h", p=P)).then_inc(loaded, 16)
            n = 0
            for i, (_, _, cols) in enumerate(parts):
                sp.wait_ge(lo_done, i + 1)
                for a, b, at in cols:
                    sp.dma_start(ck[0, :, at:at + b - a], hi[:, a:b].bitcast(F32)).then_inc(out_ck, 16)
                    sp.dma_start(ck[1, :, at:at + b - a], lo[:, a:b].bitcast(F32)).then_inc(out_ck, 16)
                    n += 32
                sp.wait_ge(out_ck, n)
            sp.wait_ge(rows_copied, 1)
            sp.dma_start(logf_prompt[0:full * SUB, :].rearrange("(a p) h -> p a h", p=SUB),
                         logf_rows[:, 0:full, :]).then_inc(out, 16)
            sp.dma_start(logf_prompt[full * SUB:SEQ, :], logf_rows[0:rest, full, :]).then_inc(out, 16)
            sp.dma_start(logf_sample, logf_rows[rest:SUB, full, :]).then_inc(out, 16)
            sp.wait_ge(out, 48)

        @block.gpsimd
        def _(pool):
            pool.memset(wf_hi[:, :, :].bitcast(F32), 0.0).then_inc(zeroed, 1)
            pool.memset(wf_lo[:, :, :].bitcast(F32), 0.0).then_inc(zeroed, 1)
            pool.memset(ones[:, :], 1.0).then_inc(zeroed, 1)

        @block.vector
        def _(dve):
            dve.wait_ge(loaded, 64)
            dve.wait_ge(zeroed, 3)
            dve.tensor_copy(wf_hi[:, :, 0:H], wf[:, :, :]).then_inc(w_hi, 1)
            dve.wait_ge(w_hi, 1)
            dve.tensor_tensor(wf_lo[:, :, 0:H], wf[:, :, :], wf_hi[:, :, 0:H].bitcast(F32), ALU.subtract)\
               .then_inc(w_lo, 1)
            for q in range(4):
                dve.wait_ge(past_turned, q + 1)
                dve.tensor_copy(past[:, q * 512:(q + 1) * 512], tq[q % 2][0:H, :]).then_inc(past_copied, 1)
            dve.wait_ge(past_copied, 4)
            dve.tensor_tensor_scan(cum_past[:, :], ones[:, :], past[:, :], 0.0, ALU.mult, ALU.add)\
               .then_inc(summed, 1)
            dve.wait_ge(hi_done, 1)
            dve.scalar_tensor_tensor(out=lo[:, 0:PAST], in0=cum_past[:, :], scalar=-8.0,
                                     in1=hi[:, 0:PAST].bitcast(F32), op0=ALU.mult, op1=ALU.subtract)\
               .then_inc(lo_done, 1)
            dve.wait_ge(soft, 3)
            dve.scalar_tensor_tensor(out=logf[:, :], in0=z[:, :], scalar=0.0, in1=cum[:, :],
                                     op0=ALU.min, op1=ALU.subtract).then_inc(logf_done, 1)
            dve.wait_ge(logf_done, 1)
            dve.tensor_tensor_scan(cum[:, 0:SEQ], ones[:, :], logf[:, 0:SEQ], 0.0, ALU.mult, ALU.add)\
               .then_inc(summed, 1)
            dve.tensor_tensor_scan(cum[:, SEQ:T], ones[:, 0:DEC], logf[:, SEQ:T], cum_past[:, PAST - 1:PAST],
                                   ALU.mult, ALU.add).then_inc(summed, 1)
            dve.wait_ge(hi_done, 2)
            dve.scalar_tensor_tensor(out=lo[:, :], in0=cum[:, :], scalar=-8.0, in1=hi[:, :].bitcast(F32),
                                     op0=ALU.mult, op1=ALU.subtract).then_inc(lo_done, 1)
            dve.wait_ge(rows_turned, 1)
            dve.tensor_copy(logf_rows[:, :, :], tp[0:SUB, 0:T // SUB * H].rearrange("p (a h) -> p a h", h=H))\
               .then_inc(rows_copied, 1)

        @block.scalar
        def _(act):
            act.wait_ge(summed, 1)
            act.activation(hi[:, 0:PAST], cum_past[:, :], ACT.Copy, scale=-8.0).then_inc(hi_done, 1)
            for n in range(NCH):
                act.wait_ge(proj_done, n + 1)
                act.activation(z[:, n * CH:(n + 1) * CH], proj[n][0:H, 0:CH], ACT.Identity,
                               bias=bias[:, :]).then_inc(z_done, 1)
            act.wait_ge(z_done, NCH)
            act.activation(cum[:, :], z[:, :], ACT.Abs).then_inc(soft, 1)
            act.wait_ge(soft, 1)
            act.activation(cum[:, :], cum[:, :], ACT.Exp, scale=-1.0).then_inc(soft, 1)
            act.wait_ge(soft, 2)
            act.activation(cum[:, :], cum[:, :], ACT.Ln, bias=1.0).then_inc(soft, 1)
            act.wait_ge(summed, 3)
            act.wait_ge(out_ck, 32)
            act.activation(hi[:, :], cum[:, :], ACT.Copy, scale=-8.0).then_inc(hi_done, 1)

        @block.tensor
        def _(pe):
            pe.wait_ge(loaded, 64)
            for q in range(4):
                if q >= 2:
                    pe.wait_ge(past_copied, q - 1)
                for b in range(4):
                    last = pe.transpose(tq[q % 2][0:H, b * P:(b + 1) * P], past_rows[:, 4 * q + b, :], eye[:, :])
                last.then_inc(past_turned, 1)
            pe.wait_ge(w_lo, 1)
            for n in range(NCH):
                tok = slice(n * CH, (n + 1) * CH)
                project(pe, proj[n][:, 0:CH], [(wf_hi[:, k, :], wf_lo[:, k, :], hT_hi[:, k, tok], hT_lo[:, k, tok])
                                               for k in range(KT)]).then_inc(proj_done, 1)
            pe.wait_ge(logf_done, 1)
            for a in range(T // SUB):
                last = pe.transpose(tp[0:SUB, a * H:(a + 1) * H], logf[:, a * SUB:(a + 1) * SUB], eye[0:H, 0:H])
            last.then_inc(rows_turned, 1)


def project(pe, out, parts):
    for i, (w_hi, w_lo, x_hi, x_lo) in enumerate(parts):
        pe.matmul(out, w_hi, x_hi, start=(i == 0), stop=False)
        pe.matmul(out, w_hi, x_lo, start=False, stop=False)
        last = pe.matmul(out, w_lo, x_hi, start=False, stop=(i == len(parts) - 1))
    return last


def projections(nc, root, s, hT_hi, hT_lo, w_tiles, conv_w, state_conv, ident,
                k_prompt, v_prompt, k_sample, v_sample, conv_prompt, conv_sample):
    with ExitStack() as ctx:
        sb, pb, sem = tools(nc, ctx, root, "pr")
        w = sb("w", [P, 2, KT, P])
        w_hi = sb("w_hi", [P, 2, KT, P], F32R)
        w_lo = sb("w_lo", [P, 2, KT, P], F32R)
        eye = sb("eye", [P, P])
        cw = sb("cw", [P, CONV // P, CW])
        GAP = SEQ + CW - 1
        U = sb("u", [P, T + 2 * (CW - 1)])
        xa = sb("xa", [P, T])
        conv = sb("conv", [P, T + CW - 1])
        full_t = sb("full_t", [P, 2, CH])
        out_a = sb("out_a", [P, 2, 512], F32R)
        out_b = sb("out_b", [P, 2, 512], F32R)
        out_c = sb("out_c", [SUB, 2, 4, P])
        bank = [pb(f"bank{i}") for i in range(NCH)]
        turn_bank = pb("turn")

        const_in = sem("const_in")
        w_in = [sem(f"w_in{i}") for i in range(2)]
        w_hi_done, w_lo_done, proj_done = sem("w_hi"), sem("w_lo"), sem("proj_done")
        bank_free = [sem(f"bank_free{i}") for i in range(NCH)]
        a_done, b_done, c_done = sem("a_done"), sem("b_done"), sem("c_done")
        a_out, b_out, c_out = ([sem(f"{x}_out{i}") for i in range(2)] for x in "abc")
        edges, state_in, conv_done, frames_out, tail_out = (
            sem("edges"), sem("state_in"), sem("conv"), sem("frames_out"), sem("tail_out"))
        full_done, gated, turned, sp_passed = sem("full"), sem("gated"), sem("turned"), sem("sp_passed")

        def toks(n):
            return slice(n * CH, (n + 1) * CH)

        def left(a, n):
            return 48 * a + 16 * (n // 2) + 16 if n % 2 == 0 else 32 * a + 16 * (n // 2) + 16

        def spans(n, shift):
            if n < NCH - 1:
                return [(slice(n * CH + shift, (n + 1) * CH + shift), slice(0, CH))]
            return [(slice(n * CH + shift, SEQ + shift), slice(0, TAIL)),
                    (slice(GAP + shift, GAP + DEC + shift), slice(TAIL, CH))]

        block = ctx.enter_context(nc.Block())

        @block.sync
        def _(sp):
            wait = settled(sp, sp_passed)
            sp.dma_start(w[:, 0], w_tiles[0]).then_inc(w_in[0], 16)
            sp.dma_start(w[:, 1], w_tiles[1]).then_inc(w_in[1], 16)
            sp.dma_start(eye[:, :], ident).then_inc(const_in, 16)
            sp.dma_start(cw[:, :, :], conv_w).then_inc(const_in, 16)
            for q in (*a_out, *b_out, *c_out, tail_out):
                sp.sem_inc(q, 16)
            sp.sem_inc(frames_out, 16)

            def next_w(t, b):
                wait(w_lo_done, t + 1)
                sp.dma_start(w[:, b], w_tiles[bass.ds(t + 2, 1)].rearrange("a p k n -> (a p) k n"))\
                  .then_inc(w_in[b], 16)

            def rows_out(dst, n, a=None, t=None):
                if a is None:
                    wait(bank_free[n], t + 2)
                else:
                    wait(a_done, 5 * a + n + 1)
                sp.dma_start(dst, out_a[:, n % 2, 0:CH].bitcast(F32)).then_inc(a_out[n % 2], 16)

            def lows_out(dst, t, n, done=None):
                if done is None:
                    wait(bank_free[n], t + 2)
                else:
                    wait(b_done, done)
                sp.dma_start(dst, out_b[:, n % 2, 0:CH].bitcast(F32)).then_inc(b_out[n % 2], 16)

            def tokens_out(dst, dst_sample, cols, c, n):
                wait(c_done, 5 * c + n + 1)
                src = out_c[:, n % 2]
                at = n * CH
                if n < NCH - 1:
                    sp.dma_start(dst[at:at + CH, cols].rearrange("(a p) c -> p a c", p=SUB), src)\
                      .then_inc(c_out[n % 2], 16)
                    return
                m = TAIL // SUB
                r = TAIL - m * SUB
                sp.dma_start(dst[at:at + m * SUB, cols].rearrange("(a p) c -> p a c", p=SUB), src[:, 0:m, :])\
                  .then_inc(tail_out, 16)
                sp.dma_start(dst[at + m * SUB:SEQ, cols], src[0:r, m, :]).then_inc(tail_out, 16)
                sp.dma_start(dst_sample[:, cols], src[r:SUB, m, :]).then_inc(c_out[n % 2], 16)

            with sp.Fori(0, 4) as j:
                ch = bass.ds(j * P, P)
                wait(conv_done, 3 * j + 1)
                sp.dma_start(U[:, GAP:GAP + CW - 1], state_conv[ch, :]).then_inc(state_in, 16)
                next_w(4 * j, 0)
                next_w(4 * j + 1, 1)
                wait(bank_free[NCH - 1], 4 * j + 3)
                sp.dma_start(conv_prompt[ch, :], U[:, SEQ:SEQ + CW - 1]).then_inc(frames_out, 16)
                sp.dma_start(conv_sample[ch, :], U[:, GAP + DEC:GAP + DEC + CW - 1]).then_inc(frames_out, 16)
                next_w(4 * j + 2, 0)
                next_w(4 * j + 3, 1)
                for n in range(NCH):
                    rows_out(s["yah"][ch, toks(n)], n, a=j)
                    lows_out(s["yal"][ch, toks(n)], 0, n, 5 * j + n + 1)
            with sp.Fori(0, 4) as j:
                ch = bass.ds(j * P, P)
                next_w(16 + 2 * j, 0)
                for n in range(NCH):
                    rows_out(s["kh"][ch, toks(n)], n, a=4 + 2 * j)
                    lows_out(s["kl"][ch, toks(n)], 16 + 2 * j, n)
                    if n:
                        tokens_out(k_prompt, k_sample, ch, 2 * j, n - 1)
                tokens_out(k_prompt, k_sample, ch, 2 * j, NCH - 1)
                next_w(17 + 2 * j, 1)
                for n in range(NCH):
                    tokens_out(v_prompt, v_sample, ch, 2 * j + 1, n)
                    for name, src, done, value, gone in (
                            ("vh", out_a, a_done, 5 * (5 + 2 * j) + n + 1, a_out[n % 2]),
                            ("vl", out_b, b_done, 5 * (4 + j) + n + 1, b_out[n % 2])):
                        wait(done, value)
                        sp.dma_start(s[name][n * CH:(n + 1) * CH, ch].rearrange("(a p) c -> p a c", p=SUB),
                                     src[0:SUB, n % 2, :].bitcast(F32).rearrange("p (a c) -> p a c", a=4))\
                          .then_inc(gone, 16)
            with sp.Fori(0, 4) as j:
                ch = bass.ds(j * P, P)
                next_w(24 + 2 * j, 0)
                for n in range(NCH):
                    rows_out(s["qh"][ch, toks(n)], n, a=12 + j)
                    lows_out(s["ql"][ch, toks(n)], 24 + 2 * j, n)
                next_w(25 + 2 * j, 1)
                for n in range(NCH):
                    rows_out(s["zb"][ch, toks(n)], n, t=25 + 2 * j)
            with sp.Fori(0, 7) as j:
                for b in range(2):
                    next_w(32 + 2 * j + b, b)
                    for n in range(NCH):
                        rows_out(s["g"][bass.ds((2 * j + b) * P, P), toks(n)], n, t=32 + 2 * j + b)
            for b in range(2):
                for n in range(NCH):
                    rows_out(s["g"][(14 + b) * P:(15 + b) * P, toks(n)], n, t=46 + b)
            for q, tiles in ((a_out, 36), (b_out, 16), (c_out, 8)):
                wait(q[0], left(tiles, 0))
                wait(q[1], left(tiles, 1))
            wait(frames_out, 16 + 32 * 4)
            wait(tail_out, 16 + 32 * 8)

        @block.tensor
        def _(pe):
            def chunk(t, b, n):
                if n == 0:
                    pe.wait_ge(w_lo_done, t + 1)
                pe.wait_ge(bank_free[n], t + 1)
                project(pe, bank[n][:, 0:CH], [(w_hi[:, b, k, :], w_lo[:, b, k, :], hT_hi[:, k, toks(n)],
                                                hT_lo[:, k, toks(n)]) for k in range(KT)]).then_inc(proj_done, 1)

            def turn(j, b, n):
                if b == 0:
                    pe.wait_ge(full_done, 5 * j + n + 1)
                else:
                    pe.wait_ge(bank_free[n], 17 + 2 * j + 2)
                if (b == 0) == (n > 0):
                    pe.wait_ge(c_done, 10 * j + n if b == 0 else 10 * j + 5)
                else:
                    pe.wait_ge(b_done, 20 + 5 * j + n)
                for a in range(4):
                    last = pe.transpose(turn_bank[0:SUB, a * P:(a + 1) * P], full_t[:, n % 2, a * SUB:(a + 1) * SUB],
                                        eye[:, :])
                last.then_inc(turned, 1)

            pe.wait_ge(const_in, 32)
            with pe.Fori(0, 8) as i:
                for b in range(2):
                    for n in range(NCH):
                        chunk(2 * i + b, b, n)
            with pe.Fori(0, 4) as j:
                for b in range(2):
                    for n in range(NCH):
                        chunk(16 + 2 * j + b, b, n)
                        if n:
                            turn(j, b, n - 1)
                    turn(j, b, NCH - 1)
            with pe.Fori(0, 12) as i:
                for b in range(2):
                    for n in range(NCH):
                        chunk(24 + 2 * i + b, b, n)

        @block.gpsimd
        def _(pool):
            def low_w(t, b):
                pool.wait_ge(w_hi_done, t + 1)
                pool.tensor_tensor(w_lo[:, b], w[:, b], w_hi[:, b].bitcast(F32), ALU.subtract).then_inc(w_lo_done, 1)

            with pool.Fori(0, N_TILES // 2) as i:
                low_w(2 * i, 0)
                low_w(2 * i + 1, 1)

        @block.scalar
        def _(act):
            def high_w(t, b):
                act.wait_ge(w_in[b], 8 * t + 16 - 8 * b)
                act.wait_ge(proj_done, 5 * t - 5)
                act.activation(w_hi[:, b], w[:, b], ACT.Copy).then_inc(w_hi_done, 1)

            def through(t, n, a, func):
                act.wait_ge(proj_done, 5 * t + n + 1)
                act.wait_ge(a_out[n % 2], left(a, n))
                to = out_a[:, n % 2, 0:CH]
                if func != ACT.Copy:
                    to = to.bitcast(F32)
                return act.activation(to, bank[n][:, 0:CH], func)

            def keep_full(t, c, n, done):
                act.wait_ge(proj_done, 5 * t + n + 1)
                act.wait_ge(turned, 5 * c + n + 1 if n == 0 else 5 * c + n)
                return act.activation(full_t[:, n % 2, :], bank[n][:, 0:CH], ACT.Copy).then_inc(done, 1)

            def rows_c(c, n):
                act.wait_ge(turned, 5 * c + n + 2)
                act.wait_ge(c_out[n % 2], left(c, n))
                if n == 0:
                    act.wait_ge(tail_out, 32 * c + 16)
                return act.activation(out_c[:, n % 2], turn_bank[0:SUB, :].rearrange("p (a c) -> p a c", a=4), ACT.Copy)

            for q in bank_free:
                act.sem_inc(q, 1)
            act.sem_inc(turned, 1)
            act.sem_inc(gated, 5)
            act.sem_inc(conv_done, 1)
            act.wait_ge(w_in[0], 16)
            act.activation(w_hi[:, 0], w[:, 0], ACT.Copy).then_inc(w_hi_done, 1)
            act.wait_ge(w_in[1], 16)
            act.activation(w_hi[:, 1], w[:, 1], ACT.Copy).then_inc(w_hi_done, 1)
            with act.Fori(0, 4) as j:
                for n in range(NCH):
                    act.wait_ge(proj_done, 20 * j + n + 1)
                    act.wait_ge(gated, 5 * j + n + 1)
                    act.activation(xa[:, toks(n)], bank[n][:, 0:CH], ACT.Copy).then_inc(bank_free[n], 1)
                high_w(4 * j + 2, 0)
                high_w(4 * j + 3, 1)
                for n in range(NCH):
                    act.wait_ge(proj_done, 20 * j + 10 + n + 1)
                    act.activation(xa[:, toks(n)], bank[n][:, 0:CH], ACT.Silu).then_inc(bank_free[n], 1)
                high_w(4 * j + 4, 0)
                for n in range(NCH):
                    if n < 2:
                        act.wait_ge(bank_free[0], 4 * j + 3)
                    else:
                        act.wait_ge(b_done, 5 * j + n - 1)
                    act.wait_ge(gated, 5 * j + n + 6)
                    act.wait_ge(a_out[n % 2], left(j, n))
                    act.activation(out_a[:, n % 2, 0:CH], full_t[:, n % 2, :], ACT.Copy).then_inc(a_done, 1)
                high_w(4 * j + 5, 1)
            act.wait_ge(b_done, 20)
            with act.Fori(0, 4) as j:
                for n in range(NCH):
                    keep_full(16 + 2 * j, 2 * j, n, full_done)
                    if n < 2:
                        act.wait_ge(b_done, 5 * (4 + j))
                    else:
                        act.wait_ge(bank_free[n - 2], 18 + 2 * j)
                    through(16 + 2 * j, n, 4 + 2 * j, ACT.Copy).then_inc(a_done, 1)
                    if n:
                        rows_c(2 * j, n - 1).then_inc(c_done, 1)
                rows_c(2 * j, NCH - 1).then_inc(c_done, 1)
                high_w(18 + 2 * j, 0)
                for n in range(NCH + 1):
                    if n < NCH:
                        keep_full(17 + 2 * j, 2 * j + 1, n, bank_free[n])
                    if n:
                        rows_c(2 * j + 1, n - 1).then_inc(c_done, 1)
                        act.wait_ge(a_out[(n - 1) % 2], left(5 + 2 * j, n - 1))
                        if n < 3:
                            act.wait_ge(bank_free[5 - n], 18 + 2 * j)
                        else:
                            act.wait_ge(b_done, 5 * (4 + j) + n - 2)
                        act.activation(out_a[0:SUB, (n - 1) % 2, :], turn_bank[0:SUB, :], ACT.Copy)\
                           .then_inc(a_done, 1)
                high_w(19 + 2 * j, 1)
            with act.Fori(0, 4) as j:
                for n in range(NCH):
                    if n >= 2:
                        act.wait_ge(bank_free[n - 2], 26 + 2 * j)
                    else:
                        act.wait_ge(b_done, 40)
                        act.wait_ge(bank_free[4 - n], 24 + 2 * j)
                    through(24 + 2 * j, n, 12 + 2 * j, ACT.Copy).then_inc(a_done, 1)
                high_w(26 + 2 * j, 0)
                for n in range(NCH):
                    if n < 2:
                        act.wait_ge(bank_free[4 - n], 26 + 2 * j)
                    through(25 + 2 * j, n, 13 + 2 * j, ACT.Silu).then_inc(bank_free[n], 1)
                high_w(27 + 2 * j, 1)
            with act.Fori(0, 7) as j:
                for b in range(2):
                    for n in range(NCH):
                        through(32 + 2 * j + b, n, 20 + 2 * j + b, ACT.Sigmoid).then_inc(bank_free[n], 1)
                    high_w(34 + 2 * j + b, b)
            for b in range(2):
                for n in range(NCH):
                    through(46 + b, n, 34 + b, ACT.Sigmoid).then_inc(bank_free[n], 1)

        @block.vector
        def _(dve):
            dve.memset(U[:, 0:CW - 1], 0.0).then_inc(edges, 1)
            dve.wait_ge(edges, 1)
            dve.wait_ge(const_in, 32)

            def low(n, a, b, src, rows, width):
                dve.wait_ge(a_done, 5 * a + n + 1)
                dve.wait_ge(b_out[n % 2], left(b, n))
                return dve.tensor_tensor(out_b[0:rows, n % 2, 0:width], src,
                                         out_a[0:rows, n % 2, 0:width].bitcast(F32), ALU.subtract)

            with dve.Fori(0, 4) as j:
                t = 4 * j + 1
                dve.wait_ge(frames_out, 32 * j + 16)
                dve.wait_ge(conv_done, 3 * j + 1)
                for n in range(NCH):
                    dve.wait_ge(proj_done, 5 * t + n + 1)
                    for to, col in spans(n, CW - 1):
                        last = dve.tensor_tensor(U[:, to], bank[n][:, col], xa[:, toks(n)][:, col], ALU.mult)
                    last.then_inc(bank_free[n], 1)
                for n in range(NCH):
                    dve.wait_ge(bank_free[n], t + 2)
                dve.wait_ge(state_in, 16 * j + 16)
                dve.wait_ge(gated, 5 * j + 5)
                L = T + CW - 1
                tap = cw[:, bass.ds(j, 1), :].rearrange("p j w -> p (j w)")
                dve.tensor_scalar(conv[:, :], U[:, 0:L], tap[:, 0:1], None, ALU.mult).then_inc(conv_done, 1)
                for x in range(1, CW):
                    dve.wait_ge(conv_done, 3 * j + x + 1)
                    dve.scalar_tensor_tensor(out=conv[:, :], in0=U[:, x:x + L], scalar=tap[:, x:x + 1],
                                             in1=conv[:, :], op0=ALU.mult, op1=ALU.add).then_inc(conv_done, 1)
                dve.wait_ge(conv_done, 3 * j + CW + 1)
                for n in range(NCH + 1):
                    if n < NCH:
                        dve.wait_ge(proj_done, 5 * (t + 2) + n + 1)
                        if n >= 2:
                            dve.wait_ge(b_done, 5 * j + n - 1)
                        for to, col in spans(n, 0):
                            last = dve.tensor_tensor(full_t[:, n % 2, col], bank[n][:, col], conv[:, to], ALU.mult)
                        last.then_inc(bank_free[n], 1)
                        dve.wait_ge(bank_free[n], t + 4)
                        dve.tensor_tensor(full_t[:, n % 2, :], full_t[:, n % 2, :], xa[:, toks(n)], ALU.mult)\
                           .then_inc(gated, 1)
                    if n:
                        low(n - 1, j, j, full_t[:, (n - 1) % 2, :], P, CH).then_inc(b_done, 1)
            with dve.Fori(0, 4) as j:
                for n in range(NCH):
                    low(n, 4 + 2 * j, 4 + 2 * j, bank[n][:, 0:CH], P, CH).then_inc(bank_free[n], 1)
                for n in range(NCH):
                    low(n, 5 + 2 * j, 5 + 2 * j, turn_bank[0:SUB, :], SUB, 4 * P).then_inc(b_done, 1)
            with dve.Fori(0, 4) as j:
                for n in range(NCH):
                    low(n, 12 + j, 12 + j, bank[n][:, 0:CH], P, CH).then_inc(bank_free[n], 1)


def prompt_attention(nc, root, s, ident, causal):
    with ExitStack() as ctx:
        sb, pb, sem = tools(nc, ctx, root, "at")
        HR = HD + 4
        ks = sb("ks", [P, 2, SEQ], F32R)
        qs = sb("qs", [P, 2, SEQ], F32R)
        k2 = sb("k2", [HR, 2, SEQ], F32R)
        q2 = sb("q2", [HR, 2, SEQ], F32R)
        km = sb("km", [HR, 2, SEQ], F32R)
        qm = sb("qm", [HR, 2, SEQ], F32R)
        v_hi = sb("v_hi", [P, 2, NB, P], F32R)
        v_lo = sb("v_lo", [P, 2, NB, P], F32R)
        zb = sb("zb", [HD, 2, SEQ])
        RING = 4
        p = sb("p", [P, RING, QW])
        p_hi = sb("p_hi", [P, RING, QW], F32R)
        p_lo = sb("p_lo", [P, RING, QW], F32R)
        eye = sb("eye", [P, P])
        mask = sb("mask", [P, P])
        eye_b = sb("eye_b", [P, P], BF16)
        mask_b = sb("mask_b", [P, P], BF16)
        piece_max = sb("piece_max", [P, NB, NQ])
        row_max = sb("row_max", [P, NB])
        neg_max = sb("neg_max", [P, 2 * NB], F32R)
        neg_rows = sb("neg_rows", [2 * NB, P])
        y = sb("y", [HD + 1, 2, SEQ])
        sums = sb("sums", [P, NB])
        rcp = sb("rcp", [P, NB])
        rcp_all = sb("rcp_all", [HD, SEQ])
        y_hi = sb("y_hi", [HD, 2, QW], F32R)
        y_lo = sb("y_lo", [HD, 2, QW], F32R)
        s_bank = [pb(f"s{i}") for i in range(RING)]
        o_bank = [pb(f"o{i}") for i in range(2)]
        m_bank = [pb(f"m{i}") for i in range(2)]

        const_in, ones_set, consts = sem("const_in"), sem("ones_set"), sem("consts")
        main_in = [sem(f"main_in{i}") for i in range(2)]
        max_in = [sem(f"max_in{i}") for i in range(2)]
        m_in = [sem(f"m_in{i}") for i in range(2)]
        s_done = sem("s_done")
        p_done = sem("p_done")
        lo_dve, lo_pool = sem("lo_dve"), sem("lo_pool")
        pv_done = sem("pv_done")
        unit_done = sem("unit_done")
        unit_read = sem("unit_read")
        maxed, split, turned, rows_done = sem("maxed"), sem("split"), sem("turned"), sem("rows_done")
        o_read = sem("o_read")
        sum_out, sums_in, rcp_done, rcp_out, rcp_in = (
            sem("sum_out"), sem("sums_in"), sem("rcp_done"), sem("rcp_out"), sem("rcp_in"))
        zb_in = [sem(f"zb_in{i}") for i in range(2)]
        y_scaled = sem("y_scaled")
        y_gated, yh_done, yl_done = sem("y_gated"), sem("yh_done"), sem("yl_done")
        y_out = [sem(f"y_out{i}") for i in range(2)]
        sp_passed = sem("sp_passed")

        steps = [(q, kb) for q in range(NQ) for kb in range(4 * q + 4)]
        NS = len(steps)
        ends = [steps.index((q, 4 * q + 3)) for q in range(NQ)]
        units = [(i, c) for i in range(NB) for c in range(i // 4 + 1)]
        NU = len(units)
        LEAD = 3
        POOLS = 4

        def step_units(st):
            return range(min(NU, st * 4 // 3), min(NU, (st + 1) * 4 // 3))

        INVERT = 9
        FINISH = {20 + 4 * q + x + x // 2: (q, x) for x in range(3) for q in range(NQ)}
        FINISH_LOW = {st + 5: q for st, (q, x) in FINISH.items() if x == 0}
        TURN = 31

        def low_value(h, st):
            if st % POOLS == POOLS - 1:
                return lo_pool, NS // POOLS * h + st // POOLS + 1
            return lo_dve, (NS - NS // POOLS) * h + st - st // POOLS + 1

        def used(h, b, per):
            return per * (h // 2 + 1) if isinstance(h, int) else (h - b) * (per // 2) + per

        def finishing(eng):
            def scale(h, b, q):
                if q == 0:
                    eng.wait_ge(rcp_in, 16 * h + 16)
                    eng.wait_ge(zb_in[b], used(h, b, 16))
                at = y[0:HD, b, q * QW:(q + 1) * QW]
                eng.tensor_tensor(at, at, rcp_all[:, q * QW:(q + 1) * QW], ALU.mult).then_inc(y_scaled, 1)

            def gate(h, b, q):
                eng.wait_ge(y_scaled, NQ * h + q + 1)
                at = y[0:HD, b, q * QW:(q + 1) * QW]
                eng.tensor_tensor(at, at, zb[:, b, q * QW:(q + 1) * QW], ALU.mult).then_inc(y_gated, 1)

            def lower(h, b, q):
                eng.wait_ge(yh_done, NQ * h + q + 1)
                eng.tensor_tensor(y_lo[:, q % 2, :], y[0:HD, b, q * QW:(q + 1) * QW], y_hi[:, q % 2, :].bitcast(F32),
                                  ALU.subtract).then_inc(yl_done, 1)
            return scale, gate, lower

        block = ctx.enter_context(nc.Block())

        @block.sync
        def _(sp):
            wait = settled(sp, sp_passed)
            sp.dma_start(eye[:, :], ident).then_inc(const_in, 16)
            sp.dma_start(mask[:, :], causal).then_inc(const_in, 16)
            for q in y_out:
                sp.sem_inc(q, 16)
            sp.wait_ge(ones_set, 6)

            def load_max(h, b):
                rows = bass.ds(h * HD, HD)
                for to, of in ((km[0:HD, b], s["kh"][rows, 0:SEQ]), (qm[0:HD, b], s["qh"][rows, 0:SEQ]),
                               (km[HD:HD + 2, b], s["ck"][:, bass.ds(h, 1), 0:SEQ].rearrange("a h t -> a (h t)"))):
                    sp.dma_start(to.bitcast(F32), of).then_inc(max_in[b], 16)

            def load_main(h, b):
                rows = bass.ds(h * HD, HD)
                ck = s["ck"][:, bass.ds(h, 1), 0:SEQ].rearrange("a h t -> a (h t)")
                for to, of in ((ks[0:HD, b], s["kh"][rows, 0:SEQ]), (ks[HD:P, b], s["kl"][rows, 0:SEQ]),
                               (qs[0:HD, b], s["qh"][rows, 0:SEQ]), (qs[HD:P, b], s["qh"][rows, 0:SEQ]),
                               (k2[0:HD, b], s["kh"][rows, 0:SEQ]), (k2[HD:HD + 2, b], ck),
                               (q2[0:HD, b], s["ql"][rows, 0:SEQ])):
                    sp.dma_start(to.bitcast(F32), of).then_inc(main_in[b], 16)
                for to, of in ((v_hi, s["vh"]), (v_lo, s["vl"])):
                    sp.dma_start(to[:, b, :, 0:HD].bitcast(F32), of[0:SEQ, rows].rearrange("(b p) c -> p b c", p=P))\
                      .then_inc(main_in[b], 16)

            def max_rows(h, b):
                wait(rows_done, h + 1)
                for i in range(2):
                    sp.dma_start(q2[HD + 2 + i:HD + 3 + i, b, :].bitcast(F32).rearrange("a (t q) -> a t q", q=P),
                                 neg_rows[i * NB:(i + 1) * NB, :]).then_inc(m_in[b], 16)

            def y_store(h, b, q):
                wait(yl_done, NQ * h + q + 1)
                for to, of in ((s["ybh"], y_hi), (s["ybl"], y_lo)):
                    sp.dma_start(to[bass.ds(h * HD, HD), q * QW:(q + 1) * QW], of[:, q % 2, :].bitcast(F32))\
                      .then_inc(y_out[q % 2], 16)

            def sum_store(h, b, q):
                wait(o_read, NQ * h + q + 3)
                sp.dma_start(s["sums"][bass.ds(h, 1), q * QW:(q + 1) * QW], y[HD:HD + 1, b, q * QW:(q + 1) * QW])\
                  .then_inc(sum_out, 16)

            def rcp_rows(h):
                row = s["sums"][bass.ds(h, 1), :]
                wait(sum_out, 64 * h + 64)
                sp.dma_start(sums[:, :], row.rearrange("a (p b) -> (a p) b", p=P)).then_inc(sums_in, 16)
                wait(rcp_done, h + 1)
                row = s["rcps"][bass.ds(h, 1), :]
                sp.dma_start(row.rearrange("a (p b) -> (a p) b", p=P), rcp[:, :]).then_inc(rcp_out, 16)
                wait(rcp_out, 16 * h + 16)
                sp.dma_start(rcp_all[:, :], row.broadcast_to([HD, SEQ])).then_inc(rcp_in, 16)

            def head(h, b, more=True, most=True):
                before = not isinstance(h, int) or h > 0
                if before:
                    sum_store(h - 1, 1 - b, 3)
                    rcp_rows(h - 1)
                sp.dma_start(zb[:, b], s["zb"][bass.ds(h * HD, HD), 0:SEQ]).then_inc(zb_in[b], 16)
                if more:
                    wait(pv_done, NS * h + RING)
                    load_main(h + 1, 1 - b)
                if most:
                    load_max(h + 2, b)
                for q in range(2):
                    sum_store(h, b, q)
                if before:
                    y_store(h - 1, 1 - b, 0)
                sum_store(h, b, 2)
                if before:
                    y_store(h - 1, 1 - b, 1)
                if more:
                    max_rows(h + 1, 1 - b)
                if before:
                    y_store(h - 1, 1 - b, 2)
                    y_store(h - 1, 1 - b, 3)

            load_max(0, 0)
            load_main(0, 0)
            load_max(1, 1)
            max_rows(0, 0)
            head(0, 0)
            head(1, 1)
            with sp.Fori(1, H // 2 - 1) as i:
                head(2 * i, 0)
                head(2 * i + 1, 1)
            head(H - 2, 0, True, False)
            head(H - 1, 1, False, False)
            sum_store(H - 1, 1, 3)
            rcp_rows(H - 1)
            for q in range(NQ):
                y_store(H - 1, 1, q)
            sp.wait_ge(y_out[0], 16 + 32 * NQ // 2 * H)
            sp.wait_ge(y_out[1], 16 + 32 * NQ // 2 * H)

        @block.tensor
        def _(pe):
            def scores(h, b, st):
                q, kb = steps[st]
                d = max(0, kb - 4 * q)
                keys, cols = slice(kb * P, (kb + 1) * P), slice(d * P, QW)
                asked = slice(q * QW + d * P, (q + 1) * QW)
                if st == 0:
                    pe.wait_ge(main_in[b], used(h, b, 144))
                    pe.wait_ge(m_in[b], used(h, b, 32))
                pe.wait_ge(p_done, NS * h + st + 1)
                bank = s_bank[st % RING]
                diagonal = kb >= 4 * q
                pe.matmul(bank[:, cols], ks[:, b, keys], qs[:, b, asked], start=True, stop=False)
                last = pe.matmul(bank[:, cols], k2[:, b, keys], q2[:, b, asked], start=False, stop=not diagonal)
                if diagonal:
                    last = pe.matmul(bank[:, d * P:(d + 1) * P], eye_b[:, :], mask_b[:, :], start=False, stop=True)
                last.then_inc(s_done, 1)

            def values(h, b, st):
                q, kb = steps[st]
                d = max(0, kb - 4 * q)
                cols = slice(d * P, QW)
                if kb == 0:
                    pe.wait_ge(o_read, NQ * h + q + 1)
                pe.wait_ge(*low_value(h, st))
                r = st % RING
                o = o_bank[q % 2][:, cols]
                pe.matmul(o, v_hi[:, b, kb, :], p_hi[:, r, cols], start=(kb == 0), stop=False)
                pe.matmul(o, v_hi[:, b, kb, :], p_lo[:, r, cols], start=False, stop=False)
                pe.matmul(o, v_lo[:, b, kb, :], p_hi[:, r, cols], start=False, stop=(kb == 4 * q + 3))\
                  .then_inc(pv_done, 1)

            def unit(h, b, u):
                i, c = units[u]
                end = min((c + 1) * QW, (i + 1) * P)
                width = end - c * QW
                if u == 0:
                    pe.wait_ge(max_in[b], used(h, b, 48))
                    if not isinstance(h, int) or h:
                        pe.wait_ge(rows_done, h)
                pe.wait_ge(unit_read, NU * h + u + 1)
                bank = m_bank[u % 2]
                last = pe.matmul(bank[:, 0:width], qm[0:HD + 2, b, i * P:(i + 1) * P], km[0:HD + 2, b, c * QW:end],
                                 start=True, stop=(c < i // 4))
                if c == i // 4:
                    last = pe.matmul(bank[:, width - P:width], mask_b[:, :], eye_b[:, :], start=False, stop=True)
                last.then_inc(unit_done, 1)

            def turn(h):
                pe.wait_ge(split, h + 1)
                pe.transpose(m_bank[0][0:2 * NB, 0:P], neg_max[:, :].bitcast(F32), eye[:, :]).then_inc(turned, 1)

            def head(h, b, more=True, ahead=True):
                for st in range(NS):
                    if st + LEAD < NS:
                        scores(h, b, st + LEAD)
                    elif ahead:
                        scores(h + 1, 1 - b, st + LEAD - NS)
                    if more:
                        for u in step_units(st):
                            unit(h + 1, 1 - b, u)
                        if st == TURN:
                            turn(h + 1)
                    values(h, b, st)

            pe.wait_ge(consts, 2)
            for u in range(NU):
                unit(0, 0, u)
            turn(0)
            for st in range(LEAD):
                scores(0, 0, st)
            with pe.Fori(0, H // 2 - 1) as i:
                head(2 * i, 0)
                head(2 * i + 1, 1)
            head(H - 2, 0)
            head(H - 1, 1, False, False)

        @block.scalar
        def _(act):
            act.sem_inc(p_done, RING)
            act.sem_inc(pv_done, RING)
            act.sem_inc(unit_read, 2)
            act.sem_inc(o_read, 2)

            def probs(h, st):
                q, kb = steps[st]
                cols = slice(max(0, kb - 4 * q) * P, QW)
                r = st % RING
                act.wait_ge(s_done, NS * h + st + 1)
                act.wait_ge(pv_done, NS * h + st + 1)
                act.activation(p[:, r, cols], s_bank[r][:, cols], ACT.Exp, scale=SCALE)
                act.activation(p_hi[:, r, cols], s_bank[r][:, cols], ACT.Exp, scale=SCALE).then_inc(p_done, 1)

            def copy_rows(h, b):
                act.wait_ge(turned, h + 1)
                if not isinstance(h, int) or h:
                    act.wait_ge(m_in[1 - b], used(h - 1, 1 - b, 32))
                act.activation(neg_rows[:, :], m_bank[0][0:2 * NB, 0:P], ACT.Copy).then_inc(rows_done, 1)

            def head(h, b, more=True):
                for st in range(NS):
                    probs(h, st)
                    if more and st == TURN + 1:
                        copy_rows(h + 1, 1 - b)
                    if st in FINISH and FINISH[st][1] == 2 and (not isinstance(h, int) or h):
                        upper(h - 1, 1 - b, FINISH[st][0])

            def upper(h, b, q):
                act.wait_ge(y_gated, NQ * h + q + 1)
                act.wait_ge(y_out[q % 2], 64 * h + 32 * (q // 2) + 16)
                act.activation(y_hi[:, q % 2, :], y[0:HD, b, q * QW:(q + 1) * QW], ACT.Copy).then_inc(yh_done, 1)

            copy_rows(0, 0)
            head(0, 0)
            head(1, 1)
            with act.Fori(1, H // 2 - 1) as i:
                head(2 * i, 0)
                head(2 * i + 1, 1)
            head(H - 2, 0)
            head(H - 1, 1, False)
            for q in range(NQ):
                upper(H - 1, 1, q)

        @block.vector
        def _(dve):
            dve.wait_ge(const_in, 32)
            dve.tensor_copy(eye_b[:, :], eye[:, :]).then_inc(consts, 1)
            dve.tensor_copy(mask_b[:, :], mask[:, :]).then_inc(consts, 1)

            scale, gate, lower = finishing(dve)

            def low(h, st):
                if st % POOLS == POOLS - 1:
                    return
                q, kb = steps[st]
                cols = slice(max(0, kb - 4 * q) * P, QW)
                r = st % RING
                dve.wait_ge(p_done, NS * h + st + 1 + RING)
                dve.tensor_tensor(p_lo[:, r, cols], p[:, r, cols], p_hi[:, r, cols].bitcast(F32), ALU.subtract)\
                   .then_inc(lo_dve, 1)

            def unit(h, u):
                i, c = units[u]
                width = min((c + 1) * QW, (i + 1) * P) - c * QW
                dve.wait_ge(unit_done, NU * h + u + 1)
                dve.tensor_reduce(piece_max[:, i, c:c + 1], m_bank[u % 2][:, 0:width], AX_X, ALU.max)\
                   .then_inc(unit_read, 1)

            def whole_max(h):
                dve.wait_ge(unit_read, NU * h + NU + 2)
                if not isinstance(h, int) or h:
                    dve.wait_ge(turned, h)
                dve.tensor_reduce(row_max[:, :], piece_max[:, :, :], AX_X, ALU.max).then_inc(maxed, 1)
                dve.wait_ge(maxed, 2 * h + 1)
                dve.tensor_scalar(neg_max[:, 0:NB], row_max[:, :], -1.0, None, ALU.mult).then_inc(maxed, 1)
                dve.wait_ge(maxed, 2 * h + 2)
                dve.scalar_tensor_tensor(out=neg_max[:, NB:2 * NB], in0=row_max[:, :], scalar=-1.0,
                                         in1=neg_max[:, 0:NB].bitcast(F32), op0=ALU.mult, op1=ALU.subtract)\
                   .then_inc(split, 1)

            def take(h, b, q):
                dve.wait_ge(pv_done, NS * h + ends[q] + 1 + RING)
                if not isinstance(h, int) or h > 1:
                    dve.wait_ge(yl_done, NQ * (h - 1))
                dve.tensor_copy(y[:, b, q * QW:(q + 1) * QW], o_bank[q % 2][0:HD + 1, :]).then_inc(o_read, 1)

            def invert(h):
                dve.wait_ge(sums_in, 16 * h + 16)
                if not isinstance(h, int) or h:
                    dve.wait_ge(rcp_out, 16 * h)
                dve.reciprocal(rcp[:, :], sums[:, :]).then_inc(rcp_done, 1)

            def head(h, b, more=True):
                for st in range(NS):
                    if st + 1 < NS:
                        low(h, st + 1)
                    elif more or not b:
                        low(h + 1, 0)
                    if more:
                        for u in step_units(st):
                            unit(h + 1, u)
                            if u == NU - 1:
                                whole_max(h + 1)
                    if st - 2 in ends[:-1]:
                        take(h, b, ends.index(st - 2))
                    if b and st == 1:
                        take(h - 1, 1 - b, NQ - 1)
                    if st == INVERT and (not isinstance(h, int) or h):
                        invert(h - 1)
                if b:
                    take(h, b, NQ - 1)

            for t in (k2, q2, qm):
                dve.memset(t[HD:HR, :, :].bitcast(F32), 1.0).then_inc(ones_set, 1)
            dve.wait_ge(ones_set, 6)
            for u in range(NU):
                unit(0, u)
            whole_max(0)
            low(0, 0)
            head(0, 0)
            head(1, 1)
            with dve.Fori(1, H // 2 - 1) as i:
                head(2 * i, 0)
                head(2 * i + 1, 1)
            head(H - 2, 0)
            head(H - 1, 1, False)
            invert(H - 1)
            for q in range(NQ):
                scale(H - 1, 1, q)
                gate(H - 1, 1, q)
            for q in range(NQ):
                lower(H - 1, 1, q)

        @block.gpsimd
        def _(pool):
            pool.memset(v_hi[:, :, :, HD:P].bitcast(F32), 1.0).then_inc(ones_set, 1)
            pool.memset(v_lo[:, :, :, HD:P].bitcast(F32), 0.0).then_inc(ones_set, 1)
            pool.memset(piece_max[:, :, :], -3e38).then_inc(ones_set, 1)

            def low(h, st):
                q, kb = steps[st]
                cols = slice(max(0, kb - 4 * q) * P, QW)
                r = st % RING
                pool.wait_ge(p_done, NS * h + st + 1 + RING)
                pool.tensor_tensor(p_lo[:, r, cols], p[:, r, cols], p_hi[:, r, cols].bitcast(F32), ALU.subtract)\
                    .then_inc(lo_pool, 1)

            scale, gate, lower = finishing(pool)

            def head(h, b):
                before = not isinstance(h, int) or h > 0
                for st in range(NS):
                    if st % POOLS == POOLS - 1:
                        low(h, st)
                    if before and st in FINISH_LOW:
                        lower(h - 1, 1 - b, FINISH_LOW[st])
                    if before and st in FINISH and FINISH[st][1] < 2:
                        (scale, gate)[FINISH[st][1]](h - 1, 1 - b, FINISH[st][0])

            head(0, 0)
            head(1, 1)
            with pool.Fori(1, H // 2) as i:
                head(2 * i, 0)
                head(2 * i + 1, 1)


def sample_attention(nc, root, s, cache_k, cache_v, ident, causal, blocks):
    with ExitStack() as ctx:
        sb, pb, sem = tools(nc, ctx, root, "sa")
        NK = NB + 1
        KEYS = PAST + DEC
        PAIRS = H // 2
        HQ = H * DEC
        PIECE = 4 * P
        NP = PAST // PIECE
        GF = ATT // 2
        WIDE = HQ + 2 * DEC
        kT_hi = sb("kT_hi", [P, PAIRS, KEYS], F32R)
        kT_lo = sb("kT_lo", [P, PAIRS, KEYS], F32R)
        v_hi = sb("v_hi", [P, NK, ATT], F32R)
        v_lo = sb("v_lo", [P, NK, ATT], F32R)
        k_rows = sb("k_rows", [P, 2, 4, ATT])
        v_rows = sb("v_rows", [P, 2, 2, ATT])
        ck = sb("ck", [2 * H, KEYS], F32R)
        pick32 = sb("pick32", [2 * H, HQ])
        pick = sb("pick", [2 * H, HQ], F32R)
        q_hi = sb("q_hi", [P, PAIRS * WIDE], F32R)
        q_lo = sb("q_lo", [P, PAIRS * WIDE], F32R)
        zb = sb("zb", [P, PAIRS, DEC])
        probs = sb("probs", [P, 2, KEYS])
        p_hi = sb("p_hi", [P, 2, 2 * HQ], F32R)
        p_lo = sb("p_lo", [P, 2, 2 * HQ], F32R)
        eye = sb("eye", [P, P])
        mask = sb("mask", [P, P])
        eye_b = sb("eye_b", [P, P], BF16)
        mask_b = sb("mask_b", [P, 4, DEC], BF16)
        piece_max = sb("piece_max", [P, 2, NP + 1])
        row_max = sb("row_max", [P, 2])
        shift = sb("shift", [P, 2])
        sums = sb("sums", [P, 2])
        rcp = sb("rcp", [P, 2])
        y_rows = sb("y_rows", [P, 2, GF])
        y = sb("y", [P, PAIRS, DEC])
        y_hi = sb("y_hi", [P, PAIRS, DEC], F32R)
        y_lo = sb("y_lo", [P, PAIRS, DEC], F32R)
        t_bank = [pb(f"t{i}") for i in range(4)]
        s_bank = [pb(f"s{i}") for i in range(2)]
        o_bank = [pb(f"o{i}") for i in range(2)]

        const_in, zeroed, consts = sem("const_in"), sem("zeroed"), sem("consts")
        k_in = [sem(f"k_in{i}") for i in range(2)]
        v_in = [sem(f"v_in{i}") for i in range(2)]
        new_in, out = sem("new_in"), sem("out")
        turned, k_hi_done, k_lo_done, v_hi_done, v_lo_done = (
            sem("turned"), sem("k_hi"), sem("k_lo"), sem("v_hi"), sem("v_lo"))
        scored, copied, piece_maxed, maxed, shifted, exped = (
            sem("scored"), sem("copied"), sem("piece_maxed"), sem("maxed"), sem("shifted"), sem("exped"))
        p_turned, ph_done, pl_done, pv_done, summed, rcp_done = (
            sem("p_turned"), sem("ph"), sem("pl"), sem("pv"), sem("summed"), sem("rcp"))
        rows_done, y_turned, y_done, yh_done, yl_done = (
            sem("rows"), sem("y_turned"), sem("y"), sem("yh"), sem("yl"))
        NEW = slice(PAST, KEYS)
        NT = NB // 2 + 1

        def piece(c):
            return slice(c * PIECE, min((c + 1) * PIECE, KEYS))

        def four(t):
            return t_bank[t % 4][:, :].rearrange("p (a c) -> p a c", a=PAIRS)

        def turned_part(n):
            return (P, 2 * HQ) if n < NT - 1 else (DEC, HQ)

        block = ctx.enter_context(nc.Block())

        @block.sync
        def _(sp):
            def load_k(c):
                sp.dma_start(k_rows[:, c % 2], cache_k[c * PIECE:(c + 1) * PIECE, :].rearrange("(b p) c -> p b c", p=P))\
                  .then_inc(k_in[c % 2], 16)

            def load_v(d):
                sp.dma_start(v_rows[:, d % 2], cache_v[d * 2 * P:(d + 1) * 2 * P, :].rearrange("(b p) c -> p b c", p=P))\
                  .then_inc(v_in[d % 2], 16)

            sp.dma_start(eye[:, :], ident).then_inc(const_in, 16)
            load_k(0)
            load_v(0)
            load_v(1)
            sp.dma_start(mask[:, :], causal).then_inc(const_in, 16)
            sp.dma_start(pick32[:, :], blocks).then_inc(const_in, 16)
            sp.dma_start(zb[:, :, :], s["zb"][:, SEQ:T].rearrange("(a p) q -> p a q", p=P)).then_inc(const_in, 16)
            sp.wait_ge(zeroed, 2)
            for to, of in ((q_hi, s["qh"]), (q_lo, s["ql"])):
                for i in range(2):
                    sp.dma_start(to[i * HD:(i + 1) * HD, :].rearrange("p (a x) -> p a x", a=PAIRS)
                                 [:, :, i * DEC:(i + 1) * DEC].bitcast(F32),
                                 of[:, SEQ:T].rearrange("(a i p) q -> i p a q", i=2, p=HD)[i]).then_inc(new_in, 16)
            for to, of in ((kT_hi, s["kh"]), (kT_lo, s["kl"])):
                sp.dma_start(to[:, :, NEW].bitcast(F32), of[:, SEQ:T].rearrange("(a p) q -> p a q", p=P)).then_inc(new_in, 16)
            for to, of in ((v_hi, s["vh"]), (v_lo, s["vl"])):
                sp.dma_start(to[0:DEC, NB, :].bitcast(F32), of[SEQ:T, :]).then_inc(new_in, 16)
            for i in range(2):
                sp.dma_start(ck[i * H:(i + 1) * H, :].bitcast(F32), s["ck"][i, :, SEQ:CKW]).then_inc(new_in, 16)
            load_k(1)
            for d in range(2, 2 * NP):
                if d % 2 == 0 and d // 2 + 1 < NP:
                    sp.wait_ge(turned, 4 * (d // 2))
                    load_k(d // 2 + 1)
                sp.wait_ge(v_lo_done, d - 1)
                load_v(d)
            sp.wait_ge(yl_done, 1)
            for to, of in ((s["ybh"], y_hi), (s["ybl"], y_lo)):
                sp.dma_start(to[:, SEQ:T].rearrange("(a p) q -> p a q", p=P), of[:, :, :].bitcast(F32)).then_inc(out, 16)
            sp.wait_ge(out, 32)

        @block.gpsimd
        def _(pool):
            pool.memset(q_hi[:, :].bitcast(F32), 0.0).then_inc(zeroed, 1)
            pool.memset(q_lo[:, :].bitcast(F32), 0.0).then_inc(zeroed, 1)
            for d in range(2 * NP):
                pool.wait_ge(v_hi_done, d + 1)
                two = slice(2 * d, 2 * d + 2)
                pool.tensor_tensor(v_lo[:, two, :], v_rows[:, d % 2], v_hi[:, two, :].bitcast(F32),
                                   ALU.subtract).then_inc(v_lo_done, 1)

        @block.scalar
        def _(act):
            def copy_scores(c):
                for g in range(2):
                    keys = piece(c)
                    act.wait_ge(scored, 2 * c + g + 1)
                    act.activation(probs[:, g, keys], s_bank[g][:, 0:keys.stop - keys.start], ACT.Copy)\
                       .then_inc(copied, 1)

            def exps(c):
                for g in range(2):
                    act.activation(probs[:, g, piece(c)], probs[:, g, piece(c)], ACT.Exp, scale=SCALE,
                                   bias=shift[:, g:g + 1]).then_inc(exped, 1)

            def upper(n):
                rows, cols = turned_part(n)
                act.wait_ge(p_turned, n + 1)
                if n >= 2:
                    act.wait_ge(pv_done, n - 1)
                act.activation(p_hi[0:rows, n % 2, 0:cols], t_bank[n % 4][0:rows, 0:cols], ACT.Copy)\
                   .then_inc(ph_done, 1)

            for c in range(NP):
                for t in range(4 * c, 4 * c + 4):
                    act.wait_ge(turned, t + 1)
                    act.activation(kT_hi[:, :, t * P:(t + 1) * P], four(t), ACT.Copy).then_inc(k_hi_done, 1)
                for d in range(2 * c, 2 * c + 2):
                    act.wait_ge(v_in[d % 2], 16 * (d // 2) + 16)
                    act.activation(v_hi[:, 2 * d:2 * d + 2, :], v_rows[:, d % 2], ACT.Copy).then_inc(v_hi_done, 1)
                if c:
                    copy_scores(c - 1)
            copy_scores(NP - 1)
            copy_scores(NP)
            act.wait_ge(copied, 2 * NP + 2)
            act.wait_ge(shifted, 1)
            exps(0)
            for c in range(NP):
                exps(c + 1)
                upper(2 * c)
                upper(2 * c + 1)
            upper(NT - 1)
            act.wait_ge(y_done, 4)
            act.activation(y_hi[:, :, :], y[:, :, :], ACT.Copy).then_inc(yh_done, 1)

        @block.vector
        def _(dve):
            dve.wait_ge(const_in, 64)
            dve.tensor_copy(pick[:, :], pick32[:, :]).then_inc(consts, 1)
            dve.tensor_copy(eye_b[:, :], eye[:, :]).then_inc(consts, 1)
            for h in range(4):
                dve.tensor_copy(mask_b[:, h, :], mask[:, 0:DEC]).then_inc(consts, 1)

            def max_scores(c):
                for g in range(2):
                    keys = piece(c)
                    dve.wait_ge(copied, 2 * c + g + 1)
                    dve.tensor_reduce(piece_max[:, g, c:c + 1], probs[:, g, keys], AX_X, ALU.max)\
                       .then_inc(piece_maxed, 1)

            def lower(n):
                rows, cols = turned_part(n)
                dve.wait_ge(ph_done, n + 1)
                dve.tensor_tensor(p_lo[0:rows, n % 2, 0:cols], t_bank[n % 4][0:rows, 0:cols],
                                  p_hi[0:rows, n % 2, 0:cols].bitcast(F32), ALU.subtract).then_inc(pl_done, 1)

            for c in range(NP):
                for t in range(4 * c, 4 * c + 4):
                    dve.wait_ge(k_hi_done, t + 1)
                    at = slice(t * P, (t + 1) * P)
                    dve.tensor_tensor(kT_lo[:, :, at], four(t), kT_hi[:, :, at].bitcast(F32), ALU.subtract)\
                       .then_inc(k_lo_done, 1)
                if c:
                    max_scores(c - 1)
            max_scores(NP - 1)
            max_scores(NP)
            dve.wait_ge(piece_maxed, 2 * NP + 2)
            dve.tensor_reduce(row_max[:, :], piece_max[:, :, :], AX_X, ALU.max).then_inc(maxed, 1)
            dve.wait_ge(maxed, 1)
            dve.tensor_scalar(shift[:, :], row_max[:, :], -SCALE, None, ALU.mult).then_inc(shifted, 1)
            for n in range(NT):
                lower(n)
                if n >= NT - 3 and n < NT - 1:
                    g = n - (NT - 3)
                    dve.wait_ge(exped, 2 * NP + 2)
                    dve.tensor_reduce(sums[:, g:g + 1], probs[:, g, :], AX_X, ALU.add).then_inc(summed, 1)
            dve.wait_ge(summed, 2)
            dve.reciprocal(rcp[:, :], sums[:, :]).then_inc(rcp_done, 1)
            dve.wait_ge(rcp_done, 1)
            dve.wait_ge(pv_done, NT)
            for g in range(2):
                dve.tensor_scalar(y_rows[:, g, :], o_bank[g][:, 0:GF], rcp[:, g:g + 1], None, ALU.mult)\
                   .then_inc(rows_done, 1)
            dve.wait_ge(y_turned, 1)
            for i in range(2):
                rows = slice(i * HD, (i + 1) * HD)
                for a in range(2):
                    own = slice((2 * a + i) * DEC, (2 * a + i + 1) * DEC)
                    o = s_bank[0][rows, :].rearrange("p (g a c) -> p g a c", g=2, a=2)[:, :, a, own]
                    pair = y[rows, :, :].rearrange("p (g a) q -> p g a q", a=2)[:, :, a, :]
                    gate = zb[rows, :, :].rearrange("p (g a) q -> p g a q", a=2)[:, :, a, :]
                    dve.tensor_tensor(pair, o, gate, ALU.mult).then_inc(y_done, 1)
            dve.wait_ge(yh_done, 1)
            dve.tensor_tensor(y_lo[:, :, :], y[:, :, :], y_hi[:, :, :].bitcast(F32), ALU.subtract).then_inc(yl_done, 1)

        @block.tensor
        def _(pe):
            def scores(c):
                pe.wait_ge(k_lo_done, min(4 * c + 4, NB))
                keys = piece(c)
                width = keys.stop - keys.start
                for g in range(2):
                    rows = slice(g * P, (g + 1) * P)
                    if c:
                        pe.wait_ge(copied, 2 * c + g - 1)
                    to = s_bank[g][:, 0:width]
                    pe.matmul(to, pick[:, rows], ck[:, keys], start=True, stop=False)
                    for a in (2 * g, 2 * g + 1):
                        own = slice(a * HQ + g * P, a * HQ + (g + 1) * P)
                        for x, k in ((q_hi, kT_hi), (q_lo, kT_hi), (q_hi, kT_lo)):
                            last = pe.matmul(to, x[:, own], k[:, a, keys], start=False,
                                             stop=(c < NP and a == 2 * g + 1 and k is kT_lo))
                    if c == NP:
                        last = pe.matmul(to, mask_b[:, :, :].rearrange("p h q -> p (h q)"), eye_b[:, 0:DEC],
                                         start=False, stop=True)
                    last.then_inc(scored, 1)

            def turn(n):
                pe.wait_ge(exped, 2 * (n // 2) + 2)
                if n >= 4:
                    pe.wait_ge(pl_done, n - 3)
                rows = turned_part(n)[0]
                for kb in range(2 * n, min(2 * n + 2, NK)):
                    for g in range(2):
                        at = (kb % 2) * HQ + g * P
                        last = pe.transpose(t_bank[n % 4][0:rows, at:at + P], probs[:, g, kb * P:kb * P + rows],
                                            eye[:, :])
                last.then_inc(p_turned, 1)

            def values(n):
                pe.wait_ge(pl_done, n + 1)
                if n < NT - 1:
                    pe.wait_ge(v_lo_done, n + 1)
                rows = turned_part(n)[0]
                for kb in range(2 * n, min(2 * n + 2, NK)):
                    for g in range(2):
                        own = slice((kb % 2) * HQ + g * P, (kb % 2) * HQ + (g + 1) * P)
                        feat = slice(g * GF, (g + 1) * GF)
                        for i, (x, v) in enumerate(((p_hi, v_hi), (p_lo, v_hi), (p_hi, v_lo))):
                            last = pe.matmul(o_bank[g][:, 0:GF], x[0:rows, n % 2, own], v[0:rows, kb, feat],
                                             start=(kb == 0 and i == 0), stop=(kb == NK - 1 and i == 2))
                last.then_inc(pv_done, 1)

            pe.wait_ge(const_in, 64)
            for c in range(NP):
                pe.wait_ge(k_in[c % 2], 16 * (c // 2) + 16)
                for t in range(4 * c, 4 * c + 4):
                    if t >= 4:
                        pe.wait_ge(k_lo_done, t - 3)
                    for a in range(PAIRS):
                        last = pe.transpose(t_bank[t % 4][:, a * P:(a + 1) * P],
                                            k_rows[:, c % 2, t % 4, a * P:(a + 1) * P], eye[:, :])
                    last.then_inc(turned, 1)
                if c == 0:
                    pe.wait_ge(consts, 6)
                    pe.wait_ge(new_in, 16 * 10)
                else:
                    scores(c - 1)
            scores(NP - 1)
            scores(NP)
            turn(0)
            turn(1)
            for n in range(NT):
                if n + 2 < NT:
                    turn(n + 2)
                values(n)
            pe.wait_ge(rows_done, 2)
            for g in range(2):
                for a in range(2):
                    at = (2 * g + a) * P
                    last = pe.transpose(s_bank[0][:, at:at + P], y_rows[:, g, a * P:(a + 1) * P], eye[:, :])
            last.then_inc(y_turned, 1)


def merge(nc, root, s, wpa_tiles, wpb_tiles):
    with ExitStack() as ctx:
        sb, pb, sem = tools(nc, ctx, root, "mg")
        YT = CONV // P
        names = ("yah", "yal", "ybh", "ybl")
        ys = {n: sb(n, [P, YT, T], F32R) for n in names}
        w = sb("w", [P, 2, 2 * YT, P])
        w_hi = sb("w_hi", [P, 2, 2 * YT, P], F32R)
        w_lo = sb("w_lo", [P, 2, 2 * YT, P], F32R)
        gates = sb("gates", [P, 2, 2, CH])
        part = sb("part", [P, 2, 2, CH])
        mixed = sb("mixed", [P, 2, CH])
        banks = [[pb(f"b{i}{x}") for x in "ab"] for i in range(2)]
        y_in = [sem(f"y_in{n}") for n in range(NCH)]
        w_in = [sem(f"w_in{i}") for i in range(2)]
        g_in = [sem(f"g_in{i}") for i in range(2)]
        m_out = [sem(f"m_out{i}") for i in range(2)]
        w_hi_done, w_lo_done, proj_done, gated, added, sp_passed = (
            sem("w_hi"), sem("w_lo"), sem("proj"), sem("gated"), sem("added"), sem("sp_passed"))
        NI = D // P

        block = ctx.enter_context(nc.Block())

        @block.sync
        def _(sp):
            wait = settled(sp, sp_passed)

            def load_w(i, b):
                for x, tiles in enumerate((wpa_tiles, wpb_tiles)):
                    sp.dma_start(w[:, b, x * YT:(x + 1) * YT], tiles[bass.ds(i, 1)].rearrange("a p k n -> (a p) k n"))\
                      .then_inc(w_in[b], 16)

            def load_gates(i, n, r):
                for x in range(2):
                    sp.dma_start(gates[:, r, x], s["g"][bass.ds(i * P + x * D, P), n * CH:(n + 1) * CH])\
                      .then_inc(g_in[r], 16)

            def store(i, n, r):
                c = 5 * i + n
                wait(added, c + 1)
                sp.dma_start(s["mixed"][bass.ds(i * P, P), n * CH:(n + 1) * CH], mixed[:, r]).then_inc(m_out[r], 16)

            load_w(0, 0)
            for n in range(NCH):
                tok = slice(n * CH, (n + 1) * CH)
                for name in names:
                    sp.dma_start(ys[name][:, :, tok].bitcast(F32), s[name][:, tok].rearrange("(k p) t -> p k t", p=P))\
                      .then_inc(y_in[n], 16)
                if n == 0:
                    load_w(1, 1)
                    load_gates(0, 0, 0)
                    load_gates(0, 1, 1)

            def tile(i, b, more=True, most=True):
                for n in range(NCH):
                    r = (b * NCH + n) % 2
                    wait(gated, 5 * i + n + 1)
                    if n < NCH - 2:
                        load_gates(i, n + 2, r)
                    elif more:
                        load_gates(i + 1, n + 2 - NCH, r)
                    if n == NCH - 1 and most:
                        wait(w_lo_done, i + 1)
                        load_w(i + 2, b)
                    store(i, n, r)

            with sp.Fori(0, NI // 2 - 1) as j:
                tile(2 * j, 0)
                tile(2 * j + 1, 1)
            tile(NI - 2, 0, True, False)
            tile(NI - 1, 1, False, False)
            sp.wait_ge(m_out[0], 16 * NI * NCH // 2)
            sp.wait_ge(m_out[1], 16 * NI * NCH // 2)

        @block.scalar
        def _(act):
            for i in range(2):
                act.wait_ge(w_in[i], 32)
                act.activation(w_hi[:, i], w[:, i], ACT.Copy).then_inc(w_hi_done, 1)
            with act.Fori(0, NI // 2 - 1) as j:
                for b in range(2):
                    i = 2 * j + b
                    act.wait_ge(w_in[b], 32 * j + 64)
                    act.wait_ge(proj_done, 5 * i + 5)
                    act.activation(w_hi[:, b], w[:, b], ACT.Copy).then_inc(w_hi_done, 1)

        @block.gpsimd
        def _(pool):
            def low_w(i, b):
                pool.wait_ge(w_hi_done, i + 1)
                pool.tensor_tensor(w_lo[:, b], w[:, b], w_hi[:, b].bitcast(F32), ALU.subtract).then_inc(w_lo_done, 1)

            def tile(i, b, most=True):
                for n in range(NCH):
                    r = (b * NCH + n) % 2
                    c = 5 * i + n
                    pool.wait_ge(gated, c + 1)
                    before = (b * NCH + n) // 2
                    if not isinstance(i, int) or i or n >= 2:
                        pool.wait_ge(m_out[r], 40 * (i - b) + 16 * before)
                    pool.tensor_tensor(mixed[:, r], part[:, r, 0], part[:, r, 1], ALU.add).then_inc(added, 1)
                if most:
                    low_w(i + 2, b)

            low_w(0, 0)
            low_w(1, 1)
            tile(0, 0)
            tile(1, 1)
            with pool.Fori(1, NI // 2 - 1) as j:
                tile(2 * j, 0)
                tile(2 * j + 1, 1)
            tile(NI - 2, 0, False)
            tile(NI - 1, 1, False)

        @block.vector
        def _(dve):
            def tile(i, b):
                for n in range(NCH):
                    r = (b * NCH + n) % 2
                    c = 5 * i + n
                    dve.wait_ge(proj_done, c + 1)
                    dve.wait_ge(g_in[r], 80 * (i - b) + 32 * ((b * NCH + n) // 2) + 32)
                    if not isinstance(i, int) or i or n >= 2:
                        dve.wait_ge(added, c - 1)
                    for x in range(2):
                        last = dve.tensor_tensor(part[:, r, x], banks[r][x][:, 0:CH], gates[:, r, x], ALU.mult)
                    last.then_inc(gated, 1)

            tile(0, 0)
            tile(1, 1)
            with dve.Fori(1, NI // 2) as j:
                tile(2 * j, 0)
                tile(2 * j + 1, 1)

        @block.tensor
        def _(pe):
            def tile(i, b):
                for n in range(NCH):
                    r = (b * NCH + n) % 2
                    c = 5 * i + n
                    tok = slice(n * CH, (n + 1) * CH)
                    if n == 0:
                        pe.wait_ge(w_lo_done, i + 1)
                    if isinstance(i, int) and i == 0:
                        pe.wait_ge(y_in[n], 64)
                    if not isinstance(i, int) or i or n >= 2:
                        pe.wait_ge(gated, c - 1)
                    for x, (hi, lo) in enumerate((("yah", "yal"), ("ybh", "ybl"))):
                        last = project(pe, banks[r][x][:, 0:CH],
                                       [(w_hi[:, b, x * YT + k, :], w_lo[:, b, x * YT + k, :], ys[hi][:, k, tok],
                                         ys[lo][:, k, tok]) for k in range(YT)])
                    last.then_inc(proj_done, 1)

            tile(0, 0)
            tile(1, 1)
            with pe.Fori(1, NI // 2) as j:
                tile(2 * j, 0)
                tile(2 * j + 1, 1)


def output_norm(nc, root, s, w_out, ln_out, y_prompt, y_sample):
    with ExitStack() as ctx:
        sb, pb, sem = tools(nc, ctx, root, "ln1")
        w = sb("w", [P, KT, D])
        w_hi = sb("w_hi", [P, KT, D], F32R)
        w_lo = sb("w_lo", [P, KT, D], F32R)
        m = [sb(f"m{i}", [P, KT, P]) for i in range(2)]
        m_hi = [sb(f"m_hi{i}", [P, KT, P], F32R) for i in range(2)]
        m_lo = [sb(f"m_lo{i}", [P, KT, P], F32R) for i in range(2)]
        h = sb("h", [P, 2, D])
        y = sb("y", [P, 2, D])
        gain = sb("gain", [P, D])
        shift = sb("shift", [P, D])
        stats = sb("stats", [P, 2, 12])
        mv = sb("mv", [P, 2, 2])
        var = sb("var", [P, 2])
        rstd = sb("rstd", [P, 2])
        nmr = sb("nmr", [P, 2])
        power = sb("power", [P, 1])
        banks = [pb(f"b{i}", (P, D)) for i in range(2)]
        const_in, w_in, aux = sem("const_in"), [sem(f"w_in{k}") for k in range(KT)], sem("aux")
        m_in = [sem(f"m_in{i}") for i in range(2)]
        h_in = [sem(f"h_in{i}") for i in range(2)]
        y_out = [sem(f"y_out{i}") for i in range(2)]
        w_hi_done, w_lo_done, m_hi_done, m_lo_done, proj_done = (
            sem("w_hi"), sem("w_lo"), sem("m_hi"), sem("m_lo"), sem("proj"))
        summed, stats_done, aggr_done, mv_done, rstd_done, coef_done, yn_done, gained, y_done, passed, sp_passed = (
            sem(x) for x in ("summed", "stats", "aggr", "mv", "rstd", "coef", "yn", "gained", "y", "passed",
                             "sp_passed"))
        N = NB + 1

        block = ctx.enter_context(nc.Block())

        @block.sync
        def _(sp):
            wait = settled(sp, sp_passed)

            def load(t, b, rows):
                sp.dma_start(m[b][:, :, 0:rows], s["mixed"][:, bass.ds(t * P, rows)].rearrange("(k p) t -> p k t", p=P))\
                  .then_inc(m_in[b], 16)

            def load_h(t, b, rows):
                sp.dma_start(h[0:rows, b], s["h"][bass.ds(t * P, rows), :]).then_inc(h_in[b], 16)

            def store(t, b, rows):
                wait(y_done, t + 1)
                to = y_sample if rows == DEC else y_prompt[bass.ds(t * P, P), :]
                sp.dma_start(to, y[0:rows, b]).then_inc(y_out[b], 16)

            for k in range(KT):
                sp.dma_start(w[:, k], w_out[k * P:(k + 1) * P, :]).then_inc(w_in[k], 16)
                if k == 0:
                    load(0, 0, P)
                    load(1, 1, P)
            load_h(0, 0, P)
            load_h(1, 1, P)
            sp.dma_start(gain[:, :], ln_out[0:1, :].broadcast_to([P, D])).then_inc(const_in, 16)
            sp.dma_start(shift[:, :], ln_out[1:2, :].broadcast_to([P, D])).then_inc(const_in, 16)

            def turn(t, b, rows, next_rows):
                if next_rows:
                    wait(m_lo_done, t + 1)
                    load(t + 2, b, next_rows)
                    wait(summed, t + 1)
                    load_h(t + 2, b, next_rows)
                store(t, b, rows)

            with sp.Fori(0, 7) as i:
                turn(2 * i, 0, P, P)
                turn(2 * i + 1, 1, P, P)
            turn(14, 0, P, DEC)
            turn(15, 1, P, 0)
            turn(16, 0, DEC, 0)
            sp.wait_ge(y_out[0], 16 * 9)
            sp.wait_ge(y_out[1], 16 * 8)

        @block.tensor
        def _(pe):
            def tile(t, b, first=False):
                pe.wait_ge(m_lo_done, t + 1)
                if not first:
                    pe.wait_ge(summed, t - 1)
                for half in range(2):
                    cols = slice(half * 512, (half + 1) * 512)
                    for k in range(KT):
                        if first and b == 0 and half == 0:
                            pe.wait_ge(w_lo_done, k + 1)
                        to = banks[b][:, cols]
                        pe.matmul(to, m_hi[b][:, k, :], w_hi[:, k, cols], start=(k == 0), stop=False)
                        pe.matmul(to, m_hi[b][:, k, :], w_lo[:, k, cols], start=False, stop=False)
                        last = pe.matmul(to, m_lo[b][:, k, :], w_hi[:, k, cols], start=False, stop=(k == KT - 1))
                last.then_inc(proj_done, 1)

            tile(0, 0, True)
            tile(1, 1, True)
            with pe.Fori(1, 8) as i:
                tile(2 * i, 0)
                tile(2 * i + 1, 1)
            tile(16, 0)

        @block.scalar
        def _(act):
            def high(t, b, rows, first=False):
                act.wait_ge(m_in[b], 8 * t + 16 - 8 * b)
                if not first:
                    act.wait_ge(proj_done, t - 1)
                act.activation(m_hi[b][:, :, 0:rows], m[b][:, :, 0:rows], ACT.Copy).then_inc(m_hi_done, 1)

            def norm(t, b, rows):
                act.wait_ge(coef_done, t + 1)
                act.activation(y[0:rows, b], y[0:rows, b], ACT.Identity, bias=nmr[0:rows, b:b + 1],
                               scale=rstd[0:rows, b:b + 1]).then_inc(yn_done, 1)

            high(0, 0, P, True)
            for k in range(KT):
                act.wait_ge(w_in[k], 16)
                act.activation(w_hi[:, k], w[:, k], ACT.Copy).then_inc(w_hi_done, 1)
            high(1, 1, P, True)
            with act.Fori(0, 7) as i:
                high(2 * i + 2, 0, P)
                norm(2 * i, 0, P)
                high(2 * i + 3, 1, P)
                norm(2 * i + 1, 1, P)
            high(16, 0, DEC)
            norm(14, 0, P)
            norm(15, 1, P)
            norm(16, 0, DEC)

        @block.vector
        def _(dve):
            def low(t, b, rows):
                dve.wait_ge(m_hi_done, t + 1)
                dve.tensor_tensor(m_lo[b][:, :, 0:rows], m[b][:, :, 0:rows], m_hi[b][:, :, 0:rows].bitcast(F32),
                                  ALU.subtract).then_inc(m_lo_done, 1)

            def stat(t, b, rows, first=False):
                r = slice(0, rows)
                dve.wait_ge(proj_done, t + 1)
                dve.wait_ge(h_in[b], 8 * t + 16 - 8 * b)
                if not first:
                    dve.wait_ge(y_out[b], 8 * t - 8 * b)
                dve.scalar_tensor_tensor(out=y[r, b], in0=h[r, b], scalar=ALPHA, in1=banks[b][r, :],
                                         op0=ALU.mult, op1=ALU.add).then_inc(summed, 1)
                dve.wait_ge(summed, t + 1)
                dve.bn_stats(stats[r, b, 0:6], y[r, b, 0:512])
                dve.bn_stats(stats[r, b, 6:12], y[r, b, 512:1024]).then_inc(stats_done, 1)
                dve.wait_ge(stats_done, t + 1)
                dve.sem_inc(passed, 1)
                dve.bn_aggr(mv[r, b, :], stats[r, b, :]).then_inc(aggr_done, 1)
                dve.wait_ge(aggr_done, t + 1)
                dve.tensor_scalar(var[r, b:b + 1], mv[r, b, 1:2], EPS, None, ALU.add).then_inc(mv_done, 1)
                dve.wait_ge(rstd_done, t + 1)
                dve.tensor_scalar(nmr[r, b:b + 1], mv[r, b, 0:1], rstd[r, b:b + 1], -1.0, ALU.mult, ALU.mult)\
                   .then_inc(coef_done, 1)

            def gained_(t, b, rows):
                r = slice(0, rows)
                dve.wait_ge(yn_done, t + 1)
                dve.tensor_tensor(y[r, b], y[r, b], gain[r, :], ALU.mult).then_inc(gained, 1)

            low(0, 0, P)
            for k in range(KT):
                dve.wait_ge(w_hi_done, k + 1)
                dve.tensor_tensor(w_lo[:, k], w[:, k], w_hi[:, k].bitcast(F32), ALU.subtract).then_inc(w_lo_done, 1)
            low(1, 1, P)
            dve.wait_ge(const_in, 32)
            stat(0, 0, P, True)
            low(2, 0, P)
            gained_(0, 0, P)
            stat(1, 1, P, True)
            low(3, 1, P)
            gained_(1, 1, P)
            with dve.Fori(1, 7) as i:
                for b in range(2):
                    stat(2 * i + b, b, P)
                    low(2 * i + b + 2, b, P)
                    gained_(2 * i + b, b, P)
            stat(14, 0, P)
            low(16, 0, DEC)
            gained_(14, 0, P)
            stat(15, 1, P)
            gained_(15, 1, P)
            stat(16, 0, DEC)
            gained_(16, 0, DEC)

        @block.gpsimd
        def _(pool):
            def tile(t, b, rows):
                r = slice(0, rows)
                pool.wait_ge(mv_done, t + 1)
                pool.tensor_tensor(rstd[r, b:b + 1], var[r, b:b + 1], power[r, :], ALU.pow).then_inc(rstd_done, 1)
                pool.wait_ge(gained, t + 1)
                pool.tensor_tensor(y[r, b], y[r, b], shift[r, :], ALU.add).then_inc(y_done, 1)

            pool.memset(power[:, :], -0.5).then_inc(aux, 1)
            pool.wait_ge(aux, 1)
            pool.wait_ge(const_in, 32)
            with pool.Fori(0, 8) as i:
                tile(2 * i, 0, P)
                tile(2 * i + 1, 1, P)
            tile(16, 0, DEC)


def kernel(**inputs):
    import numpy as np
    import concourse.bacc as bacc
    from concourse.bass_utils import run_bass_kernel_spmd

    a = {k: np.asarray(v) for k, v in inputs.items()}
    w = a["w_in"][0]
    xa, b, c, za, q, k, v, f, zb, g = (0, 512, 1024, 1536, 2048, 2560, 3072, 3584, 3592, 4104)
    at = [x + P * j for j in range(4) for x in (xa, c, za, b)]
    at += [x + P * j for j in range(4) for x in (k, v)] + [x + P * j for j in range(4) for x in (q, zb)]
    at += [g + P * i for i in range(2 * D // P)]

    def tiles(m, starts):
        return np.ascontiguousarray(np.stack([m[:, x:x + P].reshape(-1, P, P).transpose(1, 0, 2) for x in starts]))

    every = range(0, D, P)
    feed = dict(
        x_prompt=a["x_prompt"][0], x_sample=a["x_sample"][0],
        cache_k=a["cache_k"][0, 0].reshape(PAST, ATT), cache_v=a["cache_v"][0, 0].reshape(PAST, ATT),
        cache_logf=a["cache_logf"][0, 0], state_conv=a["state_conv"][0, 0].T,
        ln_in=np.stack([a["ln_in_g"], a["ln_in_b"]]), w_tiles=tiles(w, at),
        w_f=w[:, f:f + H].reshape(KT, P, H).transpose(1, 0, 2), b_f=a["b_f"][0].reshape(H, 1),
        conv_w=a["conv_w"][0].reshape(CW, CONV // P, P).transpose(2, 1, 0), wpa_tiles=tiles(a["w_proj_a"][0], every), wpb_tiles=tiles(a["w_proj_b"][0], every),
        w_out=a["w_out"][0], ln_out=np.stack([a["ln_g"][0], a["ln_b"][0]]),
        ident=np.eye(P, dtype=np.float32), causal=np.tril(np.full((P, P), MASKED, np.float32), -1),
        blocks=np.tile(np.repeat(np.eye(H, dtype=np.float32), DEC, axis=1), (2, 1)),
    )
    feed = {n: np.ascontiguousarray(x) for n, x in feed.items()}
    shapes = dict(
        y_prompt=(SEQ, D), y_sample=(DEC, D), k_prompt=(SEQ, ATT), v_prompt=(SEQ, ATT), logf_prompt=(SEQ, H),
        conv_prompt=(CONV, CW - 1), k_sample=(DEC, ATT), v_sample=(DEC, ATT), logf_sample=(DEC, H),
        conv_sample=(CONV, CW - 1))
    nc = bacc.Bacc("TRN2", target_bir_lowering=False, num_devices=1)
    args = {n: nc.dram_tensor(n, x.shape, mybir.dt.from_np(x.dtype), kind="ExternalInput").ap()
            for n, x in feed.items()}
    args |= {n: nc.dram_tensor(n, x, F32, kind="ExternalOutput").ap() for n, x in shapes.items()}
    build(nc, **args)
    r = run_bass_kernel_spmd(nc, [feed], core_ids=[0]).results[0]
    y = {n: np.asarray(r[n]) for n in shapes}
    return (y["y_prompt"].reshape(1, SEQ, D), y["y_sample"].reshape(1, DEC, D),
            y["k_prompt"].reshape(1, 1, SEQ, H, HD), y["v_prompt"].reshape(1, 1, SEQ, H, HD),
            y["logf_prompt"].reshape(1, 1, SEQ, H), y["conv_prompt"].T.reshape(1, 1, CW - 1, CONV),
            y["k_sample"].reshape(1, 1, DEC, H, HD), y["v_sample"].reshape(1, 1, DEC, H, HD),
            y["logf_sample"].reshape(1, 1, DEC, H), y["conv_sample"].T.reshape(1, 1, CW - 1, CONV))
```

```python
from contextlib import ExitStack

import concourse.bass as bass
from concourse import mybir

F32 = mybir.dt.float32
F32R = mybir.dt.float32r
BF16 = mybir.dt.bfloat16
ALU = mybir.AluOpType
ACT = mybir.ActivationFunctionType
AX_X = mybir.AxisListType.X

P = 128
D = 1024
KT = D // P
SEQ = 2048
DEC = 32
PAST = 2048
T = SEQ + DEC
CH = 416
NCH = T // CH
SUB = CH // 4
TAIL = SEQ - (NCH - 1) * CH
H = 8
HD = 64
ATT = H * HD
CONV = 512
CW = 3
NB = SEQ // P
QW = 512
NQ = SEQ // QW
EPS = 1e-5
ALPHA = 2.0 ** 0.25
SCALE = HD ** -0.5
MASKED = -1e30
CKW = SEQ + PAST + DEC

N_TILES = 48


def build(nc, x_prompt, x_sample, cache_k, cache_v, cache_logf, state_conv, ln_in, w_tiles, w_f, b_f,
          conv_w, wpa_tiles, wpb_tiles, w_out, ln_out, ident, causal, blocks,
          y_prompt, y_sample, k_prompt, v_prompt, logf_prompt, conv_prompt,
          k_sample, v_sample, logf_sample, conv_sample):
    held = []

    def clear():
        nc.clear_and_free_semaphores(held)
        nc.all_engine_barrier()
        held.clear()

    def dram(name, shape):
        return nc.dram_tensor(name, shape, F32, kind="Internal").ap()

    s = dict(
        h=dram("h_rows", (T, D)), qh=dram("q_hi", (ATT, T)), ql=dram("q_lo", (ATT, T)),
        kh=dram("k_hi", (ATT, T)), kl=dram("k_lo", (ATT, T)),
        vh=dram("v_hi", (T, ATT)), vl=dram("v_lo", (T, ATT)),
        zb=dram("silu_zb", (ATT, T)), g=dram("merge_gates", (2 * D, T)),
        yah=dram("ya_hi", (CONV, T)), yal=dram("ya_lo", (CONV, T)),
        ybh=dram("yb_hi", (ATT, T)), ybl=dram("yb_lo", (ATT, T)),
        ck=dram("forget_rows", (2, H, CKW)), sums=dram("sums", (H, SEQ)), rcps=dram("rcps", (H, SEQ)), mixed=dram("mixed", (D, T)),
    )
    with ExitStack() as ctx:
        hT_hi = ctx.enter_context(nc.sbuf_tensor("hT_hi", [P, KT, T], F32R))
        hT_lo = ctx.enter_context(nc.sbuf_tensor("hT_lo", [P, KT, T], F32R))
        input_norm(nc, held, s, hT_hi, hT_lo, x_prompt, x_sample, ln_in, ident)
        first_w = (ctx.enter_context(nc.sbuf_tensor("w0", [P, KT, P], F32)),
                   *(ctx.enter_context(nc.sbuf_tensor(n, [P, KT, P], F32R)) for n in ("w0_hi", "w0_lo")))
        forget_gates(nc, held, s, hT_hi, hT_lo, first_w, w_tiles[0], w_f, b_f, cache_logf, ident, logf_prompt, logf_sample)
        projections(nc, held, s, hT_hi, hT_lo, first_w, w_tiles, conv_w, state_conv, ident,
                    k_prompt, v_prompt, k_sample, v_sample, conv_prompt, conv_sample)
    clear()
    prompt_attention(nc, held, s, ident, causal)
    sample_attention(nc, held, s, cache_k, cache_v, ident, causal, blocks)
    merge(nc, held, s, wpa_tiles, wpb_tiles)
    output_norm(nc, held, s, w_out, ln_out, y_prompt, y_sample)
    clear()


def tools(nc, ctx, held, tag):
    def sb(name, shape, dt=F32):
        return ctx.enter_context(nc.sbuf_tensor(f"{tag}_{name}", shape, dt))

    def pb(name, shape=(P, 512), dt=F32):
        return ctx.enter_context(nc.psum_tensor(f"{tag}_{name}", list(shape), dt))

    def sem(name):
        held.append(nc.alloc_semaphore(name=f"{tag}_{name}"))
        return held[-1]

    return sb, pb, sem


def settled(sp, passed):
    def wait(q, n):
        sp.wait_ge(q, n)
        if not isinstance(n, int):
            sp.sem_inc(passed, 1)
    return wait


def input_norm(nc, held, s, hT_hi, hT_lo, x_prompt, x_sample, ln_in, ident):
    with ExitStack() as ctx:
        sb, pb, sem = tools(nc, ctx, held, "ln0")
        x = sb("x", [P, 4, D])
        xn = sb("xn", [P, 2, D])
        h = sb("h", [P, 2, D])
        gain = sb("gain", [P, D])
        shift = sb("shift", [P, D])
        eye = sb("eye", [P, P])
        stats = sb("stats", [P, 2, 12])
        mv = sb("mv", [P, 2, 2])
        rstd = sb("rstd", [P, 2])
        nmr = sb("nmr", [P, 2])
        var = sb("var", [P, 2])
        power = sb("power", [P, 1])
        tp = [pb(f"tp{i}", (P, KT, P)) for i in range(4)]

        const_in = sem("const_in")
        x_in = [sem(f"x_in{i}") for i in range(4)]
        aux, aggr_done, passed, sp_passed = sem("aux"), sem("aggr"), sem("passed"), sem("sp_passed")
        stats_done, mv_done, rstd_done, coef_done = sem("stats"), sem("mv"), sem("rstd"), sem("coef")
        xn_done, gained, h_done, turned, hi_done, lo_done = (
            sem("xn"), sem("gained"), sem("h"), sem("turned"), sem("hi"), sem("lo"))
        h_out = [sem(f"h_out{i}") for i in range(2)]
        N = NB + 1

        block = ctx.enter_context(nc.Block())

        @block.sync
        def _(sp):
            wait = settled(sp, sp_passed)

            def load(t, rows=P, slot=None):
                src = x_sample if rows == DEC else x_prompt[bass.ds(t * P, P), :]
                sp.dma_start(x[0:rows, slot, :], src).then_inc(x_in[slot], 16)

            def store(t, b, rows=P):
                wait(h_done, t + 1)
                sp.dma_start(s["h"][bass.ds(t * P, rows), :], h[0:rows, b, :]).then_inc(h_out[b], 16)

            for t in range(4):
                load(t, P, t)
                if t == 0:
                    sp.dma_start(gain[:, :], ln_in[0:1, :].broadcast_to([P, D])).then_inc(const_in, 16)
                    sp.dma_start(shift[:, :], ln_in[1:2, :].broadcast_to([P, D])).then_inc(const_in, 16)
                    sp.dma_start(eye[:, :], ident).then_inc(const_in, 16)
            with sp.Fori(0, 3) as i:
                for c in range(4):
                    wait(xn_done, 4 * i + c + 1)
                    load(4 * i + c + 4, P, c)
                    store(4 * i + c, c % 2)
            sp.wait_ge(xn_done, 13)
            load(16, DEC, 0)
            for t in range(12, 16):
                store(t, t % 2)
            store(16, 0, DEC)
            sp.wait_ge(h_out[0], 16 * 9)
            sp.wait_ge(h_out[1], 16 * 8)

        @block.vector
        def _(dve):
            def stat(t, c, rows=P):
                r, b = slice(0, rows), c % 2
                dve.wait_ge(x_in[c], t * 4 + 16 - 4 * c)
                dve.bn_stats(stats[r, b, 0:6], x[r, c, 0:512])
                dve.bn_stats(stats[r, b, 6:12], x[r, c, 512:1024]).then_inc(stats_done, 1)
                dve.wait_ge(stats_done, t + 1)
                dve.sem_inc(passed, 1)
                dve.bn_aggr(mv[r, b, :], stats[r, b, :]).then_inc(aggr_done, 1)
                dve.wait_ge(aggr_done, t + 1)
                dve.tensor_scalar(var[r, b:b + 1], mv[r, b, 1:2], EPS, None, ALU.add).then_inc(mv_done, 1)

            def coef(t, c, rows=P):
                r, b = slice(0, rows), c % 2
                dve.wait_ge(rstd_done, t + 1)
                dve.tensor_scalar(nmr[r, b:b + 1], mv[r, b, 0:1], rstd[r, b:b + 1], -1.0, ALU.mult, ALU.mult)\
                   .then_inc(coef_done, 1)

            def times_gain(t, c, rows=P):
                r, b = slice(0, rows), c % 2
                dve.wait_ge(xn_done, t + 1)
                dve.tensor_tensor(xn[r, b, :], xn[r, b, :], gain[r, :], ALU.mult).then_inc(gained, 1)

            def low(t, c, rows=P):
                dve.wait_ge(hi_done, t + 1)
                tok = bass.ds(t * P, rows)
                dve.tensor_tensor(hT_lo[:, :, tok], tp[c][:, :, 0:rows], hT_hi[:, :, tok].bitcast(F32),
                                  ALU.subtract).then_inc(lo_done, 1)

            def step(t, c, next_rows=P):
                stat(t + 1, (c + 1) % 4, next_rows)
                times_gain(t, c)
                coef(t + 1, (c + 1) % 4, next_rows)
                if not isinstance(t, int) or t >= 2:
                    low(t - 2, (c + 2) % 4)

            stat(0, 0)
            coef(0, 0)
            dve.wait_ge(const_in, 48)
            step(0, 0)
            step(1, 1)
            with dve.Fori(0, 3) as i:
                for c in range(4):
                    step(4 * i + c + 2, (c + 2) % 4)
            step(14, 2)
            step(15, 3, DEC)
            times_gain(16, 0, DEC)
            low(14, 2)
            low(15, 3)
            low(16, 0, DEC)

        @block.scalar
        def _(act):
            def norm(t, c, rows=P):
                r, b = slice(0, rows), c % 2
                act.wait_ge(coef_done, t + 1)
                if not isinstance(t, int) or t >= 2:
                    act.wait_ge(h_done, t - 1)
                act.activation(xn[r, b, :], x[r, c, :], ACT.Identity, bias=nmr[r, b:b + 1],
                               scale=rstd[r, b:b + 1]).then_inc(xn_done, 1)

            def high(t, c, rows=P):
                act.wait_ge(turned, t + 1)
                act.activation(hT_hi[:, :, bass.ds(t * P, rows)], tp[c][:, :, 0:rows], ACT.Copy)\
                   .then_inc(hi_done, 1)

            norm(0, 0)
            norm(1, 1)
            with act.Fori(0, 3) as i:
                for c in range(4):
                    norm(4 * i + c + 2, (c + 2) % 4)
                    high(4 * i + c, c)
            norm(14, 2)
            high(12, 0)
            norm(15, 3)
            high(13, 1)
            norm(16, 0, DEC)
            for t in (14, 15):
                high(t, t % 4)
            high(16, 0, DEC)

        @block.gpsimd
        def _(pool):
            def add_shift(t, c, rows=P):
                r, b = slice(0, rows), c % 2
                pool.wait_ge(gained, t + 1)
                if not isinstance(t, int) or t >= 2:
                    pool.wait_ge(turned, t - 1)
                    pool.wait_ge(h_out[b], t * 8 - 8 * b)
                pool.tensor_tensor(h[r, b, :], xn[r, b, :], shift[r, :], ALU.add).then_inc(h_done, 1)

            def inverse_std(t, c, rows=P):
                r, b = slice(0, rows), c % 2
                pool.wait_ge(mv_done, t + 1)
                pool.tensor_tensor(rstd[r, b:b + 1], var[r, b:b + 1], power[r, :], ALU.pow).then_inc(rstd_done, 1)

            pool.memset(power[:, :], -0.5).then_inc(aux, 1)
            pool.wait_ge(aux, 1)
            inverse_std(0, 0)
            pool.wait_ge(const_in, 48)
            for t in range(2):
                inverse_std(t + 1, t + 1)
                add_shift(t, t)
            with pool.Fori(0, 3) as i:
                for c in range(4):
                    inverse_std(4 * i + c + 3, (c + 3) % 4)
                    add_shift(4 * i + c + 2, (c + 2) % 4)
            inverse_std(15, 3)
            add_shift(14, 2)
            inverse_std(16, 0, DEC)
            add_shift(15, 3)
            add_shift(16, 0, DEC)

        @block.tensor
        def _(pe):
            def turn(t, c, rows=P):
                pe.wait_ge(h_done, t + 1)
                if not isinstance(t, int) or t >= 4:
                    pe.wait_ge(lo_done, t - 3)
                for k in range(KT):
                    last = pe.transpose(tp[c][:, k, 0:rows], h[0:rows, c % 2, k * P:(k + 1) * P],
                                        eye[0:rows, 0:rows])
                last.then_inc(turned, 1)

            pe.wait_ge(const_in, 48)
            for t in range(4):
                turn(t, t)
            with pe.Fori(1, 4) as i:
                for c in range(4):
                    turn(4 * i + c, c)
            turn(16, 0, DEC)


def forget_gates(nc, held, s, hT_hi, hT_lo, first_w, first_tile, w_f, b_f, cache_logf, ident, logf_prompt, logf_sample):
    with ExitStack() as ctx:
        sb, pb, sem = tools(nc, ctx, held, "fg")
        wf = sb("wf", [P, KT, H])
        wf_hi = sb("wf_hi", [P, KT, P], F32R)
        wf_lo = sb("wf_lo", [P, KT, P], F32R)
        bias = sb("bias", [H, 1])
        eye = sb("eye", [P, P])
        past_rows = sb("past_rows", [P, NB, H])
        logf = sb("logf", [H, T])
        cum = sb("cum", [H, T])
        cum_past = sb("cum_past", [H, PAST])
        ones = sb("ones", [H, PAST])
        hi = sb("hi", [H, T], F32R)
        lo = sb("lo", [H, T], F32R)
        logf_rows = sb("logf_rows", [SUB, T // SUB, H])
        proj = [pb(f"proj{i}") for i in range(NCH)]
        tp = pb("tp")
        tq = [pb(f"tq{i}") for i in range(2)]
        loaded, zeroed, w_hi, w_lo, proj_done = sem("loaded"), sem("zeroed"), sem("w_hi"), sem("w_lo"), sem("proj")
        z_done, soft, logf_done, summed = sem("z"), sem("soft"), sem("logf"), sem("summed")
        past_turned, past_copied, rows_turned, rows_copied = (
            sem("past_turned"), sem("past_copied"), sem("rows_turned"), sem("rows_copied"))
        past_summed, past_hi, logged = sem("past_summed"), sem("past_hi"), sem("logged")
        tile_in, tile_hi, tile_lo = sem("tile_in"), sem("tile_hi"), sem("tile_lo")
        hi_done, lo_done, out, out_ck = sem("hi"), sem("lo"), sem("out"), sem("out_ck")
        ck = s["ck"]
        parts = [(cum_past, PAST, [(0, PAST, SEQ)]), (cum, T, [(0, SEQ, 0), (SEQ, T, SEQ + PAST)])]
        full = SEQ // SUB
        rest = SEQ - full * SUB

        block = ctx.enter_context(nc.Block())

        @block.sync
        def _(sp):
            sp.dma_start(wf[:, :, :], w_f).then_inc(loaded, 16)
            sp.dma_start(bias[:, :], b_f).then_inc(loaded, 16)
            sp.dma_start(eye[:, :], ident).then_inc(loaded, 16)
            sp.dma_start(past_rows[:, :, :], cache_logf.rearrange("(b p) h -> p b h", p=P)).then_inc(loaded, 16)
            sp.dma_start(first_w[0][:, :, :], first_tile).then_inc(tile_in, 16)
            n = 0
            for i, (_, _, cols) in enumerate(parts):
                sp.wait_ge(lo_done, (1, 1 + NCH)[i])
                for a, b, at in cols:
                    sp.dma_start(ck[0, :, at:at + b - a], hi[:, a:b].bitcast(F32)).then_inc(out_ck, 16)
                    sp.dma_start(ck[1, :, at:at + b - a], lo[:, a:b].bitcast(F32)).then_inc(out_ck, 16)
                    n += 32
                sp.wait_ge(out_ck, n)
            sp.wait_ge(rows_copied, 1)
            sp.dma_start(logf_prompt[0:full * SUB, :].rearrange("(a p) h -> p a h", p=SUB),
                         logf_rows[:, 0:full, :]).then_inc(out, 16)
            sp.dma_start(logf_prompt[full * SUB:SEQ, :], logf_rows[0:rest, full, :]).then_inc(out, 16)
            sp.dma_start(logf_sample, logf_rows[rest:SUB, full, :]).then_inc(out, 16)
            sp.wait_ge(out, 48)

        @block.gpsimd
        def _(pool):
            pool.memset(wf_hi[:, :, :].bitcast(F32), 0.0).then_inc(zeroed, 1)
            pool.memset(wf_lo[:, :, :].bitcast(F32), 0.0).then_inc(zeroed, 1)
            pool.memset(ones[:, :], 1.0).then_inc(zeroed, 1)
            pool.wait_ge(tile_hi, 1)
            pool.tensor_tensor(first_w[2][:, :, :], first_w[0][:, :, :], first_w[1][:, :, :].bitcast(F32),
                               ALU.subtract).then_inc(tile_lo, 1)

        @block.vector
        def _(dve):
            dve.wait_ge(loaded, 64)
            dve.wait_ge(zeroed, 3)
            dve.tensor_copy(wf_hi[:, :, 0:H], wf[:, :, :]).then_inc(w_hi, 1)
            dve.wait_ge(w_hi, 1)
            dve.tensor_tensor(wf_lo[:, :, 0:H], wf[:, :, :], wf_hi[:, :, 0:H].bitcast(F32), ALU.subtract)\
               .then_inc(w_lo, 1)
            for q in range(4):
                dve.wait_ge(past_turned, q + 1)
                dve.tensor_copy(cum_past[:, q * 512:(q + 1) * 512], tq[q % 2][0:H, :]).then_inc(past_copied, 1)
            dve.wait_ge(past_copied, 4)
            dve.tensor_tensor_scan(cum_past[:, :], ones[:, :], cum_past[:, :], 0.0, ALU.mult, ALU.add)\
               .then_inc(past_summed, 1)
            dve.wait_ge(past_hi, 1)
            dve.scalar_tensor_tensor(out=lo[:, 0:PAST], in0=cum_past[:, :], scalar=-8.0,
                                     in1=hi[:, 0:PAST].bitcast(F32), op0=ALU.mult, op1=ALU.subtract)\
               .then_inc(lo_done, 1)

            def sums(n):
                tok = slice(n * CH, (n + 1) * CH)
                dve.wait_ge(logged, n + 1)
                dve.scalar_tensor_tensor(out=logf[:, tok], in0=logf[:, tok], scalar=0.0, in1=cum[:, tok],
                                         op0=ALU.min, op1=ALU.subtract).then_inc(logf_done, 1)
                dve.wait_ge(logf_done, n + 1)
                end = min(tok.stop, SEQ)
                before = 0.0
                if n:
                    dve.wait_ge(summed, n)
                    before = cum[:, tok.start - 1:tok.start]
                last = dve.tensor_tensor_scan(cum[:, tok.start:end], ones[:, tok.start:end], logf[:, tok.start:end],
                                              before, ALU.mult, ALU.add)
                if n == NCH - 1:
                    last = dve.tensor_tensor_scan(cum[:, SEQ:T], ones[:, 0:DEC], logf[:, SEQ:T],
                                                  cum_past[:, PAST - 1:PAST], ALU.mult, ALU.add)
                last.then_inc(summed, 1)

            def sums_low(n):
                tok = slice(n * CH, (n + 1) * CH)
                dve.wait_ge(hi_done, n + 1)
                dve.scalar_tensor_tensor(out=lo[:, tok], in0=cum[:, tok], scalar=-8.0, in1=hi[:, tok].bitcast(F32),
                                         op0=ALU.mult, op1=ALU.subtract).then_inc(lo_done, 1)

            for n in range(NCH):
                sums(n)
                if n >= 2:
                    sums_low(n - 2)
            sums_low(NCH - 2)
            sums_low(NCH - 1)
            dve.wait_ge(rows_turned, 1)
            dve.tensor_copy(logf_rows[:, :, :], tp[0:SUB, 0:T // SUB * H].rearrange("p (a h) -> p a h", h=H))\
               .then_inc(rows_copied, 1)

        @block.scalar
        def _(act):
            act.wait_ge(tile_in, 16)
            act.activation(first_w[1][:, :, :], first_w[0][:, :, :], ACT.Copy).then_inc(tile_hi, 1)

            def sums_high(n):
                tok = slice(n * CH, (n + 1) * CH)
                act.wait_ge(summed, n + 1)
                if n == 0:
                    act.wait_ge(out_ck, 32)
                act.activation(hi[:, tok], cum[:, tok], ACT.Copy, scale=-8.0).then_inc(hi_done, 1)

            for n in range(NCH):
                tok = slice(n * CH, (n + 1) * CH)
                act.wait_ge(proj_done, n + 1)
                act.activation(logf[:, tok], proj[n][0:H, 0:CH], ACT.Identity, bias=bias[:, :]).then_inc(z_done, 1)
                act.wait_ge(z_done, n + 1)
                act.activation(cum[:, tok], logf[:, tok], ACT.Abs).then_inc(soft, 1)
                act.wait_ge(soft, 2 * n + 1)
                act.activation(cum[:, tok], cum[:, tok], ACT.Exp, scale=-1.0).then_inc(soft, 1)
                if n == 2:
                    act.wait_ge(past_summed, 1)
                    act.activation(hi[:, 0:PAST], cum_past[:, :], ACT.Copy, scale=-8.0).then_inc(past_hi, 1)
            act.wait_ge(soft, 2 * NCH)
            for n in range(NCH + 2):
                if n < NCH:
                    tok = slice(n * CH, (n + 1) * CH)
                    act.activation(cum[:, tok], cum[:, tok], ACT.Ln, bias=1.0).then_inc(logged, 1)
                if n >= 2:
                    sums_high(n - 2)

        @block.tensor
        def _(pe):
            pe.wait_ge(loaded, 64)
            pe.wait_ge(w_lo, 1)
            for n in range(NCH):
                tok = slice(n * CH, (n + 1) * CH)
                project(pe, proj[n][:, 0:CH], [(wf_hi[:, k, :], wf_lo[:, k, :], hT_hi[:, k, tok], hT_lo[:, k, tok])
                                               for k in range(KT)]).then_inc(proj_done, 1)
                if n == 0:
                    for q in range(4):
                        if q >= 2:
                            pe.wait_ge(past_copied, q - 1)
                        for b in range(4):
                            last = pe.transpose(tq[q % 2][0:H, b * P:(b + 1) * P], past_rows[:, 4 * q + b, :],
                                                eye[:, :])
                        last.then_inc(past_turned, 1)
            pe.wait_ge(logf_done, NCH)
            for a in range(T // SUB):
                last = pe.transpose(tp[0:SUB, a * H:(a + 1) * H], logf[:, a * SUB:(a + 1) * SUB], eye[0:H, 0:H])
            last.then_inc(rows_turned, 1)


def project(pe, out, parts):
    for i, (w_hi, w_lo, x_hi, x_lo) in enumerate(parts):
        pe.matmul(out, w_hi, x_hi, start=(i == 0), stop=False)
        pe.matmul(out, w_hi, x_lo, start=False, stop=False)
        last = pe.matmul(out, w_lo, x_hi, start=False, stop=(i == len(parts) - 1))
    return last


def projections(nc, held, s, hT_hi, hT_lo, first_w, w_tiles, conv_w, state_conv, ident,
                k_prompt, v_prompt, k_sample, v_sample, conv_prompt, conv_sample):
    with ExitStack() as ctx:
        sb, pb, sem = tools(nc, ctx, held, "pr")
        w = [first_w[0], sb("w", [P, KT, P])]
        w_hi = [first_w[1], sb("w_hi", [P, KT, P], F32R)]
        w_lo = [first_w[2], sb("w_lo", [P, KT, P], F32R)]
        eye = sb("eye", [P, P])
        cw = sb("cw", [P, CONV // P, CW])
        GAP = SEQ + CW - 1
        U = sb("u", [P, T + 2 * (CW - 1)])
        xa = sb("xa", [P, T])
        conv = sb("conv", [P, T + CW - 1])
        full_t = sb("full_t", [P, 2, CH])
        out_a = sb("out_a", [P, 2, 512], F32R)
        out_b = sb("out_b", [P, 2, 512], F32R)
        out_c = sb("out_c", [SUB, 2, 4, P])
        bank = [pb(f"bank{i}") for i in range(NCH)]
        turn_bank = pb("turn")

        const_in = sem("const_in")
        w_in = [sem(f"w_in{i}") for i in range(2)]
        w_hi_done, w_lo_done, proj_done = sem("w_hi"), sem("w_lo"), sem("proj_done")
        bank_free = [sem(f"bank_free{i}") for i in range(NCH)]
        a_done, b_done, c_done = sem("a_done"), sem("b_done"), sem("c_done")
        a_out, b_out, c_out = ([sem(f"{x}_out{i}") for i in range(2)] for x in "abc")
        edges, state_in, conv_done, frames_out, tail_out = (
            sem("edges"), sem("state_in"), sem("conv"), sem("frames_out"), sem("tail_out"))
        full_done, gated, turned, sp_passed = sem("full"), sem("gated"), sem("turned"), sem("sp_passed")

        def toks(n):
            return slice(n * CH, (n + 1) * CH)

        def left(a, n):
            return 48 * a + 16 * (n // 2) + 16 if n % 2 == 0 else 32 * a + 16 * (n // 2) + 16

        def spans(n, shift):
            if n < NCH - 1:
                return [(slice(n * CH + shift, (n + 1) * CH + shift), slice(0, CH))]
            return [(slice(n * CH + shift, SEQ + shift), slice(0, TAIL)),
                    (slice(GAP + shift, GAP + DEC + shift), slice(TAIL, CH))]

        block = ctx.enter_context(nc.Block())

        @block.sync
        def _(sp):
            wait = settled(sp, sp_passed)
            sp.dma_start(w[1][:, :, :], w_tiles[1]).then_inc(w_in[1], 16)
            sp.sem_inc(w_in[0], 16)
            sp.dma_start(eye[:, :], ident).then_inc(const_in, 16)
            sp.dma_start(cw[:, :, :], conv_w).then_inc(const_in, 16)
            for q in (*a_out, *b_out, *c_out, tail_out):
                sp.sem_inc(q, 16)
            sp.sem_inc(frames_out, 16)

            def next_w(t, b):
                wait(w_lo_done, t + 1)
                sp.dma_start(w[b][:, :, :], w_tiles[bass.ds(t + 2, 1)].rearrange("a p k n -> (a p) k n"))\
                  .then_inc(w_in[b], 16)

            def rows_out(dst, n, a=None, t=None):
                if a is None:
                    wait(bank_free[n], t + 2)
                else:
                    wait(a_done, 5 * a + n + 1)
                sp.dma_start(dst, out_a[:, n % 2, 0:CH].bitcast(F32)).then_inc(a_out[n % 2], 16)

            def lows_out(dst, t, n, done=None):
                if done is None:
                    wait(bank_free[n], t + 2)
                else:
                    wait(b_done, done)
                sp.dma_start(dst, out_b[:, n % 2, 0:CH].bitcast(F32)).then_inc(b_out[n % 2], 16)

            def tokens_out(dst, dst_sample, cols, c, n):
                wait(c_done, 5 * c + n + 1)
                src = out_c[:, n % 2]
                at = n * CH
                if n < NCH - 1:
                    sp.dma_start(dst[at:at + CH, cols].rearrange("(a p) c -> p a c", p=SUB), src)\
                      .then_inc(c_out[n % 2], 16)
                    return
                m = TAIL // SUB
                r = TAIL - m * SUB
                sp.dma_start(dst[at:at + m * SUB, cols].rearrange("(a p) c -> p a c", p=SUB), src[:, 0:m, :])\
                  .then_inc(tail_out, 16)
                sp.dma_start(dst[at + m * SUB:SEQ, cols], src[0:r, m, :]).then_inc(tail_out, 16)
                sp.dma_start(dst_sample[:, cols], src[r:SUB, m, :]).then_inc(c_out[n % 2], 16)

            with sp.Fori(0, 4) as j:
                ch = bass.ds(j * P, P)
                wait(conv_done, 3 * j + 1)
                sp.dma_start(U[:, GAP:GAP + CW - 1], state_conv[ch, :]).then_inc(state_in, 16)
                next_w(4 * j, 0)
                next_w(4 * j + 1, 1)
                wait(bank_free[NCH - 1], 4 * j + 3)
                sp.dma_start(conv_prompt[ch, :], U[:, SEQ:SEQ + CW - 1]).then_inc(frames_out, 16)
                sp.dma_start(conv_sample[ch, :], U[:, GAP + DEC:GAP + DEC + CW - 1]).then_inc(frames_out, 16)
                next_w(4 * j + 2, 0)
                next_w(4 * j + 3, 1)
                for n in range(NCH):
                    rows_out(s["yah"][ch, toks(n)], n, a=j)
                    lows_out(s["yal"][ch, toks(n)], 0, n, 5 * j + n + 1)
            with sp.Fori(0, 4) as j:
                ch = bass.ds(j * P, P)
                next_w(16 + 2 * j, 0)
                for n in range(NCH):
                    rows_out(s["kh"][ch, toks(n)], n, a=4 + 2 * j)
                    lows_out(s["kl"][ch, toks(n)], 16 + 2 * j, n)
                    if n:
                        tokens_out(k_prompt, k_sample, ch, 2 * j, n - 1)
                tokens_out(k_prompt, k_sample, ch, 2 * j, NCH - 1)
                next_w(17 + 2 * j, 1)
                for n in range(NCH):
                    tokens_out(v_prompt, v_sample, ch, 2 * j + 1, n)
                    for name, src, done, value, gone in (
                            ("vh", out_a, a_done, 5 * (5 + 2 * j) + n + 1, a_out[n % 2]),
                            ("vl", out_b, b_done, 5 * (4 + j) + n + 1, b_out[n % 2])):
                        wait(done, value)
                        sp.dma_start(s[name][n * CH:(n + 1) * CH, ch].rearrange("(a p) c -> p a c", p=SUB),
                                     src[0:SUB, n % 2, :].bitcast(F32).rearrange("p (a c) -> p a c", a=4))\
                          .then_inc(gone, 16)
            with sp.Fori(0, 4) as j:
                ch = bass.ds(j * P, P)
                next_w(24 + 2 * j, 0)
                for n in range(NCH):
                    rows_out(s["qh"][ch, toks(n)], n, a=12 + j)
                    lows_out(s["ql"][ch, toks(n)], 24 + 2 * j, n)
                next_w(25 + 2 * j, 1)
                for n in range(NCH):
                    rows_out(s["zb"][ch, toks(n)], n, t=25 + 2 * j)
            with sp.Fori(0, 7) as j:
                for b in range(2):
                    next_w(32 + 2 * j + b, b)
                    for n in range(NCH):
                        rows_out(s["g"][bass.ds((2 * j + b) * P, P), toks(n)], n, t=32 + 2 * j + b)
            for b in range(2):
                for n in range(NCH):
                    rows_out(s["g"][(14 + b) * P:(15 + b) * P, toks(n)], n, t=46 + b)
            for q, tiles in ((a_out, 36), (b_out, 16), (c_out, 8)):
                wait(q[0], left(tiles, 0))
                wait(q[1], left(tiles, 1))
            wait(frames_out, 16 + 32 * 4)
            wait(tail_out, 16 + 32 * 8)

        @block.tensor
        def _(pe):
            def chunk(t, b, n):
                if n == 0:
                    pe.wait_ge(w_lo_done, t + 1)
                pe.wait_ge(bank_free[n], t + 1)
                project(pe, bank[n][:, 0:CH], [(w_hi[b][:, k, :], w_lo[b][:, k, :], hT_hi[:, k, toks(n)],
                                                hT_lo[:, k, toks(n)]) for k in range(KT)]).then_inc(proj_done, 1)

            def turn(j, b, n):
                if b == 0:
                    pe.wait_ge(full_done, 5 * j + n + 1)
                else:
                    pe.wait_ge(bank_free[n], 17 + 2 * j + 2)
                if (b == 0) == (n > 0):
                    pe.wait_ge(c_done, 10 * j + n if b == 0 else 10 * j + 5)
                else:
                    pe.wait_ge(b_done, 20 + 5 * j + n)
                for a in range(4):
                    last = pe.transpose(turn_bank[0:SUB, a * P:(a + 1) * P], full_t[:, n % 2, a * SUB:(a + 1) * SUB],
                                        eye[:, :])
                last.then_inc(turned, 1)

            with pe.Fori(0, 8) as i:
                for b in range(2):
                    for n in range(NCH):
                        chunk(2 * i + b, b, n)
            pe.wait_ge(const_in, 32)
            with pe.Fori(0, 4) as j:
                for b in range(2):
                    for n in range(NCH):
                        chunk(16 + 2 * j + b, b, n)
                        if n:
                            turn(j, b, n - 1)
                    turn(j, b, NCH - 1)
            with pe.Fori(0, 12) as i:
                for b in range(2):
                    for n in range(NCH):
                        chunk(24 + 2 * i + b, b, n)

        @block.gpsimd
        def _(pool):
            def low_w(t, b):
                pool.wait_ge(w_hi_done, t + 1)
                pool.tensor_tensor(w_lo[b][:, :, :], w[b][:, :, :], w_hi[b][:, :, :].bitcast(F32), ALU.subtract).then_inc(w_lo_done, 1)

            pool.sem_inc(w_lo_done, 1)
            low_w(1, 1)
            with pool.Fori(1, N_TILES // 2) as i:
                low_w(2 * i, 0)
                low_w(2 * i + 1, 1)

        @block.scalar
        def _(act):
            def high_w(t, b):
                act.wait_ge(w_in[b], 8 * t + 16 - 8 * b)
                act.wait_ge(proj_done, 5 * t - 5)
                act.activation(w_hi[b][:, :, :], w[b][:, :, :], ACT.Copy).then_inc(w_hi_done, 1)

            def through(t, n, a, func):
                act.wait_ge(proj_done, 5 * t + n + 1)
                act.wait_ge(a_out[n % 2], left(a, n))
                to = out_a[:, n % 2, 0:CH]
                if func != ACT.Copy:
                    to = to.bitcast(F32)
                return act.activation(to, bank[n][:, 0:CH], func)

            def keep_full(t, c, n, done):
                act.wait_ge(proj_done, 5 * t + n + 1)
                act.wait_ge(turned, 5 * c + n + 1 if n == 0 else 5 * c + n)
                return act.activation(full_t[:, n % 2, :], bank[n][:, 0:CH], ACT.Copy).then_inc(done, 1)

            def rows_c(c, n):
                act.wait_ge(turned, 5 * c + n + 2)
                act.wait_ge(c_out[n % 2], left(c, n))
                if n == 0:
                    act.wait_ge(tail_out, 32 * c + 16)
                return act.activation(out_c[:, n % 2], turn_bank[0:SUB, :].rearrange("p (a c) -> p a c", a=4), ACT.Copy)

            for q in bank_free:
                act.sem_inc(q, 1)
            act.sem_inc(turned, 1)
            act.sem_inc(gated, 5)
            act.sem_inc(conv_done, 1)
            act.sem_inc(w_hi_done, 1)
            act.wait_ge(w_in[1], 16)
            act.activation(w_hi[1][:, :, :], w[1][:, :, :], ACT.Copy).then_inc(w_hi_done, 1)
            with act.Fori(0, 4) as j:
                for n in range(NCH):
                    act.wait_ge(proj_done, 20 * j + n + 1)
                    act.wait_ge(gated, 5 * j + n + 1)
                    act.activation(xa[:, toks(n)], bank[n][:, 0:CH], ACT.Copy).then_inc(bank_free[n], 1)
                high_w(4 * j + 2, 0)
                high_w(4 * j + 3, 1)
                for n in range(NCH):
                    act.wait_ge(proj_done, 20 * j + 10 + n + 1)
                    act.activation(xa[:, toks(n)], bank[n][:, 0:CH], ACT.Silu).then_inc(bank_free[n], 1)
                high_w(4 * j + 4, 0)
                for n in range(NCH):
                    if n < 2:
                        act.wait_ge(bank_free[0], 4 * j + 3)
                    else:
                        act.wait_ge(b_done, 5 * j + n - 1)
                    act.wait_ge(gated, 5 * j + n + 6)
                    act.wait_ge(a_out[n % 2], left(j, n))
                    act.activation(out_a[:, n % 2, 0:CH], full_t[:, n % 2, :], ACT.Copy).then_inc(a_done, 1)
                high_w(4 * j + 5, 1)
            act.wait_ge(b_done, 20)
            with act.Fori(0, 4) as j:
                for n in range(NCH):
                    keep_full(16 + 2 * j, 2 * j, n, full_done)
                    if n < 2:
                        act.wait_ge(b_done, 5 * (4 + j))
                    else:
                        act.wait_ge(bank_free[n - 2], 18 + 2 * j)
                    through(16 + 2 * j, n, 4 + 2 * j, ACT.Copy).then_inc(a_done, 1)
                    if n:
                        rows_c(2 * j, n - 1).then_inc(c_done, 1)
                rows_c(2 * j, NCH - 1).then_inc(c_done, 1)
                high_w(18 + 2 * j, 0)
                for n in range(NCH + 1):
                    if n < NCH:
                        keep_full(17 + 2 * j, 2 * j + 1, n, bank_free[n])
                    if n:
                        rows_c(2 * j + 1, n - 1).then_inc(c_done, 1)
                        act.wait_ge(a_out[(n - 1) % 2], left(5 + 2 * j, n - 1))
                        if n < 3:
                            act.wait_ge(bank_free[5 - n], 18 + 2 * j)
                        else:
                            act.wait_ge(b_done, 5 * (4 + j) + n - 2)
                        act.activation(out_a[0:SUB, (n - 1) % 2, :], turn_bank[0:SUB, :], ACT.Copy)\
                           .then_inc(a_done, 1)
                high_w(19 + 2 * j, 1)
            with act.Fori(0, 4) as j:
                for n in range(NCH):
                    if n >= 2:
                        act.wait_ge(bank_free[n - 2], 26 + 2 * j)
                    else:
                        act.wait_ge(b_done, 40)
                        act.wait_ge(bank_free[4 - n], 24 + 2 * j)
                    through(24 + 2 * j, n, 12 + 2 * j, ACT.Copy).then_inc(a_done, 1)
                high_w(26 + 2 * j, 0)
                for n in range(NCH):
                    if n < 2:
                        act.wait_ge(bank_free[4 - n], 26 + 2 * j)
                    through(25 + 2 * j, n, 13 + 2 * j, ACT.Silu).then_inc(bank_free[n], 1)
                high_w(27 + 2 * j, 1)
            with act.Fori(0, 7) as j:
                for b in range(2):
                    for n in range(NCH):
                        through(32 + 2 * j + b, n, 20 + 2 * j + b, ACT.Sigmoid).then_inc(bank_free[n], 1)
                    high_w(34 + 2 * j + b, b)
            for b in range(2):
                for n in range(NCH):
                    through(46 + b, n, 34 + b, ACT.Sigmoid).then_inc(bank_free[n], 1)

        @block.vector
        def _(dve):
            dve.memset(U[:, 0:CW - 1], 0.0).then_inc(edges, 1)
            dve.wait_ge(edges, 1)
            dve.wait_ge(const_in, 32)

            def low(n, a, b, src, rows, width):
                dve.wait_ge(a_done, 5 * a + n + 1)
                dve.wait_ge(b_out[n % 2], left(b, n))
                return dve.tensor_tensor(out_b[0:rows, n % 2, 0:width], src,
                                         out_a[0:rows, n % 2, 0:width].bitcast(F32), ALU.subtract)

            with dve.Fori(0, 4) as j:
                t = 4 * j + 1
                dve.wait_ge(frames_out, 32 * j + 16)
                dve.wait_ge(conv_done, 3 * j + 1)
                for n in range(NCH):
                    dve.wait_ge(proj_done, 5 * t + n + 1)
                    for to, col in spans(n, CW - 1):
                        last = dve.tensor_tensor(U[:, to], bank[n][:, col], xa[:, toks(n)][:, col], ALU.mult)
                    last.then_inc(bank_free[n], 1)
                for n in range(NCH):
                    dve.wait_ge(bank_free[n], t + 2)
                dve.wait_ge(state_in, 16 * j + 16)
                dve.wait_ge(gated, 5 * j + 5)
                L = T + CW - 1
                tap = cw[:, bass.ds(j, 1), :].rearrange("p j w -> p (j w)")
                dve.tensor_scalar(conv[:, :], U[:, 0:L], tap[:, 0:1], None, ALU.mult).then_inc(conv_done, 1)
                for x in range(1, CW):
                    dve.wait_ge(conv_done, 3 * j + x + 1)
                    dve.scalar_tensor_tensor(out=conv[:, :], in0=U[:, x:x + L], scalar=tap[:, x:x + 1],
                                             in1=conv[:, :], op0=ALU.mult, op1=ALU.add).then_inc(conv_done, 1)
                dve.wait_ge(conv_done, 3 * j + CW + 1)
                for n in range(NCH + 1):
                    if n < NCH:
                        dve.wait_ge(proj_done, 5 * (t + 2) + n + 1)
                        if n >= 2:
                            dve.wait_ge(b_done, 5 * j + n - 1)
                        for to, col in spans(n, 0):
                            last = dve.tensor_tensor(full_t[:, n % 2, col], bank[n][:, col], conv[:, to], ALU.mult)
                        last.then_inc(bank_free[n], 1)
                        dve.wait_ge(bank_free[n], t + 4)
                        dve.tensor_tensor(full_t[:, n % 2, :], full_t[:, n % 2, :], xa[:, toks(n)], ALU.mult)\
                           .then_inc(gated, 1)
                    if n:
                        low(n - 1, j, j, full_t[:, (n - 1) % 2, :], P, CH).then_inc(b_done, 1)
            with dve.Fori(0, 4) as j:
                for n in range(NCH):
                    low(n, 4 + 2 * j, 4 + 2 * j, bank[n][:, 0:CH], P, CH).then_inc(bank_free[n], 1)
                for n in range(NCH):
                    low(n, 5 + 2 * j, 5 + 2 * j, turn_bank[0:SUB, :], SUB, 4 * P).then_inc(b_done, 1)
            with dve.Fori(0, 4) as j:
                for n in range(NCH):
                    low(n, 12 + j, 12 + j, bank[n][:, 0:CH], P, CH).then_inc(bank_free[n], 1)


def prompt_attention(nc, held, s, ident, causal):
    with ExitStack() as ctx:
        sb, pb, sem = tools(nc, ctx, held, "at")
        HR = HD + 4
        ks = sb("ks", [P, 2, SEQ], F32R)
        qs = sb("qs", [P, 2, SEQ], F32R)
        k2 = sb("k2", [HR, 2, SEQ], F32R)
        q2 = sb("q2", [HR, 2, SEQ], F32R)
        km = sb("km", [HR, 2, SEQ], F32R)
        qm = sb("qm", [HR, 2, SEQ], F32R)
        v_hi = sb("v_hi", [P, 2, NB, P], F32R)
        v_lo = sb("v_lo", [P, 2, NB, P], F32R)
        zb = sb("zb", [HD, 2, SEQ])
        RING = 4
        p = sb("p", [P, RING, QW])
        p_hi = sb("p_hi", [P, RING, QW], F32R)
        p_lo = sb("p_lo", [P, RING, QW], F32R)
        eye = sb("eye", [P, P])
        mask = sb("mask", [P, P])
        eye_b = sb("eye_b", [P, P], BF16)
        mask_b = sb("mask_b", [P, P], BF16)
        piece_max = sb("piece_max", [P, NB, NQ])
        row_max = sb("row_max", [P, NB])
        neg_max = sb("neg_max", [P, 2 * NB], F32R)
        neg_rows = sb("neg_rows", [2 * NB, P])
        y = sb("y", [HD + 1, 2, SEQ])
        sums = sb("sums", [P, NB])
        rcp = sb("rcp", [P, NB])
        rcp_all = sb("rcp_all", [HD, SEQ])
        y_hi = sb("y_hi", [HD, 2, QW], F32R)
        y_lo = sb("y_lo", [HD, 2, QW], F32R)
        s_bank = [pb(f"s{i}") for i in range(RING)]
        o_bank = [pb(f"o{i}") for i in range(2)]
        m_bank = [pb(f"m{i}") for i in range(2)]
        first_banks = m_bank + s_bank

        const_in, ones_set, q2_set, consts = sem("const_in"), sem("ones_set"), sem("q2_set"), sem("consts")
        main_in = [sem(f"main_in{i}") for i in range(2)]
        max_in = [sem(f"max_in{i}") for i in range(2)]
        m_in = [sem(f"m_in{i}") for i in range(2)]
        s_done = sem("s_done")
        p_done = sem("p_done")
        lo_dve, lo_pool = sem("lo_dve"), sem("lo_pool")
        pv_done = sem("pv_done")
        unit_done = sem("unit_done")
        unit_read = sem("unit_read")
        maxed, split, turned, rows_done = sem("maxed"), sem("split"), sem("turned"), sem("rows_done")
        o_read = sem("o_read")
        sum_out, sums_in, rcp_done, rcp_out, rcp_in = (
            sem("sum_out"), sem("sums_in"), sem("rcp_done"), sem("rcp_out"), sem("rcp_in"))
        zb_in = [sem(f"zb_in{i}") for i in range(2)]
        y_scaled = sem("y_scaled")
        y_gated, yh_done, yl_done = sem("y_gated"), sem("yh_done"), sem("yl_done")
        y_out = [sem(f"y_out{i}") for i in range(2)]
        sp_passed = sem("sp_passed")

        steps = [(q, kb) for q in range(NQ) for kb in range(4 * q + 4)]
        NS = len(steps)
        ends = [steps.index((q, 4 * q + 3)) for q in range(NQ)]
        units = [(i, c) for i in range(NB) for c in range(i // 4 + 1)]
        NU = len(units)
        LEAD = 3
        POOLS = 4

        def step_units(st):
            return range(min(NU, st * 4 // 3), min(NU, (st + 1) * 4 // 3))

        INVERT = 9
        FINISH = {20 + 4 * q + x + x // 2: (q, x) for x in range(3) for q in range(NQ)}
        FINISH_LOW = {st + 5: q for st, (q, x) in FINISH.items() if x == 0}
        TURN = 31

        def low_value(h, st):
            if st % POOLS == POOLS - 1:
                return lo_pool, NS // POOLS * h + st // POOLS + 1
            return lo_dve, (NS - NS // POOLS) * h + st - st // POOLS + 1

        def used(h, b, per):
            return per * (h // 2 + 1) if isinstance(h, int) else (h - b) * (per // 2) + per

        def finishing(eng):
            def scale(h, b, q):
                if q == 0:
                    eng.wait_ge(rcp_in, 16 * h + 16)
                    eng.wait_ge(zb_in[b], used(h, b, 16))
                at = y[0:HD, b, q * QW:(q + 1) * QW]
                eng.tensor_tensor(at, at, rcp_all[:, q * QW:(q + 1) * QW], ALU.mult).then_inc(y_scaled, 1)

            def gate(h, b, q):
                eng.wait_ge(y_scaled, NQ * h + q + 1)
                at = y[0:HD, b, q * QW:(q + 1) * QW]
                eng.tensor_tensor(at, at, zb[:, b, q * QW:(q + 1) * QW], ALU.mult).then_inc(y_gated, 1)

            def lower(h, b, q):
                eng.wait_ge(yh_done, NQ * h + q + 1)
                eng.tensor_tensor(y_lo[:, q % 2, :], y[0:HD, b, q * QW:(q + 1) * QW], y_hi[:, q % 2, :].bitcast(F32),
                                  ALU.subtract).then_inc(yl_done, 1)
            return scale, gate, lower

        block = ctx.enter_context(nc.Block())

        @block.sync
        def _(sp):
            wait = settled(sp, sp_passed)
            sp.dma_start(eye[:, :], ident).then_inc(const_in, 16)
            sp.dma_start(mask[:, :], causal).then_inc(const_in, 16)
            for q in y_out:
                sp.sem_inc(q, 16)

            def load_max(h, b):
                rows = bass.ds(h * HD, HD)
                for to, of in ((km[0:HD, b], s["kh"][rows, 0:SEQ]), (qm[0:HD, b], s["qh"][rows, 0:SEQ]),
                               (km[HD:HD + 2, b], s["ck"][:, bass.ds(h, 1), 0:SEQ].rearrange("a h t -> a (h t)"))):
                    sp.dma_start(to.bitcast(F32), of).then_inc(max_in[b], 16)

            def load_main(h, b):
                rows = bass.ds(h * HD, HD)
                ck = s["ck"][:, bass.ds(h, 1), 0:SEQ].rearrange("a h t -> a (h t)")
                for to, of in ((ks[0:HD, b], s["kh"][rows, 0:SEQ]), (ks[HD:P, b], s["kl"][rows, 0:SEQ]),
                               (qs[0:HD, b], s["qh"][rows, 0:SEQ]), (qs[HD:P, b], s["qh"][rows, 0:SEQ]),
                               (k2[0:HD, b], s["kh"][rows, 0:SEQ]), (k2[HD:HD + 2, b], ck),
                               (q2[0:HD, b], s["ql"][rows, 0:SEQ])):
                    sp.dma_start(to.bitcast(F32), of).then_inc(main_in[b], 16)
                for to, of in ((v_hi, s["vh"]), (v_lo, s["vl"])):
                    sp.dma_start(to[:, b, :, 0:HD].bitcast(F32), of[0:SEQ, rows].rearrange("(b p) c -> p b c", p=P))\
                      .then_inc(main_in[b], 16)

            def max_rows(h, b):
                wait(rows_done, h + 1)
                for i in range(2):
                    sp.dma_start(q2[HD + 2 + i:HD + 3 + i, b, :].bitcast(F32).rearrange("a (t q) -> a t q", q=P),
                                 neg_rows[i * NB:(i + 1) * NB, :]).then_inc(m_in[b], 16)

            def y_store(h, b, q):
                wait(yl_done, NQ * h + q + 1)
                for to, of in ((s["ybh"], y_hi), (s["ybl"], y_lo)):
                    sp.dma_start(to[bass.ds(h * HD, HD), q * QW:(q + 1) * QW], of[:, q % 2, :].bitcast(F32))\
                      .then_inc(y_out[q % 2], 16)

            def sum_store(h, b, q):
                wait(o_read, NQ * h + q + 3)
                sp.dma_start(s["sums"][bass.ds(h, 1), q * QW:(q + 1) * QW], y[HD:HD + 1, b, q * QW:(q + 1) * QW])\
                  .then_inc(sum_out, 16)

            def rcp_rows(h):
                row = s["sums"][bass.ds(h, 1), :]
                wait(sum_out, 64 * h + 64)
                sp.dma_start(sums[:, :], row.rearrange("a (p b) -> (a p) b", p=P)).then_inc(sums_in, 16)
                wait(rcp_done, h + 1)
                row = s["rcps"][bass.ds(h, 1), :]
                sp.dma_start(row.rearrange("a (p b) -> (a p) b", p=P), rcp[:, :]).then_inc(rcp_out, 16)
                wait(rcp_out, 16 * h + 16)
                sp.dma_start(rcp_all[:, :], row.broadcast_to([HD, SEQ])).then_inc(rcp_in, 16)

            def head(h, b, more=True, most=True):
                before = not isinstance(h, int) or h > 0
                if before:
                    sum_store(h - 1, 1 - b, 3)
                    rcp_rows(h - 1)
                sp.dma_start(zb[:, b], s["zb"][bass.ds(h * HD, HD), 0:SEQ]).then_inc(zb_in[b], 16)
                if more:
                    wait(pv_done, NS * h + RING)
                    load_main(h + 1, 1 - b)
                if most:
                    load_max(h + 2, b)
                for q in range(2):
                    sum_store(h, b, q)
                if before:
                    y_store(h - 1, 1 - b, 0)
                sum_store(h, b, 2)
                if before:
                    y_store(h - 1, 1 - b, 1)
                if more:
                    max_rows(h + 1, 1 - b)
                if before:
                    y_store(h - 1, 1 - b, 2)
                    y_store(h - 1, 1 - b, 3)

            load_max(0, 0)
            sp.wait_ge(q2_set, 1)
            sp.wait_ge(ones_set, 5)
            load_main(0, 0)
            load_max(1, 1)
            max_rows(0, 0)
            head(0, 0)
            head(1, 1)
            with sp.Fori(1, H // 2 - 1) as i:
                head(2 * i, 0)
                head(2 * i + 1, 1)
            head(H - 2, 0, True, False)
            head(H - 1, 1, False, False)
            sum_store(H - 1, 1, 3)
            rcp_rows(H - 1)
            for q in range(NQ):
                y_store(H - 1, 1, q)
            sp.wait_ge(y_out[0], 16 + 32 * NQ // 2 * H)
            sp.wait_ge(y_out[1], 16 + 32 * NQ // 2 * H)

        @block.tensor
        def _(pe):
            def scores(h, b, st):
                q, kb = steps[st]
                d = max(0, kb - 4 * q)
                keys, cols = slice(kb * P, (kb + 1) * P), slice(d * P, QW)
                asked = slice(q * QW + d * P, (q + 1) * QW)
                if st == 0:
                    pe.wait_ge(main_in[b], used(h, b, 144))
                    pe.wait_ge(m_in[b], used(h, b, 32))
                pe.wait_ge(p_done, NS * h + st + 1)
                bank = s_bank[st % RING]
                diagonal = kb >= 4 * q
                pe.matmul(bank[:, cols], ks[:, b, keys], qs[:, b, asked], start=True, stop=False)
                last = pe.matmul(bank[:, cols], k2[:, b, keys], q2[:, b, asked], start=False, stop=not diagonal)
                if diagonal:
                    last = pe.matmul(bank[:, d * P:(d + 1) * P], eye_b[:, :], mask_b[:, :], start=False, stop=True)
                last.then_inc(s_done, 1)

            def values(h, b, st):
                q, kb = steps[st]
                d = max(0, kb - 4 * q)
                cols = slice(d * P, QW)
                if kb == 0:
                    pe.wait_ge(o_read, NQ * h + q + 1)
                pe.wait_ge(*low_value(h, st))
                r = st % RING
                o = o_bank[q % 2][:, cols]
                pe.matmul(o, v_hi[:, b, kb, :], p_hi[:, r, cols], start=(kb == 0), stop=False)
                pe.matmul(o, v_hi[:, b, kb, :], p_lo[:, r, cols], start=False, stop=False)
                pe.matmul(o, v_lo[:, b, kb, :], p_hi[:, r, cols], start=False, stop=(kb == 4 * q + 3))\
                  .then_inc(pv_done, 1)

            def unit(h, b, u, bank, ring=2):
                i, c = units[u]
                end = min((c + 1) * QW, (i + 1) * P)
                width = end - c * QW
                if u == 0:
                    pe.wait_ge(max_in[b], used(h, b, 48))
                    if not isinstance(h, int) or h:
                        pe.wait_ge(rows_done, h)
                if not isinstance(h, int) or h or u >= ring:
                    pe.wait_ge(unit_read, NU * h + u + 3 - ring)
                last = pe.matmul(bank[:, 0:width], qm[0:HD + 2, b, i * P:(i + 1) * P], km[0:HD + 2, b, c * QW:end],
                                 start=True, stop=(c < i // 4))
                if c == i // 4:
                    last = pe.matmul(bank[:, width - P:width], mask_b[:, :], eye_b[:, :], start=False, stop=True)
                last.then_inc(unit_done, 1)

            def turn(h):
                pe.wait_ge(split, h + 1)
                pe.transpose(m_bank[0][0:2 * NB, 0:P], neg_max[:, :].bitcast(F32), eye[:, :]).then_inc(turned, 1)

            def head(h, b, more=True, ahead=True):
                for st in range(NS):
                    if st + LEAD < NS:
                        scores(h, b, st + LEAD)
                    elif ahead:
                        scores(h + 1, 1 - b, st + LEAD - NS)
                    if more:
                        for u in step_units(st):
                            unit(h + 1, 1 - b, u, m_bank[u % 2])
                        if st == TURN:
                            turn(h + 1)
                    values(h, b, st)

            pe.wait_ge(consts, 2)
            pe.wait_ge(ones_set, 5)
            pe.wait_ge(unit_read, 2)
            for u in range(NU):
                unit(0, 0, u, first_banks[u % 6], 6)
            turn(0)
            for st in range(LEAD):
                scores(0, 0, st)
            with pe.Fori(0, H // 2 - 1) as i:
                head(2 * i, 0)
                head(2 * i + 1, 1)
            head(H - 2, 0)
            head(H - 1, 1, False, False)

        @block.scalar
        def _(act):
            act.sem_inc(p_done, RING)
            act.sem_inc(pv_done, RING)
            act.sem_inc(unit_read, 2)
            act.sem_inc(o_read, 2)

            def probs(h, st):
                q, kb = steps[st]
                cols = slice(max(0, kb - 4 * q) * P, QW)
                r = st % RING
                act.wait_ge(s_done, NS * h + st + 1)
                act.wait_ge(pv_done, NS * h + st + 1)
                act.activation(p[:, r, cols], s_bank[r][:, cols], ACT.Exp, scale=SCALE)
                act.activation(p_hi[:, r, cols], s_bank[r][:, cols], ACT.Exp, scale=SCALE).then_inc(p_done, 1)

            def copy_rows(h, b):
                act.wait_ge(turned, h + 1)
                if not isinstance(h, int) or h:
                    act.wait_ge(m_in[1 - b], used(h - 1, 1 - b, 32))
                act.activation(neg_rows[:, :], m_bank[0][0:2 * NB, 0:P], ACT.Copy).then_inc(rows_done, 1)

            def head(h, b, more=True):
                for st in range(NS):
                    probs(h, st)
                    if more and st == TURN + 1:
                        copy_rows(h + 1, 1 - b)
                    if st in FINISH and FINISH[st][1] == 2 and (not isinstance(h, int) or h):
                        upper(h - 1, 1 - b, FINISH[st][0])

            def upper(h, b, q):
                act.wait_ge(y_gated, NQ * h + q + 1)
                act.wait_ge(y_out[q % 2], 64 * h + 32 * (q // 2) + 16)
                act.activation(y_hi[:, q % 2, :], y[0:HD, b, q * QW:(q + 1) * QW], ACT.Copy).then_inc(yh_done, 1)

            copy_rows(0, 0)
            head(0, 0)
            head(1, 1)
            with act.Fori(1, H // 2 - 1) as i:
                head(2 * i, 0)
                head(2 * i + 1, 1)
            head(H - 2, 0)
            head(H - 1, 1, False)
            for q in range(NQ):
                upper(H - 1, 1, q)

        @block.vector
        def _(dve):
            for t in (qm, k2):
                dve.memset(t[HD:HR, :, :].bitcast(F32), 1.0).then_inc(ones_set, 1)
            dve.wait_ge(const_in, 32)
            dve.tensor_copy(eye_b[:, :], eye[:, :]).then_inc(consts, 1)
            dve.tensor_copy(mask_b[:, :], mask[:, :]).then_inc(consts, 1)

            scale, gate, lower = finishing(dve)

            def low(h, st):
                if st % POOLS == POOLS - 1:
                    return
                q, kb = steps[st]
                cols = slice(max(0, kb - 4 * q) * P, QW)
                r = st % RING
                dve.wait_ge(p_done, NS * h + st + 1 + RING)
                dve.tensor_tensor(p_lo[:, r, cols], p[:, r, cols], p_hi[:, r, cols].bitcast(F32), ALU.subtract)\
                   .then_inc(lo_dve, 1)

            def unit(h, u, bank):
                i, c = units[u]
                width = min((c + 1) * QW, (i + 1) * P) - c * QW
                dve.wait_ge(unit_done, NU * h + u + 1)
                dve.tensor_reduce(piece_max[:, i, c:c + 1], bank[:, 0:width], AX_X, ALU.max)\
                   .then_inc(unit_read, 1)

            def whole_max(h):
                dve.wait_ge(unit_read, NU * h + NU + 2)
                if not isinstance(h, int) or h:
                    dve.wait_ge(turned, h)
                dve.tensor_reduce(row_max[:, :], piece_max[:, :, :], AX_X, ALU.max).then_inc(maxed, 1)
                dve.wait_ge(maxed, 2 * h + 1)
                dve.tensor_scalar(neg_max[:, 0:NB], row_max[:, :], -1.0, None, ALU.mult).then_inc(maxed, 1)
                dve.wait_ge(maxed, 2 * h + 2)
                dve.scalar_tensor_tensor(out=neg_max[:, NB:2 * NB], in0=row_max[:, :], scalar=-1.0,
                                         in1=neg_max[:, 0:NB].bitcast(F32), op0=ALU.mult, op1=ALU.subtract)\
                   .then_inc(split, 1)

            def take(h, b, q):
                dve.wait_ge(pv_done, NS * h + ends[q] + 1 + RING)
                if not isinstance(h, int) or h > 1:
                    dve.wait_ge(yl_done, NQ * (h - 1))
                dve.tensor_copy(y[:, b, q * QW:(q + 1) * QW], o_bank[q % 2][0:HD + 1, :]).then_inc(o_read, 1)

            def invert(h):
                dve.wait_ge(sums_in, 16 * h + 16)
                if not isinstance(h, int) or h:
                    dve.wait_ge(rcp_out, 16 * h)
                dve.reciprocal(rcp[:, :], sums[:, :]).then_inc(rcp_done, 1)

            def head(h, b, more=True):
                for st in range(NS):
                    if st + 1 < NS:
                        low(h, st + 1)
                    elif more or not b:
                        low(h + 1, 0)
                    if more:
                        for u in step_units(st):
                            unit(h + 1, u, m_bank[u % 2])
                            if u == NU - 1:
                                whole_max(h + 1)
                    if st - 2 in ends[:-1]:
                        take(h, b, ends.index(st - 2))
                    if b and st == 1:
                        take(h - 1, 1 - b, NQ - 1)
                    if st == INVERT and (not isinstance(h, int) or h):
                        invert(h - 1)
                if b:
                    take(h, b, NQ - 1)

            dve.wait_ge(ones_set, 5)
            for u in range(NU):
                unit(0, u, first_banks[u % 6])
            whole_max(0)
            low(0, 0)
            head(0, 0)
            head(1, 1)
            with dve.Fori(1, H // 2 - 1) as i:
                head(2 * i, 0)
                head(2 * i + 1, 1)
            head(H - 2, 0)
            head(H - 1, 1, False)
            invert(H - 1)
            for q in range(NQ):
                scale(H - 1, 1, q)
                gate(H - 1, 1, q)
            for q in range(NQ):
                lower(H - 1, 1, q)

        @block.gpsimd
        def _(pool):
            pool.memset(q2[HD:HR, :, :].bitcast(F32), 1.0).then_inc(q2_set, 1)
            pool.wait_ge(q2_set, 1)
            pool.memset(v_hi[:, :, :, HD:P].bitcast(F32), 1.0).then_inc(ones_set, 1)
            pool.memset(v_lo[:, :, :, HD:P].bitcast(F32), 0.0).then_inc(ones_set, 1)
            pool.memset(piece_max[:, :, :], -3e38).then_inc(ones_set, 1)

            def low(h, st):
                q, kb = steps[st]
                cols = slice(max(0, kb - 4 * q) * P, QW)
                r = st % RING
                pool.wait_ge(p_done, NS * h + st + 1 + RING)
                pool.tensor_tensor(p_lo[:, r, cols], p[:, r, cols], p_hi[:, r, cols].bitcast(F32), ALU.subtract)\
                    .then_inc(lo_pool, 1)

            scale, gate, lower = finishing(pool)

            def head(h, b):
                before = not isinstance(h, int) or h > 0
                for st in range(NS):
                    if st % POOLS == POOLS - 1:
                        low(h, st)
                    if before and st in FINISH_LOW:
                        lower(h - 1, 1 - b, FINISH_LOW[st])
                    if before and st in FINISH and FINISH[st][1] < 2:
                        (scale, gate)[FINISH[st][1]](h - 1, 1 - b, FINISH[st][0])

            head(0, 0)
            head(1, 1)
            with pool.Fori(1, H // 2) as i:
                head(2 * i, 0)
                head(2 * i + 1, 1)


def sample_attention(nc, held, s, cache_k, cache_v, ident, causal, blocks):
    with ExitStack() as ctx:
        sb, pb, sem = tools(nc, ctx, held, "sa")
        NK = NB + 1
        KEYS = PAST + DEC
        PAIRS = H // 2
        HQ = H * DEC
        PIECE = 4 * P
        NP = PAST // PIECE
        GF = ATT // 2
        WIDE = HQ + 2 * DEC
        kT_hi = sb("kT_hi", [P, PAIRS, KEYS], F32R)
        kT_lo = sb("kT_lo", [P, PAIRS, KEYS], F32R)
        v_hi = sb("v_hi", [P, NK, ATT], F32R)
        v_lo = sb("v_lo", [P, NK, ATT], F32R)
        k_rows = sb("k_rows", [P, 2, 4, ATT])
        v_rows = sb("v_rows", [P, 2, 2, ATT])
        ck = sb("ck", [2 * H, KEYS], F32R)
        pick32 = sb("pick32", [2 * H, HQ])
        pick = sb("pick", [2 * H, HQ], F32R)
        q_hi = sb("q_hi", [P, PAIRS * WIDE], F32R)
        q_lo = sb("q_lo", [P, PAIRS * WIDE], F32R)
        zb = sb("zb", [P, PAIRS, DEC])
        probs = sb("probs", [P, 2, KEYS])
        p_hi = sb("p_hi", [P, 2, 2 * HQ], F32R)
        p_lo = sb("p_lo", [P, 2, 2 * HQ], F32R)
        eye = sb("eye", [P, P])
        mask = sb("mask", [P, P])
        eye_b = sb("eye_b", [P, P], BF16)
        mask_b = sb("mask_b", [P, 4, DEC], BF16)
        piece_max = sb("piece_max", [P, 2, NP + 1])
        row_max = sb("row_max", [P, 2])
        shift = sb("shift", [P, 2])
        sums = sb("sums", [P, 2])
        rcp = sb("rcp", [P, 2])
        y_rows = sb("y_rows", [P, 2, GF])
        y = sb("y", [P, PAIRS, DEC])
        y_hi = sb("y_hi", [P, PAIRS, DEC], F32R)
        y_lo = sb("y_lo", [P, PAIRS, DEC], F32R)
        t_bank = [pb(f"t{i}") for i in range(4)]
        s_bank = [pb(f"s{i}") for i in range(2)]
        o_bank = [pb(f"o{i}") for i in range(2)]

        const_in, zeroed, consts = sem("const_in"), sem("zeroed"), sem("consts")
        k_in = [sem(f"k_in{i}") for i in range(2)]
        v_in = [sem(f"v_in{i}") for i in range(2)]
        new_in, out = sem("new_in"), sem("out")
        turned, k_hi_done, k_lo_done, v_hi_done, v_lo_done = (
            sem("turned"), sem("k_hi"), sem("k_lo"), sem("v_hi"), sem("v_lo"))
        scored, copied, piece_maxed, maxed, shifted, exped = (
            sem("scored"), sem("copied"), sem("piece_maxed"), sem("maxed"), sem("shifted"), sem("exped"))
        p_turned, ph_done, pl_done, pv_done, summed, rcp_done = (
            sem("p_turned"), sem("ph"), sem("pl"), sem("pv"), sem("summed"), sem("rcp"))
        rows_done, y_turned, y_done, yh_done, yl_done = (
            sem("rows"), sem("y_turned"), sem("y"), sem("yh"), sem("yl"))
        NEW = slice(PAST, KEYS)
        NT = NB // 2 + 1

        def piece(c):
            return slice(c * PIECE, min((c + 1) * PIECE, KEYS))

        def four(t):
            return t_bank[t % 4][:, :].rearrange("p (a c) -> p a c", a=PAIRS)

        def turned_part(n):
            return (P, 2 * HQ) if n < NT - 1 else (DEC, HQ)

        block = ctx.enter_context(nc.Block())

        @block.sync
        def _(sp):
            def load_k(c):
                sp.dma_start(k_rows[:, c % 2], cache_k[c * PIECE:(c + 1) * PIECE, :].rearrange("(b p) c -> p b c", p=P))\
                  .then_inc(k_in[c % 2], 16)

            def load_v(d):
                sp.dma_start(v_rows[:, d % 2], cache_v[d * 2 * P:(d + 1) * 2 * P, :].rearrange("(b p) c -> p b c", p=P))\
                  .then_inc(v_in[d % 2], 16)

            sp.dma_start(eye[:, :], ident).then_inc(const_in, 16)
            load_k(0)
            load_v(0)
            load_v(1)
            sp.dma_start(mask[:, :], causal).then_inc(const_in, 16)
            sp.dma_start(pick32[:, :], blocks).then_inc(const_in, 16)
            sp.dma_start(zb[:, :, :], s["zb"][:, SEQ:T].rearrange("(a p) q -> p a q", p=P)).then_inc(const_in, 16)
            sp.wait_ge(zeroed, 2)
            for to, of in ((q_hi, s["qh"]), (q_lo, s["ql"])):
                for i in range(2):
                    sp.dma_start(to[i * HD:(i + 1) * HD, :].rearrange("p (a x) -> p a x", a=PAIRS)
                                 [:, :, i * DEC:(i + 1) * DEC].bitcast(F32),
                                 of[:, SEQ:T].rearrange("(a i p) q -> i p a q", i=2, p=HD)[i]).then_inc(new_in, 16)
            for to, of in ((kT_hi, s["kh"]), (kT_lo, s["kl"])):
                sp.dma_start(to[:, :, NEW].bitcast(F32), of[:, SEQ:T].rearrange("(a p) q -> p a q", p=P)).then_inc(new_in, 16)
            for to, of in ((v_hi, s["vh"]), (v_lo, s["vl"])):
                sp.dma_start(to[0:DEC, NB, :].bitcast(F32), of[SEQ:T, :]).then_inc(new_in, 16)
            for i in range(2):
                sp.dma_start(ck[i * H:(i + 1) * H, :].bitcast(F32), s["ck"][i, :, SEQ:CKW]).then_inc(new_in, 16)
            load_k(1)
            for d in range(2, 2 * NP):
                if d % 2 == 0 and d // 2 + 1 < NP:
                    sp.wait_ge(turned, 4 * (d // 2))
                    load_k(d // 2 + 1)
                sp.wait_ge(v_lo_done, d - 1)
                load_v(d)
            sp.wait_ge(yl_done, 1)
            for to, of in ((s["ybh"], y_hi), (s["ybl"], y_lo)):
                sp.dma_start(to[:, SEQ:T].rearrange("(a p) q -> p a q", p=P), of[:, :, :].bitcast(F32)).then_inc(out, 16)
            sp.wait_ge(out, 32)

        @block.gpsimd
        def _(pool):
            pool.memset(q_hi[:, :].bitcast(F32), 0.0).then_inc(zeroed, 1)
            pool.memset(q_lo[:, :].bitcast(F32), 0.0).then_inc(zeroed, 1)
            for d in range(2 * NP):
                pool.wait_ge(v_hi_done, d + 1)
                two = slice(2 * d, 2 * d + 2)
                pool.tensor_tensor(v_lo[:, two, :], v_rows[:, d % 2], v_hi[:, two, :].bitcast(F32),
                                   ALU.subtract).then_inc(v_lo_done, 1)

        @block.scalar
        def _(act):
            def copy_scores(c):
                for g in range(2):
                    keys = piece(c)
                    act.wait_ge(scored, 2 * c + g + 1)
                    act.activation(probs[:, g, keys], s_bank[g][:, 0:keys.stop - keys.start], ACT.Copy)\
                       .then_inc(copied, 1)

            def exps(c):
                for g in range(2):
                    act.activation(probs[:, g, piece(c)], probs[:, g, piece(c)], ACT.Exp, scale=SCALE,
                                   bias=shift[:, g:g + 1]).then_inc(exped, 1)

            def upper(n):
                rows, cols = turned_part(n)
                act.wait_ge(p_turned, n + 1)
                if n >= 2:
                    act.wait_ge(pv_done, n - 1)
                act.activation(p_hi[0:rows, n % 2, 0:cols], t_bank[n % 4][0:rows, 0:cols], ACT.Copy)\
                   .then_inc(ph_done, 1)

            for c in range(NP):
                for t in range(4 * c, 4 * c + 4):
                    act.wait_ge(turned, t + 1)
                    act.activation(kT_hi[:, :, t * P:(t + 1) * P], four(t), ACT.Copy).then_inc(k_hi_done, 1)
                for d in range(2 * c, 2 * c + 2):
                    act.wait_ge(v_in[d % 2], 16 * (d // 2) + 16)
                    act.activation(v_hi[:, 2 * d:2 * d + 2, :], v_rows[:, d % 2], ACT.Copy).then_inc(v_hi_done, 1)
                if c:
                    copy_scores(c - 1)
            copy_scores(NP - 1)
            copy_scores(NP)
            act.wait_ge(copied, 2 * NP + 2)
            act.wait_ge(shifted, 1)
            exps(0)
            for c in range(NP):
                exps(c + 1)
                upper(2 * c)
                upper(2 * c + 1)
            upper(NT - 1)
            act.wait_ge(y_done, 4)
            act.activation(y_hi[:, :, :], y[:, :, :], ACT.Copy).then_inc(yh_done, 1)

        @block.vector
        def _(dve):
            dve.wait_ge(const_in, 64)
            dve.tensor_copy(pick[:, :], pick32[:, :]).then_inc(consts, 1)
            dve.tensor_copy(eye_b[:, :], eye[:, :]).then_inc(consts, 1)
            for h in range(4):
                dve.tensor_copy(mask_b[:, h, :], mask[:, 0:DEC]).then_inc(consts, 1)

            def max_scores(c):
                for g in range(2):
                    keys = piece(c)
                    dve.wait_ge(copied, 2 * c + g + 1)
                    dve.tensor_reduce(piece_max[:, g, c:c + 1], probs[:, g, keys], AX_X, ALU.max)\
                       .then_inc(piece_maxed, 1)

            def lower(n):
                rows, cols = turned_part(n)
                dve.wait_ge(ph_done, n + 1)
                dve.tensor_tensor(p_lo[0:rows, n % 2, 0:cols], t_bank[n % 4][0:rows, 0:cols],
                                  p_hi[0:rows, n % 2, 0:cols].bitcast(F32), ALU.subtract).then_inc(pl_done, 1)

            for c in range(NP):
                for t in range(4 * c, 4 * c + 4):
                    dve.wait_ge(k_hi_done, t + 1)
                    at = slice(t * P, (t + 1) * P)
                    dve.tensor_tensor(kT_lo[:, :, at], four(t), kT_hi[:, :, at].bitcast(F32), ALU.subtract)\
                       .then_inc(k_lo_done, 1)
                if c:
                    max_scores(c - 1)
            max_scores(NP - 1)
            max_scores(NP)
            dve.wait_ge(piece_maxed, 2 * NP + 2)
            dve.tensor_reduce(row_max[:, :], piece_max[:, :, :], AX_X, ALU.max).then_inc(maxed, 1)
            dve.wait_ge(maxed, 1)
            dve.tensor_scalar(shift[:, :], row_max[:, :], -SCALE, None, ALU.mult).then_inc(shifted, 1)
            for n in range(NT):
                lower(n)
                if n >= NT - 3 and n < NT - 1:
                    g = n - (NT - 3)
                    dve.wait_ge(exped, 2 * NP + 2)
                    dve.tensor_reduce(sums[:, g:g + 1], probs[:, g, :], AX_X, ALU.add).then_inc(summed, 1)
            dve.wait_ge(summed, 2)
            dve.reciprocal(rcp[:, :], sums[:, :]).then_inc(rcp_done, 1)
            dve.wait_ge(rcp_done, 1)
            dve.wait_ge(pv_done, NT)
            for g in range(2):
                dve.tensor_scalar(y_rows[:, g, :], o_bank[g][:, 0:GF], rcp[:, g:g + 1], None, ALU.mult)\
                   .then_inc(rows_done, 1)
            dve.wait_ge(y_turned, 1)
            for i in range(2):
                rows = slice(i * HD, (i + 1) * HD)
                for a in range(2):
                    own = slice((2 * a + i) * DEC, (2 * a + i + 1) * DEC)
                    o = s_bank[0][rows, :].rearrange("p (g a c) -> p g a c", g=2, a=2)[:, :, a, own]
                    pair = y[rows, :, :].rearrange("p (g a) q -> p g a q", a=2)[:, :, a, :]
                    gate = zb[rows, :, :].rearrange("p (g a) q -> p g a q", a=2)[:, :, a, :]
                    dve.tensor_tensor(pair, o, gate, ALU.mult).then_inc(y_done, 1)
            dve.wait_ge(yh_done, 1)
            dve.tensor_tensor(y_lo[:, :, :], y[:, :, :], y_hi[:, :, :].bitcast(F32), ALU.subtract).then_inc(yl_done, 1)

        @block.tensor
        def _(pe):
            def scores(c):
                pe.wait_ge(k_lo_done, min(4 * c + 4, NB))
                keys = piece(c)
                width = keys.stop - keys.start
                for g in range(2):
                    rows = slice(g * P, (g + 1) * P)
                    if c:
                        pe.wait_ge(copied, 2 * c + g - 1)
                    to = s_bank[g][:, 0:width]
                    pe.matmul(to, pick[:, rows], ck[:, keys], start=True, stop=False)
                    for a in (2 * g, 2 * g + 1):
                        own = slice(a * HQ + g * P, a * HQ + (g + 1) * P)
                        for x, k in ((q_hi, kT_hi), (q_lo, kT_hi), (q_hi, kT_lo)):
                            last = pe.matmul(to, x[:, own], k[:, a, keys], start=False,
                                             stop=(c < NP and a == 2 * g + 1 and k is kT_lo))
                    if c == NP:
                        last = pe.matmul(to, mask_b[:, :, :].rearrange("p h q -> p (h q)"), eye_b[:, 0:DEC],
                                         start=False, stop=True)
                    last.then_inc(scored, 1)

            def turn(n):
                pe.wait_ge(exped, 2 * (n // 2) + 2)
                if n >= 4:
                    pe.wait_ge(pl_done, n - 3)
                rows = turned_part(n)[0]
                for kb in range(2 * n, min(2 * n + 2, NK)):
                    for g in range(2):
                        at = (kb % 2) * HQ + g * P
                        last = pe.transpose(t_bank[n % 4][0:rows, at:at + P], probs[:, g, kb * P:kb * P + rows],
                                            eye[:, :])
                last.then_inc(p_turned, 1)

            def values(n):
                pe.wait_ge(pl_done, n + 1)
                if n < NT - 1:
                    pe.wait_ge(v_lo_done, n + 1)
                rows = turned_part(n)[0]
                for kb in range(2 * n, min(2 * n + 2, NK)):
                    for g in range(2):
                        own = slice((kb % 2) * HQ + g * P, (kb % 2) * HQ + (g + 1) * P)
                        feat = slice(g * GF, (g + 1) * GF)
                        for i, (x, v) in enumerate(((p_hi, v_hi), (p_lo, v_hi), (p_hi, v_lo))):
                            last = pe.matmul(o_bank[g][:, 0:GF], x[0:rows, n % 2, own], v[0:rows, kb, feat],
                                             start=(kb == 0 and i == 0), stop=(kb == NK - 1 and i == 2))
                last.then_inc(pv_done, 1)

            pe.wait_ge(const_in, 64)
            for c in range(NP):
                pe.wait_ge(k_in[c % 2], 16 * (c // 2) + 16)
                for t in range(4 * c, 4 * c + 4):
                    if t >= 4:
                        pe.wait_ge(k_lo_done, t - 3)
                    for a in range(PAIRS):
                        last = pe.transpose(t_bank[t % 4][:, a * P:(a + 1) * P],
                                            k_rows[:, c % 2, t % 4, a * P:(a + 1) * P], eye[:, :])
                    last.then_inc(turned, 1)
                if c == 0:
                    pe.wait_ge(consts, 6)
                    pe.wait_ge(new_in, 16 * 10)
                else:
                    scores(c - 1)
            scores(NP - 1)
            scores(NP)
            turn(0)
            turn(1)
            for n in range(NT):
                if n + 2 < NT:
                    turn(n + 2)
                values(n)
            pe.wait_ge(rows_done, 2)
            for g in range(2):
                for a in range(2):
                    at = (2 * g + a) * P
                    last = pe.transpose(s_bank[0][:, at:at + P], y_rows[:, g, a * P:(a + 1) * P], eye[:, :])
            last.then_inc(y_turned, 1)


def merge(nc, held, s, wpa_tiles, wpb_tiles):
    with ExitStack() as ctx:
        sb, pb, sem = tools(nc, ctx, held, "mg")
        YT = CONV // P
        names = ("yah", "yal", "ybh", "ybl")
        ys = {n: sb(n, [P, YT, T], F32R) for n in names}
        w = sb("w", [P, 2, 2 * YT, P])
        w_hi = sb("w_hi", [P, 4, 2 * YT, P], F32R)
        w_lo = sb("w_lo", [P, 4, 2 * YT, P], F32R)
        gates = sb("gates", [P, 4, 2, CH])
        part = sb("part", [P, 2, 2, CH])
        mixed = sb("mixed", [P, 2, CH])
        banks = [[pb(f"b{i}{x}") for x in "ab"] for i in range(4)]
        y_in = [sem(f"y_in{n}") for n in range(NCH)]
        w_in = [sem(f"w_in{i}") for i in range(2)]
        g_in = [sem(f"g_in{i}") for i in range(4)]
        m_out = [sem(f"m_out{i}") for i in range(2)]
        w_hi_done, w_lo_done, proj_done = sem("w_hi"), sem("w_lo"), sem("proj")
        gated = sem("gated")
        added = sem("added")
        NT = D // P // 4
        IT = 4 * NCH
        items = [(n, b) for n in range(NCH) for b in range(4)]

        block = ctx.enter_context(nc.Block())

        @block.sync
        def _(sp):
            for q in m_out:
                sp.sem_inc(q, 16)

            def load_w(t, b):
                for x, tiles in enumerate((wpa_tiles, wpb_tiles)):
                    sp.dma_start(w[:, b % 2, x * YT:(x + 1) * YT], tiles[4 * t + b]).then_inc(w_in[b % 2], 16)

            def load_y(n):
                tok = slice(n * CH, (n + 1) * CH)
                for name in names:
                    sp.dma_start(ys[name][:, :, tok].bitcast(F32), s[name][:, tok].rearrange("(k p) t -> p k t", p=P))\
                      .then_inc(y_in[n], 16)

            def load_gates(t, n, b):
                own = slice((4 * t + b) * P, (4 * t + b + 1) * P)
                sp.dma_start(gates[:, b], s["g"].rearrange("(x r) t -> r x t", x=2)[own, :, n * CH:(n + 1) * CH])\
                  .then_inc(g_in[b], 16)

            load_w(0, 0)
            load_y(0)
            load_w(0, 1)
            for b in range(4):
                load_gates(0, 0, b)
            for b in range(2, 4):
                sp.wait_ge(w_lo_done, b - 1)
                load_w(0, b)
            load_y(1)
            load_y(2)
            for t in range(NT):
                for n, b in items:
                    c = IT * t + 4 * n + b
                    sp.wait_ge(gated, c + 5)
                    if n < NCH - 1:
                        load_gates(t, n + 1, b)
                    elif t + 1 < NT:
                        load_gates(t + 1, 0, b)
                    if t == 0 and b == 3 and n + 3 < NCH:
                        load_y(n + 3)
                    sp.wait_ge(added, c + 3)
                    sp.dma_start(s["mixed"][(4 * t + b) * P:(4 * t + b + 1) * P, n * CH:(n + 1) * CH], mixed[:, b % 2])\
                      .then_inc(m_out[b % 2], 16)
                    if t + 1 < NT and (n, b // 2) in ((1, 0), (NCH - 1, 1)):
                        sp.wait_ge(w_lo_done, 4 * (t + 1) + b - 1)
                        load_w(t + 1, b)
            for q in m_out:
                sp.wait_ge(q, 16 + 16 * NT * IT // 2)

        @block.scalar
        def _(act):
            act.sem_inc(gated, 4)
            act.sem_inc(added, 2)
            for t in range(NT):
                for b in range(4):
                    act.wait_ge(w_in[b % 2], 32 * (2 * t + b // 2) + 32)
                    if t:
                        act.wait_ge(proj_done, IT * t - 3 + b)
                    act.activation(w_hi[:, b], w[:, b % 2], ACT.Copy).then_inc(w_hi_done, 1)

        @block.gpsimd
        def _(pool):
            def low_w(t, b):
                pool.wait_ge(w_hi_done, 4 * t + b + 1)
                pool.tensor_tensor(w_lo[:, b], w[:, b % 2], w_hi[:, b].bitcast(F32), ALU.subtract)\
                    .then_inc(w_lo_done, 1)

            for b in range(4):
                low_w(0, b)
            for t in range(NT):
                for n, b in items:
                    c = IT * t + 4 * n + b
                    pool.wait_ge(gated, c + 5)
                    pool.wait_ge(m_out[b % 2], 16 * (c // 2) + 16)
                    pool.tensor_tensor(mixed[:, b % 2], part[:, b % 2, 0], part[:, b % 2, 1], ALU.add)\
                        .then_inc(added, 1)
                    if n == NCH - 1 and t + 1 < NT:
                        low_w(t + 1, b)

        @block.vector
        def _(dve):
            with dve.Fori(0, NT) as t:
                for n, b in items:
                    c = IT * t + 4 * n + b
                    dve.wait_ge(proj_done, c + 1)
                    dve.wait_ge(g_in[b], 16 * (NCH * t + n) + 16)
                    dve.wait_ge(added, c + 1)
                    for x in range(2):
                        last = dve.tensor_tensor(part[:, b % 2, x], banks[b][x][:, 0:CH], gates[:, b, x], ALU.mult)
                    last.then_inc(gated, 1)

        @block.tensor
        def _(pe):
            with pe.Fori(0, NT) as t:
                for n, b in items:
                    c = IT * t + 4 * n + b
                    tok = slice(n * CH, (n + 1) * CH)
                    if n == 0:
                        pe.wait_ge(w_lo_done, 4 * t + b + 1)
                    pe.wait_ge(y_in[n], 64)
                    pe.wait_ge(gated, c + 1)
                    for x, (hi, lo) in enumerate((("yah", "yal"), ("ybh", "ybl"))):
                        last = project(pe, banks[b][x][:, 0:CH],
                                       [(w_hi[:, b, x * YT + k, :], w_lo[:, b, x * YT + k, :],
                                         ys[hi][:, k, tok], ys[lo][:, k, tok]) for k in range(YT)])
                    last.then_inc(proj_done, 1)


def output_norm(nc, held, s, w_out, ln_out, y_prompt, y_sample):
    with ExitStack() as ctx:
        sb, pb, sem = tools(nc, ctx, held, "ln1")
        w = sb("w", [P, KT, D])
        w_hi = sb("w_hi", [P, KT, D], F32R)
        w_lo = sb("w_lo", [P, KT, D], F32R)
        m = [sb(f"m{i}", [P, KT, P]) for i in range(2)]
        m_hi = [sb(f"m_hi{i}", [P, KT, P], F32R) for i in range(4)]
        m_lo = [sb(f"m_lo{i}", [P, KT, P], F32R) for i in range(4)]
        h = sb("h", [P, 2, D])
        y = sb("y", [P, 2, D])
        gain = sb("gain", [P, D])
        shift = sb("shift", [P, D])
        stats = sb("stats", [P, 2, 12])
        mv = sb("mv", [P, 2, 2])
        var = sb("var", [P, 2])
        rstd = sb("rstd", [P, 2])
        nmr = sb("nmr", [P, 2])
        power = sb("power", [P, 1])
        first_banks = [pb(f"f{i}", (P, D)) for i in range(2)]
        banks = [pb(f"b{i}", (P, D)) for i in range(2)]
        const_in, w_in, aux = sem("const_in"), [sem(f"w_in{k}") for k in range(KT)], sem("aux")
        m_in = [sem(f"m_in{i}") for i in range(2)]
        h_in = [sem(f"h_in{i}") for i in range(2)]
        y_out = [sem(f"y_out{i}") for i in range(2)]
        w_hi_done, w_lo_done, m_hi_done, m_lo_done, proj_done = (
            sem("w_hi"), sem("w_lo"), sem("m_hi"), sem("m_lo"), sem("proj"))
        summed, stats_done, aggr_done, mv_done, rstd_done, coef_done, yn_done, gained, y_done, passed, sp_passed = (
            sem(x) for x in ("summed", "stats", "aggr", "mv", "rstd", "coef", "yn", "gained", "y", "passed",
                             "sp_passed"))
        N = NB + 1

        block = ctx.enter_context(nc.Block())

        @block.sync
        def _(sp):
            wait = settled(sp, sp_passed)

            def load(t, b, rows):
                sp.dma_start(m[b][:, :, 0:rows], s["mixed"][:, bass.ds(t * P, rows)].rearrange("(k p) t -> p k t", p=P))\
                  .then_inc(m_in[b], 16)

            def load_h(t, b, rows):
                sp.dma_start(h[0:rows, b], s["h"][bass.ds(t * P, rows), :]).then_inc(h_in[b], 16)

            def store(t, b, rows):
                wait(y_done, t + 1)
                to = y_sample if rows == DEC else y_prompt[bass.ds(t * P, P), :]
                sp.dma_start(to, y[0:rows, b]).then_inc(y_out[b], 16)

            load(0, 0, P)
            load(1, 1, P)
            for k in range(KT):
                sp.dma_start(w[:, k], w_out[k * P:(k + 1) * P, :]).then_inc(w_in[k], 16)
            load_h(0, 0, P)
            load_h(1, 1, P)
            sp.dma_start(gain[:, :], ln_out[0:1, :].broadcast_to([P, D])).then_inc(const_in, 16)
            sp.dma_start(shift[:, :], ln_out[1:2, :].broadcast_to([P, D])).then_inc(const_in, 16)

            def turn(t, b, rows=P, m_rows=0, h_rows=0):
                if m_rows:
                    wait(m_lo_done, t + 3)
                    load(t + 4, b, m_rows)
                if h_rows:
                    wait(summed, t + 1)
                    load_h(t + 2, b, h_rows)
                store(t, b, rows)

            for t in range(2):
                wait(m_lo_done, t + 1)
                load(t + 2, t, P)
            with sp.Fori(0, 6) as i:
                turn(2 * i, 0, P, P, P)
                turn(2 * i + 1, 1, P, P, P)
            turn(12, 0, P, DEC, P)
            turn(13, 1, P, 0, P)
            turn(14, 0, P, 0, DEC)
            turn(15, 1)
            turn(16, 0, DEC)
            sp.wait_ge(y_out[0], 16 * 9)
            sp.wait_ge(y_out[1], 16 * 8)

        @block.tensor
        def _(pe):
            def tile(t, b):
                pe.wait_ge(m_lo_done, t + 1)
                if not isinstance(t, int) or t >= 4:
                    pe.wait_ge(summed, t - 1)
                for half in range(2):
                    for k in range(KT):
                        last = piece(banks[b], 2 + b, half, k)
                last.then_inc(proj_done, 1)

            def piece(bank, slot, half, k):
                cols = slice(half * 512, (half + 1) * 512)
                to = bank[:, cols]
                pe.matmul(to, m_hi[slot][:, k, :], w_hi[:, k, cols], start=(k == 0), stop=False)
                pe.matmul(to, m_hi[slot][:, k, :], w_lo[:, k, cols], start=False, stop=False)
                return pe.matmul(to, m_lo[slot][:, k, :], w_hi[:, k, cols], start=False, stop=(k == KT - 1))

            pe.wait_ge(m_lo_done, 2)
            for k in range(KT):
                pe.wait_ge(w_lo_done, k + 1)
                for b in range(2):
                    for half in range(2):
                        last = piece(first_banks[b], b, half, k)
                    if k == KT - 1:
                        last.then_inc(proj_done, 1)
            tile(2, 0)
            tile(3, 1)
            with pe.Fori(2, 8) as i:
                tile(2 * i, 0)
                tile(2 * i + 1, 1)
            tile(16, 0)

        @block.scalar
        def _(act):
            def high(t, b, rows, first=False):
                act.wait_ge(m_in[b], 8 * t + 16 - 8 * b)
                if not isinstance(t, int) or t >= 4:
                    act.wait_ge(proj_done, t - 1)
                act.activation(m_hi[b if first else 2 + b][:, :, 0:rows], m[b][:, :, 0:rows], ACT.Copy).then_inc(m_hi_done, 1)

            def norm(t, b, rows):
                act.wait_ge(coef_done, t + 1)
                act.activation(y[0:rows, b], y[0:rows, b], ACT.Identity, bias=nmr[0:rows, b:b + 1],
                               scale=rstd[0:rows, b:b + 1]).then_inc(yn_done, 1)

            high(0, 0, P, True)
            high(1, 1, P, True)
            for k in range(KT):
                act.wait_ge(w_in[k], 16)
                act.activation(w_hi[:, k], w[:, k], ACT.Copy).then_inc(w_hi_done, 1)
            high(2, 0, P)
            high(3, 1, P)
            norm(0, 0, P)
            norm(1, 1, P)
            with act.Fori(1, 7) as i:
                high(2 * i + 2, 0, P)
                norm(2 * i, 0, P)
                high(2 * i + 3, 1, P)
                norm(2 * i + 1, 1, P)
            high(16, 0, DEC)
            norm(14, 0, P)
            norm(15, 1, P)
            norm(16, 0, DEC)

        @block.vector
        def _(dve):
            def low(t, b, rows):
                slot = b if isinstance(t, int) and t < 2 else 2 + b
                dve.wait_ge(m_hi_done, t + 1)
                dve.tensor_tensor(m_lo[slot][:, :, 0:rows], m[b][:, :, 0:rows], m_hi[slot][:, :, 0:rows].bitcast(F32),
                                  ALU.subtract).then_inc(m_lo_done, 1)

            def stat(t, b, rows, first=False):
                r = slice(0, rows)
                dve.wait_ge(proj_done, t + 1)
                dve.wait_ge(h_in[b], 8 * t + 16 - 8 * b)
                if not first:
                    dve.wait_ge(y_out[b], 8 * t - 8 * b)
                dve.scalar_tensor_tensor(out=y[r, b], in0=h[r, b], scalar=ALPHA, in1=(first_banks if first else banks)[b][r, :],
                                         op0=ALU.mult, op1=ALU.add).then_inc(summed, 1)
                dve.wait_ge(summed, t + 1)
                dve.bn_stats(stats[r, b, 0:6], y[r, b, 0:512])
                dve.bn_stats(stats[r, b, 6:12], y[r, b, 512:1024]).then_inc(stats_done, 1)
                dve.wait_ge(stats_done, t + 1)
                dve.sem_inc(passed, 1)
                dve.bn_aggr(mv[r, b, :], stats[r, b, :]).then_inc(aggr_done, 1)
                dve.wait_ge(aggr_done, t + 1)
                dve.tensor_scalar(var[r, b:b + 1], mv[r, b, 1:2], EPS, None, ALU.add).then_inc(mv_done, 1)
                dve.wait_ge(rstd_done, t + 1)
                dve.tensor_scalar(nmr[r, b:b + 1], mv[r, b, 0:1], rstd[r, b:b + 1], -1.0, ALU.mult, ALU.mult)\
                   .then_inc(coef_done, 1)

            def gained_(t, b, rows):
                r = slice(0, rows)
                dve.wait_ge(yn_done, t + 1)
                dve.tensor_tensor(y[r, b], y[r, b], gain[r, :], ALU.mult).then_inc(gained, 1)

            low(0, 0, P)
            low(1, 1, P)
            for k in range(KT):
                dve.wait_ge(w_hi_done, k + 1)
                dve.tensor_tensor(w_lo[:, k], w[:, k], w_hi[:, k].bitcast(F32), ALU.subtract).then_inc(w_lo_done, 1)
            low(2, 0, P)
            low(3, 1, P)
            dve.wait_ge(const_in, 32)
            for t in range(2):
                stat(t, t, P, True)
                gained_(t, t, P)
            with dve.Fori(1, 7) as i:
                for b in range(2):
                    stat(2 * i + b, b, P)
                    low(2 * i + b + 2, b, P)
                    gained_(2 * i + b, b, P)
            stat(14, 0, P)
            low(16, 0, DEC)
            gained_(14, 0, P)
            stat(15, 1, P)
            gained_(15, 1, P)
            stat(16, 0, DEC)
            gained_(16, 0, DEC)
            dve.wait_ge(gained, 17)
            dve.wait_ge(y_done, 16)
            dve.tensor_tensor(y[0:DEC, 0], y[0:DEC, 0], shift[0:DEC, :], ALU.add).then_inc(y_done, 1)

        @block.gpsimd
        def _(pool):
            def tile(t, b, rows):
                r = slice(0, rows)
                pool.wait_ge(mv_done, t + 1)
                pool.tensor_tensor(rstd[r, b:b + 1], var[r, b:b + 1], power[r, :], ALU.pow).then_inc(rstd_done, 1)
                if rows == DEC:
                    return
                pool.wait_ge(gained, t + 1)
                pool.tensor_tensor(y[r, b], y[r, b], shift[r, :], ALU.add).then_inc(y_done, 1)

            pool.memset(power[:, :], -0.5).then_inc(aux, 1)
            pool.wait_ge(aux, 1)
            pool.wait_ge(const_in, 32)
            with pool.Fori(0, 8) as i:
                tile(2 * i, 0, P)
                tile(2 * i + 1, 1, P)
            tile(16, 0, DEC)


def kernel(**inputs):
    import numpy as np
    import concourse.bacc as bacc
    from concourse.bass_utils import run_bass_kernel_spmd

    a = {k: np.asarray(v) for k, v in inputs.items()}
    w = a["w_in"][0]
    xa, b, c, za, q, k, v, f, zb, g = (0, 512, 1024, 1536, 2048, 2560, 3072, 3584, 3592, 4104)
    at = [x + P * j for j in range(4) for x in (xa, c, za, b)]
    at += [x + P * j for j in range(4) for x in (k, v)] + [x + P * j for j in range(4) for x in (q, zb)]
    at += [g + P * i for i in range(2 * D // P)]

    def tiles(m, starts):
        return np.ascontiguousarray(np.stack([m[:, x:x + P].reshape(-1, P, P).transpose(1, 0, 2) for x in starts]))

    every = range(0, D, P)
    feed = dict(
        x_prompt=a["x_prompt"][0], x_sample=a["x_sample"][0],
        cache_k=a["cache_k"][0, 0].reshape(PAST, ATT), cache_v=a["cache_v"][0, 0].reshape(PAST, ATT),
        cache_logf=a["cache_logf"][0, 0], state_conv=a["state_conv"][0, 0].T,
        ln_in=np.stack([a["ln_in_g"], a["ln_in_b"]]), w_tiles=tiles(w, at),
        w_f=w[:, f:f + H].reshape(KT, P, H).transpose(1, 0, 2), b_f=a["b_f"][0].reshape(H, 1),
        conv_w=a["conv_w"][0].reshape(CW, CONV // P, P).transpose(2, 1, 0), wpa_tiles=tiles(a["w_proj_a"][0], every), wpb_tiles=tiles(a["w_proj_b"][0], every),
        w_out=a["w_out"][0], ln_out=np.stack([a["ln_g"][0], a["ln_b"][0]]),
        ident=np.eye(P, dtype=np.float32), causal=np.tril(np.full((P, P), MASKED, np.float32), -1),
        blocks=np.tile(np.repeat(np.eye(H, dtype=np.float32), DEC, axis=1), (2, 1)),
    )
    feed = {n: np.ascontiguousarray(x) for n, x in feed.items()}
    shapes = dict(
        y_prompt=(SEQ, D), y_sample=(DEC, D), k_prompt=(SEQ, ATT), v_prompt=(SEQ, ATT), logf_prompt=(SEQ, H),
        conv_prompt=(CONV, CW - 1), k_sample=(DEC, ATT), v_sample=(DEC, ATT), logf_sample=(DEC, H),
        conv_sample=(CONV, CW - 1))
    nc = bacc.Bacc("TRN2", target_bir_lowering=False, num_devices=1)
    args = {n: nc.dram_tensor(n, x.shape, mybir.dt.from_np(x.dtype), kind="ExternalInput").ap()
            for n, x in feed.items()}
    args |= {n: nc.dram_tensor(n, x, F32, kind="ExternalOutput").ap() for n, x in shapes.items()}
    build(nc, **args)
    r = run_bass_kernel_spmd(nc, [feed], core_ids=[0]).results[0]
    y = {n: np.asarray(r[n]) for n in shapes}
    return (y["y_prompt"].reshape(1, SEQ, D), y["y_sample"].reshape(1, DEC, D),
            y["k_prompt"].reshape(1, 1, SEQ, H, HD), y["v_prompt"].reshape(1, 1, SEQ, H, HD),
            y["logf_prompt"].reshape(1, 1, SEQ, H), y["conv_prompt"].T.reshape(1, 1, CW - 1, CONV),
            y["k_sample"].reshape(1, 1, DEC, H, HD), y["v_sample"].reshape(1, 1, DEC, H, HD),
            y["logf_sample"].reshape(1, 1, DEC, H), y["conv_sample"].T.reshape(1, 1, CW - 1, CONV))
```
